# Optimizing a Trainium2 kernel written in Bass

```python
import math
import jax
import jax.numpy as jnp
from jax import lax
import numpy as np
import jax, jax.numpy as jnp

D_MODEL = 1024
BATCH = 1
SEQ = 256
DEPTH = 2

HEAD_DIM_ATTN = 64
N_HEADS_SB = 8
N_HEADS_DIL = 8
WIDTH_SB = N_HEADS_SB * HEAD_DIM_ATTN
WIDTH_DIL = N_HEADS_DIL * HEAD_DIM_ATTN
ATTN_WIDTH = WIDTH_SB + WIDTH_DIL
DIL_CONFIGS = ((128, 1), (512, 4), (2048, 16))
Q_BLOCK = 128
NUM_BUCKETS = 32
MAX_DISTANCE = 2048
N_HEADS_MLSTM = 8
HEAD_DIM_MLSTM = D_MODEL // N_HEADS_MLSTM
MLSTM_WIDTH = N_HEADS_MLSTM * HEAD_DIM_MLSTM
MLSTM_CHUNK = 128
CONV_WIDTH = 4
FORGET_BIAS_LO = 3.0
FORGET_BIAS_HI = 6.0
D_FF = 2816
N_EVEN = (DEPTH + 1) // 2
N_ODD = DEPTH // 2
EPS = 1e-6


def _rms_norm(x, g):
    xf = x.astype(jnp.float32)
    y = xf * lax.rsqrt(jnp.mean(xf * xf, axis=-1, keepdims=True) + EPS)
    return (y * g.astype(jnp.float32)).astype(x.dtype)

def _swiglu(x, w_gate, w_up, w_down):
    return (jax.nn.silu(x @ w_gate) * (x @ w_up)) @ w_down

def _t5_bucket(dist):
    max_exact = NUM_BUCKETS // 2
    d = jnp.maximum(dist, 1).astype(jnp.float32)
    log_b = max_exact + (jnp.log(d / max_exact) / math.log(MAX_DISTANCE / max_exact)
                         * (NUM_BUCKETS - max_exact)).astype(jnp.int32)
    log_b = jnp.minimum(log_b, NUM_BUCKETS - 1)
    return jnp.where(dist < max_exact, dist, log_b)

def _stick_breaking_attention(q, k, v):
    bsz, t, h, dh = q.shape
    nb = t // Q_BLOCK
    qb = q.reshape(bsz, nb, Q_BLOCK, h, dh).transpose(1, 0, 2, 3, 4)
    starts = jnp.arange(nb) * Q_BLOCK
    k_pos = jnp.arange(t)
    scale = 1.0 / math.sqrt(dh)

    def block(args):
        q_blk, start = args
        z = jnp.einsum('bqhd,bkhd->bhqk', q_blk, k) * scale
        causal = k_pos[None, :] < (start + jnp.arange(Q_BLOCK))[:, None]
        log_keep = jnp.where(causal, jax.nn.log_sigmoid(-z), 0.0)
        later = lax.cumsum(log_keep, axis=3, reverse=True) - log_keep
        log_w = jnp.where(causal, jax.nn.log_sigmoid(z) + later, -jnp.inf)
        return jnp.einsum('bhqk,bkhd->bqhd', jnp.exp(log_w), v)

    out = lax.map(block, (qb, starts))
    return out.transpose(1, 0, 2, 3, 4).reshape(bsz, t, h, dh)

def _dilated_branch(q, k, v, rel_bias, window, dil):
    bsz, t, h, dh = q.shape
    steps = window // dil
    seq_l = t // dil
    nb = -(-seq_l // Q_BLOCK)
    lp = nb * Q_BLOCK
    n = bsz * dil

    def to_res(a):
        return a.reshape(bsz, seq_l, dil, h, dh).transpose(0, 2, 1, 3, 4).reshape(n, seq_l, h, dh)

    qb = jnp.pad(to_res(q), ((0, 0), (0, lp - seq_l), (0, 0), (0, 0))).reshape(n, nb, Q_BLOCK, h, dh)

    def band(a):
        a = jnp.pad(to_res(a), ((0, 0), (Q_BLOCK, lp - seq_l), (0, 0), (0, 0)))
        a = a.reshape(n, nb + 1, Q_BLOCK, h, dh)
        return jnp.concatenate([a[:, :-1], a[:, 1:]], axis=2)

    kb, vb = band(k), band(v)
    qi = jnp.arange(Q_BLOCK)[:, None]
    ki = jnp.arange(2 * Q_BLOCK)[None, :]
    dist = qi + Q_BLOCK - ki
    bias = rel_bias[_t5_bucket(jnp.maximum(dist, 0) * dil)].transpose(2, 0, 1)
    key_pos = jnp.arange(nb)[:, None, None] * Q_BLOCK + ki[None] - Q_BLOCK
    valid = (dist >= 0) & (dist <= steps) & (key_pos >= 0)
    s = jnp.einsum('nbqhd,nbkhd->nbhqk', qb, kb) / math.sqrt(dh) + bias
    s = jnp.where(valid[None, :, None], s, -jnp.inf)
    m = jnp.max(s, axis=-1)
    p = jnp.exp(s - m[..., None])
    l = jnp.sum(p, axis=-1)
    num = jnp.einsum('nbhqk,nbkhd->nbqhd', p, vb)

    def back(a):
        a = a[:, :seq_l]
        rest = a.shape[2:]
        a = a.reshape((bsz, dil, seq_l) + rest)
        a = a.transpose((0, 2, 1) + tuple(range(3, a.ndim)))
        return a.reshape((bsz, t) + rest)

    num = back(num.reshape(n, lp, h, dh))
    m = back(m.transpose(0, 1, 3, 2).reshape(n, lp, h))
    l = back(l.transpose(0, 1, 3, 2).reshape(n, lp, h))
    return num, m, l

def _dilated_attention(q, k, v, rel_bias):
    outs = [_dilated_branch(q, k, v, rel_bias, w, d) for (w, d) in DIL_CONFIGS]
    m_all = jnp.stack([o[1] for o in outs])
    wts = jnp.exp(m_all - jnp.max(m_all, axis=0))
    num = sum(wts[i][..., None] * outs[i][0] for i in range(len(outs)))
    den = sum(wts[i] * outs[i][2] for i in range(len(outs)))
    return num / den[..., None]

def _attn_mixer(xn, w_in, w_out, rel_bias):
    bsz, t, _ = xn.shape
    proj = (xn @ w_in).astype(jnp.float32)
    idx = [WIDTH_SB, 2 * WIDTH_SB, 3 * WIDTH_SB, 3 * WIDTH_SB + WIDTH_DIL, 3 * WIDTH_SB + 2 * WIDTH_DIL]
    qa, ka, va, qd, kd, vd = jnp.split(proj, idx, axis=-1)
    sb = lambda a: a.reshape(bsz, t, N_HEADS_SB, HEAD_DIM_ATTN)
    dl = lambda a: a.reshape(bsz, t, N_HEADS_DIL, HEAD_DIM_ATTN)
    out_sb = _stick_breaking_attention(sb(qa), sb(ka), sb(va))
    out_dil = _dilated_attention(dl(qd), dl(kd), dl(vd), rel_bias.astype(jnp.float32))
    mixed = jnp.concatenate([out_sb.reshape(bsz, t, WIDTH_SB), out_dil.reshape(bsz, t, WIDTH_DIL)], axis=-1)
    return mixed.astype(xn.dtype) @ w_out

def _causal_depthwise_conv(x, w):
    return lax.conv_general_dilated(
        x, w[:, None, :], window_strides=(1,), padding=((CONV_WIDTH - 1, 0),),
        dimension_numbers=('NWC', 'WIO', 'NWC'), feature_group_count=x.shape[-1])

def _mlstm(q, k, v, i_pre, f_pre):
    bsz, t, h, dh = q.shape
    nc = t // MLSTM_CHUNK
    cl = MLSTM_CHUNK

    def chunks(a):
        a = a.reshape((bsz, nc, cl, h) + a.shape[3:])
        return a.transpose((0, 3, 1, 2) + tuple(range(4, a.ndim)))

    qc = chunks(q) / math.sqrt(dh)
    kc, vc = chunks(k), chunks(v)
    ic = chunks(i_pre)
    bc = jnp.cumsum(jax.nn.log_sigmoid(chunks(f_pre)), axis=-1)

    def step(carry, xs):
        c_st, n_st, m_st = carry
        k_, v_, i_, b_ = xs
        g = b_[..., -1]
        w = g[..., None] - b_ + i_
        m_new = jnp.maximum(g + m_st, jnp.max(w, axis=-1))
        decay = jnp.exp(g + m_st - m_new)
        ws = jnp.exp(w - m_new[..., None])
        c_new = decay[..., None, None] * c_st + jnp.einsum('bhs,bhsk,bhsv->bhkv', ws, k_, v_)
        n_new = decay[..., None] * n_st + jnp.einsum('bhs,bhsk->bhk', ws, k_)
        return (c_new, n_new, m_new), (c_st, n_st, m_st)

    init = (jnp.zeros((bsz, h, dh, dh), jnp.float32),
            jnp.zeros((bsz, h, dh), jnp.float32),
            jnp.zeros((bsz, h), jnp.float32))
    xs = tuple(jnp.moveaxis(a, 2, 0) for a in (kc, vc, ic, bc))
    _, (c_prev, n_prev, m_prev) = lax.scan(step, init, xs)
    c_prev = jnp.moveaxis(c_prev, 0, 2)
    n_prev = jnp.moveaxis(n_prev, 0, 2)
    m_prev = jnp.moveaxis(m_prev, 0, 2)

    a = bc + m_prev[..., None]
    tri = jnp.arange(cl)[:, None] >= jnp.arange(cl)[None, :]
    dmat = jnp.where(tri, bc[..., :, None] - bc[..., None, :] + ic[..., None, :], -jnp.inf)
    m_t = jnp.maximum(a, jnp.max(dmat, axis=-1))
    p = jnp.einsum('bhcld,bhcsd->bhcls', qc, kc) * jnp.exp(dmat - m_t[..., None])
    w_inter = jnp.exp(a - m_t)
    h_num = (jnp.einsum('bhcls,bhcsd->bhcld', p, vc)
             + w_inter[..., None] * jnp.einsum('bhcld,bhcde->bhcle', qc, c_prev))
    n_num = jnp.sum(p, axis=-1) + w_inter * jnp.einsum('bhcld,bhcd->bhcl', qc, n_prev)
    hid = h_num / jnp.maximum(jnp.abs(n_num), jnp.exp(-m_t))[..., None]
    return hid.transpose(0, 2, 3, 1, 4).reshape(bsz, t, h, dh)

def _mlstm_mixer(xn, w_in, b_gates, conv_w, head_g, w_out):
    bsz, t, _ = xn.shape
    proj = (xn @ w_in).astype(jnp.float32)
    qk, v, o, gates = jnp.split(proj, [2 * MLSTM_WIDTH, 3 * MLSTM_WIDTH, 4 * MLSTM_WIDTH], axis=-1)
    qk = jax.nn.silu(_causal_depthwise_conv(qk, conv_w.astype(jnp.float32)))
    q, k = jnp.split(qk, 2, axis=-1)
    gates = gates + b_gates.astype(jnp.float32)
    i_pre, f_pre = gates[..., :N_HEADS_MLSTM], gates[..., N_HEADS_MLSTM:]
    hd = lambda a: a.reshape(bsz, t, N_HEADS_MLSTM, HEAD_DIM_MLSTM)
    hid = _mlstm(hd(q), hd(k), hd(v), i_pre, f_pre)
    hid = hid * lax.rsqrt(jnp.mean(hid * hid, axis=-1, keepdims=True) + EPS)
    hid = hid * head_g.astype(jnp.float32).reshape(N_HEADS_MLSTM, HEAD_DIM_MLSTM)
    hid = hid.reshape(bsz, t, MLSTM_WIDTH) * jax.nn.sigmoid(o)
    return hid.astype(xn.dtype) @ w_out

def first_inputs(seed: int = 0) -> dict:
    key = jax.random.key(seed)
    ks = jax.random.split(key, 16)
    nrm = jax.random.normal
    x = nrm(ks[0], (BATCH, SEQ, D_MODEL), jnp.float32)
    norm_g = 1.0 + 0.02 * nrm(ks[1], (DEPTH, 6, D_MODEL), jnp.float32)
    ffn_w_gate = nrm(ks[2], (DEPTH, 2, D_MODEL, D_FF), jnp.float32) * D_MODEL ** -0.5
    ffn_w_up = nrm(ks[3], (DEPTH, 2, D_MODEL, D_FF), jnp.float32) * D_MODEL ** -0.5
    ffn_w_down = nrm(ks[4], (DEPTH, 2, D_FF, D_MODEL), jnp.float32) * D_FF ** -0.5
    attn_w_in = nrm(ks[5], (N_EVEN, D_MODEL, 3 * ATTN_WIDTH), jnp.float32) * D_MODEL ** -0.5
    attn_w_out = nrm(ks[6], (N_EVEN, ATTN_WIDTH, D_MODEL), jnp.float32) * ATTN_WIDTH ** -0.5
    rel_bias = 0.5 * nrm(ks[7], (NUM_BUCKETS, N_HEADS_DIL), jnp.float32)
    mlstm_w_in = nrm(ks[8], (N_ODD, D_MODEL, 4 * MLSTM_WIDTH + 2 * N_HEADS_MLSTM), jnp.float32) * D_MODEL ** -0.5
    b_i = 0.1 * nrm(ks[9], (N_ODD, N_HEADS_MLSTM), jnp.float32)
    b_f = (jnp.linspace(FORGET_BIAS_LO, FORGET_BIAS_HI, N_HEADS_MLSTM, dtype=jnp.float32)[None]
           + 0.1 * nrm(ks[10], (N_ODD, N_HEADS_MLSTM), jnp.float32))
    mlstm_b_gates = jnp.concatenate([b_i, b_f], axis=-1)
    mlstm_conv_w = nrm(ks[11], (N_ODD, CONV_WIDTH, 2 * MLSTM_WIDTH), jnp.float32) * CONV_WIDTH ** -0.5
    mlstm_head_g = 1.0 + 0.02 * nrm(ks[12], (N_ODD, MLSTM_WIDTH), jnp.float32)
    mlstm_w_out = nrm(ks[13], (N_ODD, MLSTM_WIDTH, D_MODEL), jnp.float32) * MLSTM_WIDTH ** -0.5
    return {'x': x, 'norm_g': norm_g, 'ffn_w_gate': ffn_w_gate, 'ffn_w_up': ffn_w_up,
            'ffn_w_down': ffn_w_down, 'attn_w_in': attn_w_in, 'attn_w_out': attn_w_out,
            'rel_bias': rel_bias, 'mlstm_w_in': mlstm_w_in, 'mlstm_b_gates': mlstm_b_gates,
            'mlstm_conv_w': mlstm_conv_w, 'mlstm_head_g': mlstm_head_g, 'mlstm_w_out': mlstm_w_out}

def first_block(x, norm_g, ffn_w_gate, ffn_w_up, ffn_w_down, attn_w_in, attn_w_out, rel_bias,
              mlstm_w_in, mlstm_b_gates, mlstm_conv_w, mlstm_head_g, mlstm_w_out):
    for layer in range(DEPTH):
        g = norm_g[layer]
        j = layer // 2
        hf = _swiglu(_rms_norm(x, g[0]), ffn_w_gate[layer, 0], ffn_w_up[layer, 0], ffn_w_down[layer, 0])
        x = x + 0.5 * _rms_norm(hf, g[1])
        xn = _rms_norm(x, g[2])
        if layer % 2 == 0:
            mix = _attn_mixer(xn, attn_w_in[j], attn_w_out[j], rel_bias)
        else:
            mix = _mlstm_mixer(xn, mlstm_w_in[j], mlstm_b_gates[j], mlstm_conv_w[j],
                               mlstm_head_g[j], mlstm_w_out[j])
        x = x + _rms_norm(mix, g[3])
        hf = _swiglu(_rms_norm(x, g[4]), ffn_w_gate[layer, 1], ffn_w_up[layer, 1], ffn_w_down[layer, 1])
        x = x + 0.5 * _rms_norm(hf, g[5])
    return x


CONV_WIDTH_2 = 512
CONV_KSIZE = 3
ATTN_HEADS = 8
HEAD_DIM = 64
ATTN_WIDTH_2 = ATTN_HEADS * HEAD_DIM
IDX_HEADS = 8
IDX_DIM = 64
INDEX_TOPK = 256
ROPE_THETA = 10000.0
POOL_WINDOWS = (2, 4, 8, 16)
POOL_GROUPS = 4
POOL_WIDTH = 512
POOL_GROUP_DIM = POOL_WIDTH // POOL_GROUPS
N_BRANCHES = 3
RMS_EPS = 1e-6

IN_SPLITS = (CONV_WIDTH_2, CONV_WIDTH_2, CONV_WIDTH_2, CONV_WIDTH_2,
             ATTN_WIDTH_2, ATTN_WIDTH_2, ATTN_WIDTH_2, ATTN_WIDTH_2,
             IDX_HEADS * IDX_DIM, IDX_DIM, IDX_HEADS,
             POOL_WIDTH, POOL_WIDTH,
             N_BRANCHES * D_MODEL)
IN_WIDTH = 4 * CONV_WIDTH_2 + 4 * ATTN_WIDTH_2 + IDX_HEADS * IDX_DIM + IDX_DIM + IDX_HEADS + 2 * POOL_WIDTH + N_BRANCHES * D_MODEL


def rms_norm(x, g):
    xf = x.astype(jnp.float32)
    y = xf * lax.rsqrt(jnp.mean(xf * xf, axis=-1, keepdims=True) + RMS_EPS)
    return (y * g.astype(jnp.float32)).astype(x.dtype)

def split_columns(p):
    out = []
    off = 0
    for n in IN_SPLITS:
        out.append(p[..., off:off + n])
        off += n
    return out

def rope_tables(seq_len, dim):
    inv = 1.0 / (ROPE_THETA ** (jnp.arange(0, dim, 2, dtype=jnp.float32) / dim))
    ang = jnp.arange(seq_len, dtype=jnp.float32)[:, None] * inv[None, :]
    return jnp.cos(ang), jnp.sin(ang)

def apply_rope(x, cos, sin):
    xf = x.astype(jnp.float32)
    half = xf.shape[-1] // 2
    x1, x2 = xf[..., :half], xf[..., half:]
    c, s = cos[None, :, None, :], sin[None, :, None, :]
    return jnp.concatenate([x1 * c - x2 * s, x2 * c + x1 * s], axis=-1).astype(x.dtype)

def short_conv_mixer(b, c, xin, gate, conv_w, w_out):
    S = xin.shape[1]
    z = c * xin
    zp = jnp.pad(z, ((0, 0), (CONV_KSIZE - 1, 0), (0, 0)))
    y = conv_w[0] * zp[:, 0:S]
    for j in range(1, CONV_KSIZE):
        y = y + conv_w[j] * zp[:, j:j + S]
    y = b * y * jax.nn.silu(gate)
    return y @ w_out

def sparse_attention_mixer(q, k, v, gate, iq, ik, iw, q_g, k_g, cos, sin, w_out):
    B, S, _ = q.shape
    q = apply_rope(rms_norm(q.reshape(B, S, ATTN_HEADS, HEAD_DIM), q_g), cos, sin)
    k = apply_rope(rms_norm(k.reshape(B, S, ATTN_HEADS, HEAD_DIM), k_g), cos, sin)
    v = v.reshape(B, S, ATTN_HEADS, HEAD_DIM)
    iq = apply_rope(iq.reshape(B, S, IDX_HEADS, IDX_DIM), cos, sin)
    ik = apply_rope(ik[:, :, None, :], cos, sin)[:, :, 0, :]
    top_k = min(INDEX_TOPK, S // 4)
    nb = S // Q_BLOCK

    def to_blocks(a):
        return jnp.swapaxes(a.reshape((B, nb, Q_BLOCK) + a.shape[2:]), 0, 1)

    starts = jnp.arange(nb, dtype=jnp.int32) * Q_BLOCK
    key_pos = jnp.arange(S, dtype=jnp.int32)

    def block_fn(args):
        qb, iqb, iwb, t0 = args
        tq = t0 + jnp.arange(Q_BLOCK, dtype=jnp.int32)
        sc = jnp.einsum('bqhd,bsd->bqhs', iqb, ik).astype(jnp.float32) * (IDX_DIM ** -0.5)
        score = jnp.einsum('bqhs,bqh->bqs', jax.nn.relu(sc), iwb.astype(jnp.float32)) * (IDX_HEADS ** -0.5)
        admissible = key_pos[None, :] <= tq[:, None]
        score = jnp.where(admissible[None], score, -jnp.inf)
        _, idx = lax.top_k(score, top_k)
        valid = idx <= tq[None, :, None]
        k_sel = jax.vmap(lambda kb, ib: kb[ib])(k, idx)
        v_sel = jax.vmap(lambda vb, ib: vb[ib])(v, idx)
        s = jnp.einsum('bqhd,bqkhd->bhqk', qb, k_sel).astype(jnp.float32) * (HEAD_DIM ** -0.5)
        s = jnp.where(valid[:, None], s, -jnp.inf)
        p = jax.nn.softmax(s, axis=-1).astype(v.dtype)
        return jnp.einsum('bhqk,bqkhd->bqhd', p, v_sel)

    o = lax.map(block_fn, (to_blocks(q), to_blocks(iq), to_blocks(iw), starts))
    o = jnp.swapaxes(o, 0, 1).reshape(B, S, ATTN_WIDTH_2)
    return (o * jax.nn.silu(gate)) @ w_out

def pool_mixer(u, gate, pool_w, pool_scale, w_out):
    B, S, _ = u.shape
    ug = u.reshape(B, S, POOL_GROUPS, POOL_GROUP_DIM)
    cs = jnp.cumsum(ug.astype(jnp.float32), axis=1)
    t = jnp.arange(S)
    means = []
    for gi, w in enumerate(POOL_WINDOWS):
        c = cs[:, :, gi]
        lagged = jnp.pad(c, ((0, 0), (w, 0), (0, 0)))[:, :S]
        cnt = jnp.minimum(t + 1, w).astype(jnp.float32)[None, :, None]
        means.append((c - lagged) / cnt)
    pooled = (jnp.stack(means, axis=2) - ug.astype(jnp.float32)).astype(u.dtype)
    mixed = jnp.einsum('bsgc,gcd->bsgd', pooled, pool_w).reshape(B, S, POOL_WIDTH)
    y = mixed * pool_scale * jax.nn.silu(gate)
    return y @ w_out

def second_inputs(seed: int = 0) -> dict:
    key = jax.random.key(seed)
    ks = jax.random.split(key, 13)
    f32 = jnp.float32
    L = DEPTH
    return {
        "x": jax.random.normal(ks[0], (BATCH, SEQ, D_MODEL), f32),
        "norm_g": 1.0 + 0.1 * jax.random.normal(ks[1], (L, D_MODEL), f32),
        "w_in": jax.random.normal(ks[2], (L, D_MODEL, IN_WIDTH), f32) * D_MODEL ** -0.5,
        "conv_w": jax.random.normal(ks[3], (L, CONV_KSIZE, CONV_WIDTH_2), f32) * CONV_KSIZE ** -0.5,
        "w_out_conv": jax.random.normal(ks[4], (L, CONV_WIDTH_2, D_MODEL), f32) * CONV_WIDTH_2 ** -0.5,
        "q_norm_g": 1.0 + 0.1 * jax.random.normal(ks[5], (L, HEAD_DIM), f32),
        "k_norm_g": 1.0 + 0.1 * jax.random.normal(ks[6], (L, HEAD_DIM), f32),
        "w_out_attn": jax.random.normal(ks[7], (L, ATTN_WIDTH_2, D_MODEL), f32) * ATTN_WIDTH_2 ** -0.5,
        "pool_w": jax.random.normal(ks[8], (L, POOL_GROUPS, POOL_GROUP_DIM, POOL_GROUP_DIM), f32) * POOL_GROUP_DIM ** -0.5,
        "pool_scale": 1.0 + 0.1 * jax.random.normal(ks[9], (L, POOL_WIDTH), f32),
        "w_out_pool": jax.random.normal(ks[10], (L, POOL_WIDTH, D_MODEL), f32) * POOL_WIDTH ** -0.5,
        "w_o": jax.random.normal(ks[11], (L, D_MODEL, D_MODEL), f32) * D_MODEL ** -0.5,
    }

def second_block(x, norm_g, w_in, conv_w, w_out_conv, q_norm_g, k_norm_g, w_out_attn, pool_w, pool_scale, w_out_pool, w_o):
    B, S, D = x.shape
    cos, sin = rope_tables(S, HEAD_DIM)
    for l in range(DEPTH):
        h = rms_norm(x, norm_g[l])
        p = h @ w_in[l]
        (cb, cc, cx, cgate, q, k, v, agate, iq, ik, iw, pu, pgate, mgate) = split_columns(p)
        y_a = short_conv_mixer(cb, cc, cx, cgate, conv_w[l], w_out_conv[l])
        y_b = sparse_attention_mixer(q, k, v, agate, iq, ik, iw, q_norm_g[l], k_norm_g[l], cos, sin, w_out_attn[l])
        y_c = pool_mixer(pu, pgate, pool_w[l], pool_scale[l], w_out_pool[l])
        g = jax.nn.sigmoid(mgate.reshape(B, S, N_BRANCHES, D))
        merged = g[:, :, 0] * y_a + g[:, :, 1] * y_b + g[:, :, 2] * y_c
        x = x + merged @ w_o[l]
    return x


def setup_inputs(seed=0):
    out = dict(first_inputs(seed))
    for name, value in second_inputs(seed + 1).items():
        if name != "x":
            out[name + "_2"] = value
    return out


def reference(
    x, norm_g, ffn_w_gate, ffn_w_up, ffn_w_down, attn_w_in, attn_w_out, rel_bias, mlstm_w_in,
    mlstm_b_gates, mlstm_conv_w, mlstm_head_g, mlstm_w_out, norm_g_2, w_in_2, conv_w_2,
    w_out_conv_2, q_norm_g_2, k_norm_g_2, w_out_attn_2, pool_w_2, pool_scale_2, w_out_pool_2,
    w_o_2,
):
    x = first_block(
        x, norm_g, ffn_w_gate, ffn_w_up, ffn_w_down, attn_w_in, attn_w_out, rel_bias,
        mlstm_w_in, mlstm_b_gates, mlstm_conv_w, mlstm_head_g, mlstm_w_out,
    )
    return second_block(
        x, norm_g_2, w_in_2, conv_w_2, w_out_conv_2, q_norm_g_2, k_norm_g_2, w_out_attn_2,
        pool_w_2, pool_scale_2, w_out_pool_2, w_o_2,
    )


_drawn_inputs = setup_inputs


def setup_inputs(seed=0):
    import zlib

    import numpy as np

    out = dict(_drawn_inputs(seed))
    spreads = {}
    factors = {'mlstm_head_g': 4.692, 'q_norm_g_2': 8.0, 'k_norm_g_2': 8.0, 'pool_scale_2': 3.069}
    for name, (base, spread) in spreads.items():
        noise = np.random.default_rng([zlib.crc32(name.encode()), seed]).standard_normal(out[name].shape)
        drawn = base * np.exp(spread * noise) if base else spread * noise
        out[name] = jnp.asarray(drawn.astype(out[name].dtype))
    for name, factor in factors.items():
        out[name] = (out[name] * factor).astype(out[name].dtype)
    return out
```

```python
from contextlib import ExitStack

import numpy as np

import concourse.bass as bass
from concourse import mybir

F32 = mybir.dt.float32
F32R = mybir.dt.float32r
ALU = mybir.AluOpType
ACT = mybir.ActivationFunctionType
AX_X = mybir.AxisListType.X

P = 128
SEQ = 256
NTOK = SEQ // P
D = 1024
KD = D // P
DFF = 2816
KF = DFF // P
DEPTH = 2
EPS = 1e-6
COLS = 512
SLOT = KD * COLS
GU = COLS // 2
NGU = DFF // GU
DOWN = (6, 6, 5, 5)
HEADS = 8
DH = 64
NEG = -1.0e30
TAKEN = -3.0e38
TOPK = SEQ // 4
WINDOWS = (2, 4, 8, 16)
TAPS_2 = 3
assert sum(DOWN) == KF and NGU * GU == DFF


class At:

    def __init__(self):
        self.chunk = self.block = self.group = self.row = 0
        self.square = self.rsqrt = self.normed = 0
        self.unit = self.ln = self.silu = self.rounded = 0
        self.staged = self.index = self.head_norm = self.side = self.branch = 0



def relative_bucket(dist, num_buckets=32, max_distance=2048):
    exact = num_buckets // 2
    d = np.maximum(dist, 1).astype(np.float32)
    log_b = exact + (np.log(d / np.float32(exact)) / np.float32(np.log(max_distance / exact))
                     * np.float32(num_buckets - exact)).astype(np.int32)
    return np.where(dist < exact, dist, np.minimum(log_b, num_buckets - 1))


def branch_count(dist):
    near = (dist >= 0) & (dist <= 128)
    return (near.astype(np.float32) + ((dist >= 0) & (dist % 4 == 0)) + ((dist >= 0) & (dist % 16 == 0))).astype(np.float32)


def rope_constants():
    exponent = np.arange(0, DH, 2) / DH
    inv = np.float32(1) / np.power(10000.0, exponent).astype(np.float32)
    angle = np.arange(SEQ, dtype=np.float32)[:, None] * inv[None, :]
    cos, sin = np.cos(angle), np.sin(angle)
    both = np.stack([np.concatenate([cos, cos], 1), np.concatenate([-sin, sin], 1)])
    return np.ascontiguousarray(both.reshape(2, NTOK, P, DH).transpose(2, 0, 1, 3)).astype(np.float32)


def pool_constants():
    s = np.arange(P)[:, None]
    t = np.arange(P)[None, :]
    tiles = []
    for w in WINDOWS:
        inside = (s <= t) & (s > t - w)
        near = (s > t + P - w)[:, 0:WINDOWS[-1]]
        tiles.append(np.concatenate([inside / np.minimum(t + 1, w) - (s == t), inside / w - (s == t), near / w], axis=1))
    return np.ascontiguousarray(np.stack(tiles, axis=1)).astype(np.float32)


def shape_constants():
    part = np.arange(P)[:, None]
    free = np.arange(P)[None, :]
    far = np.concatenate([free, free, free + P], axis=1)
    dist = (np.arange(3 * P) - P)[::-1]
    onehot = np.zeros((33, 3 * P), np.float32)
    seen = branch_count(dist) > 0
    onehot[relative_bucket(np.maximum(dist, 0)), np.arange(3 * P)] = seen
    onehot[32] = ~seen
    q_of = np.concatenate([part + 0 * free, part + P + 0 * free, part + P + 0 * free], axis=1)
    k_of = np.concatenate([free + 0 * part, free + 0 * part, free + P + 0 * part], axis=1)
    goes_on = (k_of + 1 < q_of).astype(np.float32)
    qt = np.concatenate([free + 0 * part, free + P + 0 * part, free + P + 0 * part], axis=1)
    kt = np.concatenate([part + 0 * free, part + 0 * free, part + P + 0 * free], axis=1)
    past = (kt < qt).astype(np.float32)
    count = branch_count(qt - kt)
    ident = np.eye(P, dtype=np.float32)
    return {"c_onehot": onehot, "c_tiles": np.concatenate([
        ident, goes_on, past, count, ident[:, ::-1],
        (part <= free).astype(np.float32),
        np.float32(-NEG) * (part > free), np.ones((P, 1)),
        np.float32(NEG) * (free > part)], axis=1).astype(np.float32),
        "c_rope": rope_constants(), "c_pool": pool_constants()}


CONSTANTS = shape_constants()
C_IDENT, C_GOES_ON, C_PAST, C_COUNT, C_FLIP = 0, P, 4 * P, 7 * P, 10 * P
C_UPTO, C_AFTER, C_ONE, C_LATER = 11 * P, 12 * P, 13 * P, 13 * P + 1


def program(nc, x, norm_g, ffn_w_gate, ffn_w_up, ffn_w_down, attn_w_in, attn_w_out, rel_bias,
            mlstm_w_in, mlstm_w_out, conv_taps, mlstm_b_gates, mlstm_head_g,
            norm_g_2, w_in_2, w_out_conv_2, q_norm_g_2, k_norm_g_2, w_out_attn_2, pool_w_2,
            w_out_pool_2, w_o_2, conv_taps_2, pool_scale_2,
            c_onehot, c_tiles, c_rope, c_pool, out):
    ctx = ExitStack()
    top = [(nc.sbuf_base + 31) // 32 * 32]

    sbuf_at = {}

    def sb(name, shape, dt=F32, offset=None):
        size = int(np.prod(shape[1:])) * 4
        sbuf_at[name] = top[0] if offset is None else offset
        t = nc.alloc_sbuf_tensor_at(name, list(shape), dt, offset=top[0] if offset is None else offset)
        if offset is None:
            top[0] += (size + 31) // 32 * 32
        return t

    def sem(name):
        return ctx.enter_context(nc.semaphore(name))

    with ctx:
        X = sb("X", [P, NTOK, D])
        RAW = sb("RAW", [P, 2, SLOT])
        WH = sb("WH", [P, 2, SLOT], F32R)
        WL = sb("WL", [P, 2, SLOT], F32R)
        XH = sb("XH", [P, KD, SEQ], F32R)
        XL = sb("XL", [P, KD, SEQ], F32R)
        XN = sb("XN", [P, NTOK, D])
        G = sb("G", [P, 2, D])
        ST = sb("ST", [P, NTOK, COLS])
        SIDE = sb("SIDE", [P, NTOK, GU])
        CT = sb("CT", list(c_tiles.shape))
        SS = sb("SS", [P, 4])
        MS = sb("MS", [P, 2])
        RS = sb("RS", [P, 2])
        HALF = sb("HALF", [P, 2])
        TMP2 = sb("TMP2", [P, 2])
        arena = top[0]
        HH = sb("HH", [P, KF, SEQ], F32R)
        HL = sb("HL", [P, KF, SEQ], F32R)
        o = arena
        QT = sb("QT", [P, 4, 4, SEQ], offset=o)
        o += 4 * 4 * SEQ * 4
        VS = sb("VS", [P, 2, NTOK, HEADS, DH + 1], offset=o)
        o += 2 * NTOK * HEADS * (DH + 1) * 4
        BT = sb("BT", [P, HEADS, SEQ], offset=o)
        o += HEADS * SEQ * 4
        assert o <= top[0]
        o = arena
        QK = sb("QK", [P, 2 * HEADS, SEQ], offset=o)
        o += 2 * HEADS * SEQ * 4
        VA = sb("VA", [P, NTOK, HEADS, P + 1], offset=o)
        o += NTOK * HEADS * (P + 1) * 4
        SO = sb("SO", [P, NTOK, D], offset=o)
        o += NTOK * D * 4
        KN = sb("KN", [P, HEADS, P], offset=o)
        o += HEADS * P * 4
        CA = sb("CA", [P, HEADS, P + 1], offset=o)
        o += HEADS * (P + 1) * 4
        assert o <= top[0]
        o = arena
        QT2 = sb("QT2", [P, 3, 4, SEQ], offset=o)
        o += 3 * 4 * SEQ * 4
        IKT = sb("IKT", [P, SEQ], offset=o)
        o += SEQ * 4
        V2 = sb("V2", [P, NTOK, HEADS, DH + 1], offset=o)
        o += NTOK * HEADS * (DH + 1) * 4
        AG = sb("AG", [P, NTOK, COLS], offset=o)
        o += NTOK * COLS * 4
        BH = sb("BH", [P, 4, SEQ], F32R, offset=o)
        o += 4 * SEQ * 4
        BL = sb("BL", [P, 4, SEQ], F32R, offset=o)
        o += 4 * SEQ * 4
        MK = sb("MK", [P, 3 * P], offset=o)
        o += 3 * P * 4
        SX = sb("SX", [P, NTOK, COLS], offset=o)
        o += NTOK * COLS * 4
        YT = sb("YT", [P, 4, SEQ], offset=o)
        o += 4 * SEQ * 4
        PM = sb("PM", list(c_pool.shape), offset=o)
        o += int(np.prod(c_pool.shape[1:])) * 4
        CS = sb("CS", list(c_rope.shape), offset=o)
        o += int(np.prod(c_rope.shape[1:])) * 4
        assert o <= top[0]
        PW = sb("PW", [P, 4, P], offset=sbuf_at["SIDE"])
        GQK = sb("GQK", [P, DEPTH, 2, DH])
        CW2 = sb("CW2", [P, DEPTH, 4, TAPS_2])
        PS2 = sb("PS2", [P, DEPTH, 4])
        IW = sb("IW", [P, NTOK, HEADS])
        HN = sb("HN", [P, NTOK * HEADS])
        HM = sb("HM", [P, NTOK * HEADS])
        HR = sb("HR", [P, NTOK * HEADS])
        M8 = sb("M8", [P, 8])
        T2 = sb("T2", [P, NTOK, DH])
        CW = sb("CW", [P, 2 * HEADS, 4])
        BG = sb("BG", [P, 2 * HEADS])
        HALF16 = sb("HALF16", [P, NTOK * HEADS])
        NM = sb("NM", [P, 2, 2])
        RD = sb("RD", [P, 2, 2])
        RB = sb("RB", [33, HEADS])
        units_at = top[0]
        UA = sb("UA", [P, 2, 3 * P])
        UL = sb("UL", [P, 2, 3 * P])
        UW = sb("UW", [P, 2, 3 * P])
        UT = sb("UT", [P, 2, 3 * P])
        ONEHOT = sb("ONEHOT", [33, 3 * P], offset=units_at)
        BROW = sb("BROW", [HEADS, 3 * P], offset=units_at + 3 * P * 4)
        YC = sb("YC", [P, 2, 2 * SEQ], offset=units_at)
        DT = sb("DT", [P, 2, SEQ], offset=units_at + 2 * 2 * SEQ * 4)
        PT = sb("PT", [P, 2, SEQ], offset=units_at + 3 * 2 * SEQ * 4)
        small_at = [units_at + 4 * 2 * SEQ * 4]
        QS = sb("QS", [P, NTOK, COLS], offset=units_at)
        SQ = sb("SQ", [P, NTOK, COLS], offset=units_at + NTOK * COLS * 4)
        T3 = sb("T3", [P, NTOK, COLS], offset=units_at + 2 * NTOK * COLS * 4)
        PL = sb("PL", [P, 4, SEQ], offset=units_at)

        def small(name, shape):
            t = sb(name, shape, offset=small_at[0])
            small_at[0] += (int(np.prod(shape[1:])) * 4 + 31) // 32 * 32
            return t

        GT = small("GT", [P, NTOK, 2 * HEADS])
        LS = small("LS", [P, NTOK, HEADS])
        LF = small("LF", [P, NTOK, HEADS])
        BC = small("BC", [P, NTOK, HEADS])
        VV = small("VV", [P, NTOK, HEADS])
        VT = small("VT", [HEADS, SEQ])
        MU = small("MU", [HEADS, SEQ])
        GL = small("GL", [HEADS, 2])
        DG = small("DG", [HEADS, 2 * HEADS])
        MUB = small("MUB", [P, 4 * HEADS])
        EA = small("EA", [P, 4 * HEADS])
        EX = small("EX", [P, 4 * HEADS])
        WI = small("WI", [P, HEADS])
        N3 = small("N3", [P, HEADS, 3])
        NI = small("NI", [P, HEADS])
        AN = small("AN", [P, NTOK, HEADS])
        RN = small("RN", [P, NTOK, HEADS])
        HS = small("HS", [P, NTOK, HEADS])
        HQ = small("HQ", [P, NTOK, HEADS])
        HF = small("HF", [P, NTOK, HEADS])
        assert small_at[0] <= top[0]
        assert top[0] <= nc.sbuf_usable_end, (top[0], nc.sbuf_usable_end)
        bias_dram = nc.dram_tensor("bias_by_distance", (HEADS, 3 * P), F32, kind="Internal").ap()

        ACC = ctx.enter_context(nc.psum_tensor("ACC", [P, 4, COLS], F32))
        ZB = ctx.enter_context(nc.psum_tensor("ZB", [P, COLS], F32))
        OB = ctx.enter_context(nc.psum_tensor("OB", [P, COLS], F32))
        TB = [ctx.enter_context(nc.psum_tensor(f"TB{i}", [P, COLS], F32)) for i in range(2)]

        raw_ready = [sem(f"raw_ready{i}") for i in range(2)]
        hi_ready = sem("hi_ready")
        lo_ready = sem("lo_ready")
        weights_used = sem("weights_used")
        tile0_ready = sem("tile0_ready")
        blocks_used = sem("blocks_used")
        groups_ready = sem("groups_ready")
        groups_hi = sem("groups_hi")
        groups_used = sem("groups_used")
        silu_ready = sem("silu_ready")
        squares = sem("squares")
        rsqrts = sem("rsqrts")
        pool_step = sem("pool_step")
        normed = sem("normed")
        x_loaded = sem("x_loaded")
        consts_loaded = sem("consts_loaded")
        row_loaded = [sem(f"row_loaded{i}") for i in range(2)]
        out_stored = sem("out_stored")
        z_ready = sem("z_ready")
        abs_ready = sem("abs_ready")
        exp_ready = sem("exp_ready")
        ln_ready = sem("ln_ready")
        dve_step = sem("dve_step")
        logits_ready = sem("logits_ready")
        w_ready = sem("w_ready")
        o_ready = sem("o_ready")
        o_used = sem("o_used")
        mask_set = sem("mask_set")
        small_loaded = sem("small_loaded")
        silus = sem("silus")
        gates_dve = sem("gates_dve")
        gates_act = sem("gates_act")
        ho_ready = sem("ho_ready")
        heads_squared = sem("heads_squared")
        heads_ready = sem("heads_ready")
        heads_scaled = sem("heads_scaled")
        mixed = sem("mixed")
        bias_summed = sem("bias_summed")
        bias_rows = sem("bias_rows")
        bias_stored = sem("bias_stored")
        bias_ready = sem("bias_ready")

        rope_done = sem("rope_done")
        head_sums = sem("head_sums")
        head_rsqrts = sem("head_rsqrts")
        tables_loaded = sem("tables_loaded")
        pool_w_loaded = sem("pool_w_loaded")
        index_z_ready = sem("index_z_ready")
        relu_ready = sem("relu_ready")
        index_summed = sem("index_summed")
        mask_ready = sem("mask_ready")
        branch_hi = sem("branch_hi")
        branch_ready = sem("branch_ready")

        ident = CT[:, C_IDENT:C_IDENT + P]
        goes_on = CT[:, C_GOES_ON:C_GOES_ON + 3 * P]
        past_t = CT[:, C_PAST:C_PAST + 3 * P]
        count_t = CT[:, C_COUNT:C_COUNT + 3 * P]
        flip = CT[:, C_FLIP:C_FLIP + P]
        upto = CT[:, C_UPTO:C_UPTO + P]
        after = CT[:, C_AFTER:C_AFTER + P]
        later = CT[:, C_LATER:C_LATER + P]
        one = CT[:, C_ONE:C_ONE + 1]

        rows = []
        for layer in range(DEPTH):
            rows += [norm_g[layer, i, :] for i in range(6)]
        rows.insert(6 + 3, mlstm_head_g[0])
        rows += [norm_g_2[layer] for layer in range(DEPTH)]

        def raw_value(chunk):
            return 32 * (chunk // 2 + 1)

        bias_by_query = bass.AP(tensor=bias_dram.tensor, offset=0, ap=[[1, P], [3 * P, HEADS], [1, SEQ]])

        FULL = KD * COLS
        DOWN_SIZES = [k * COLS for k in DOWN] * 2

        stages = [("ffn", 0, 0), ("attn", 0), ("ffn", 0, 1), ("ffn", 1, 0), ("mlstm", 1), ("ffn", 1, 1),
                  ("mix2", 0), ("mix2", 1)]

        BLOCKS = {"ffn": NGU + 2, "attn": 8, "mlstm": 11, "mix2": 26}
        last_block = sum(BLOCKS[stage[0]] for stage in stages)

        W2 = dict(cb=0, cc=512, cx=1024, cgate=1536, q=2048, k=2560, v=3072, agate=3584, iq=4096,
                  ik_iw=4608, pu=4680, pgate=5192, mgate=5704)
        IKW = DH + HEADS
        ORDER = ["ik_iw", "q", "k", "iq", "v", "agate", "cx", "cc", "cgate", "cb", "pu", "pgate"]
        BRANCHES = [(w_out_conv_2, 0), (w_out_pool_2, 2), (w_out_attn_2, 1)]
        for branch in range(3):
            ORDER += ["mgate", "branch", "mgate", "branch"]
        ORDER += ["out", "out"]
        SIZES = [KD * IKW if kind == "ik_iw" else 4 * COLS if kind == "branch" else FULL for kind in ORDER]
        TASKS = {3: ["ik"], 5: ["q"], 7: ["k"], 9: ["iq"], 16: ["conv_in"], 20: ["conv_gate"],
                 22: ["pooled"], 24: ["pool_gate"], 25: ["pool_mix"], 34: ["attn_out"]}
        for h in range(HEADS):
            TASKS.setdefault(10 + h, []).append(("index", h))
        TASKS.setdefault(18, []).append(("select", 0))
        TASKS.setdefault(20, []).append(("select", 1))
        for s in range(HEADS + 2):
            TASKS.setdefault(21 + s, []).append(("unit", s))
        TASKS[20].append(("split", 0))
        TASKS.setdefault(32, []).append(("split", 1))
        TASKS.setdefault(40, []).append(("split", 2))

        def run_tasks(tasks, slot):
            for task in TASKS.get(slot, []):
                name, args = (task, ()) if isinstance(task, str) else (task[0], task[1:])
                tasks[name](*args)

        def first_size(i):
            if i >= len(stages):
                return None
            return {"mlstm": KD * 2 * HEADS, "mix2": KD * IKW}.get(stages[i][0], FULL)

        block = ctx.enter_context(nc.Block())

        @block.sync
        def _(sp):
            at = At()

            def load(chunk, slot, wait, dst_src):
                if wait is not None:
                    sp.wait_ge(lo_ready, wait)
                for dst, src in dst_src:
                    sp.dma_start(dst, src).then_inc(raw_ready[slot], 16)

            def tiles(slot, k, n):
                return RAW[:, slot, 0:k * n].rearrange("p (k n) -> p k n", k=k)

            def load_cols(w, k0, k, col, n):
                c = at.chunk
                dst = tiles(c % 2, k, n)
                src = w.rearrange("(k p) n -> p k n", p=P)[:, k0:k0 + k, col:col + n]
                cut = k // 2
                load(c, c % 2, c - 1 if c >= 2 else None,
                     [(dst[:, :cut, :], src[:, :cut, :]), (dst[:, cut:, :], src[:, cut:, :])])
                at.chunk += 1

            def ffn(layer, which):
                wg = ffn_w_gate[layer, which].rearrange("(k p) n -> p k n", p=P)
                wu = ffn_w_up[layer, which].rearrange("(k p) n -> p k n", p=P)
                c0 = at.chunk

                def gate_up(j, slot, wait):
                    dst = tiles(slot, KD, COLS)
                    load(None, slot, wait,
                         [(dst[:, :, 0:GU], wg[:, :, bass.ds(j * GU, GU)]),
                          (dst[:, :, GU:COLS], wu[:, :, bass.ds(j * GU, GU)])])

                first = 3 if c0 == 0 else 1
                for j in range(first):
                    c = c0 + j
                    gate_up(j, c % 2, c - 1 if c >= 2 else None)
                with sp.Fori(0, (NGU - first) // 2) as i:
                    for odd in range(2):
                        j = 2 * i + (first + odd)
                        gate_up(j, (c0 + first + odd) % 2, 2 * i + (c0 + first + odd - 1))
                at.chunk += NGU
                for half in range(2):
                    k0 = 0
                    for k in DOWN:
                        load_cols(ffn_w_down[layer, which], k0, k, half * COLS, COLS)
                        k0 += k

            def attn(layer):
                for col in (0, 1, 3, 4, 2, 5):
                    load_cols(attn_w_in[layer], 0, KD, col * COLS, COLS)
                for half in range(2):
                    load_cols(attn_w_out[layer], 0, KD, half * COLS, COLS)

            def mlstm(layer):
                load_cols(mlstm_w_in[0], 0, KD, 4 * D, 2 * HEADS)
                for j in range(8):
                    load_cols(mlstm_w_in[0], 0, KD, j * COLS, COLS)
                for half in range(2):
                    load_cols(mlstm_w_out[0], 0, KD, half * COLS, COLS)

            def mix2(layer):
                mgate = branch = out_half = 0
                for kind in ORDER:
                    if kind == "mgate":
                        gate = BRANCHES[mgate // 2][1]
                        load_cols(w_in_2[layer], 0, KD, W2["mgate"] + gate * D + (mgate % 2) * COLS, COLS)
                        mgate += 1
                    elif kind == "branch":
                        load_cols(BRANCHES[branch // 2][0][layer], 0, 4, (branch % 2) * COLS, COLS)
                        branch += 1
                    elif kind == "out":
                        load_cols(w_o_2[layer], 0, KD, out_half * COLS, COLS)
                        out_half += 1
                    else:
                        load_cols(w_in_2[layer], 0, KD, W2[kind], IKW if kind == "ik_iw" else COLS)

            for tok in range(NTOK):
                sp.dma_start(X[:, tok, :], x[0].rearrange("(t p) d -> p t d", p=P)[:, tok, :]).then_inc(x_loaded, 16)
            sp.dma_start(CT[:, :], c_tiles).then_inc(consts_loaded, 16)
            sp.dma_start(ONEHOT[:, :], c_onehot).then_inc(consts_loaded, 16)
            sp.dma_start(RB[0:32, :], rel_bias).then_inc(consts_loaded, 16)
            for stage in stages:
                {"ffn": ffn, "attn": attn, "mlstm": mlstm, "mix2": mix2}[stage[0]](*stage[1:])
            sp.wait_ge(blocks_used, last_block + 1)
            for tok in range(NTOK):
                sp.dma_start(out[0].rearrange("(t p) d -> p t d", p=P)[:, tok, :], X[:, tok, :]).then_inc(out_stored, 16)
            sp.wait_ge(out_stored, 16 * NTOK)

        @block.tensor
        def _(pe):
            at = At()

            def product(xh, xl, chunk, slot, b_wait, block_odd, k0, k, n, first, last, between=None,
                        acc_of=None):
                pe.wait_ge(lo_ready, chunk + 1)
                if first:
                    pe.wait_ge(blocks_used, b_wait)
                wh = WH[:, slot, 0:k * n].rearrange("p (k n) -> p k n", k=k)
                wl = WL[:, slot, 0:k * n].rearrange("p (k n) -> p k n", k=k)
                for tok in range(NTOK):
                    bank = acc_of(tok) if acc_of else ACC[:, block_odd * 2 + tok, 0:n]
                    for i in range(k):
                        lh = xh[:, k0 + i, tok * P:(tok + 1) * P]
                        ll = xl[:, k0 + i, tok * P:(tok + 1) * P]
                        nc.tensor.matmul(bank, lh, wl[:, i, :], start=first and i == 0, stop=False)
                        nc.tensor.matmul(bank, lh, wh[:, i, :], start=False, stop=False)
                        mm = nc.tensor.matmul(bank, ll, wh[:, i, :], start=False, stop=last and i == k - 1)
                    if tok == 0:
                        if last:
                            mm.then_inc(tile0_ready, 1)
                        if between:
                            between()
                mm.then_inc(weights_used, 1)

            def group(bank_odd, used, source, wait=None):
                if wait:
                    pe.wait_ge(*wait)
                pe.wait_ge(groups_used, used)
                for kk in range(2):
                    for tok in range(NTOK):
                        o = (kk * NTOK + tok) * P
                        mm = nc.tensor.transpose(TB[bank_odd][:, o:o + P], source(tok, kk), ident)
                mm.then_inc(groups_ready, 1)

            def activations(wait):
                for g in range(KD // 2):
                    group(at.group % 2, at.group,
                          lambda tok, kk: XN[:, tok, (2 * g + kk) * P:(2 * g + kk + 1) * P],
                          wait if g == 0 else None)
                    at.group += 1
                pe.wait_ge(groups_used, at.group + 1)

            def prenorm():
                at.normed += NTOK
                activations((normed, at.normed))

            def out_product():
                for half in range(2):
                    product(XH, XL, at.chunk, at.chunk % 2, at.block + 1, half, 0, KD, COLS, True, True)
                    at.chunk += 1
                at.block += 2

            def ffn(layer, which):
                prenorm()
                c0, b0, t0 = at.chunk, at.block, at.group

                def hidden(bank_odd, g, b):
                    group(bank_odd, g, lambda tok, kk: ST[:, tok, kk * P:(kk + 1) * P],
                          (blocks_used, b + 2))

                product(XH, XL, c0, c0 % 2, b0, b0 % 2, 0, KD, COLS, True, True)
                with pe.Fori(0, (NGU - 1) // 2) as i:
                    for odd in range(2):
                        j = 2 * i + (1 + odd)
                        product(XH, XL, j + c0, (c0 + 1 + odd) % 2, j + b0, (b0 + 1 + odd) % 2, 0, KD, COLS,
                                True, True,
                                between=lambda: hidden((t0 + odd) % 2, j + (t0 - 1), j + (b0 - 1)))
                hidden((t0 + NGU - 1) % 2, t0 + NGU - 1, b0 + NGU - 1)
                at.chunk += NGU
                at.block += NGU
                at.group += NGU
                pe.wait_ge(groups_used, at.group + 1)
                c0, b0 = at.chunk, at.block
                with pe.Fori(0, 2) as half:
                    k0 = 0
                    for q, k in enumerate(DOWN):
                        product(HH, HL, half * len(DOWN) + (c0 + q), (c0 + q) % 2, b0 + 1, None,
                                k0, k, COLS, q == 0, q == len(DOWN) - 1,
                                acc_of=lambda tok: ACC[:, bass.ds(half * 2 + tok, 1), :])
                        k0 += k
                at.chunk += 2 * len(DOWN)
                at.block += 2
                at.normed += 4

            def staged(j_groups, used, b, of=ST):
                for g in range(2):
                    group(j_groups[g], used + g, lambda tok, kk: ST[:, tok, (2 * g + kk) * P:(2 * g + kk + 1) * P],
                          (blocks_used, b + 2) if g == 0 else None)

            def projections(n_staged, n_more, hooks=()):
                c0, b0, t0 = at.chunk, at.block, at.group

                def multiply(j, odd, between=None):
                    product(XH, XL, j + c0, (c0 + odd) % 2, j + b0, (b0 + odd) % 2, 0, KD, COLS, True, True,
                            between=between)

                multiply(0, 0)
                with pe.Fori(0, n_staged // 2) as i:
                    for k in range(2):
                        j = 2 * i + (1 + k)
                        multiply(j, 1 + k, lambda: staged([t0 % 2, (t0 + 1) % 2], 4 * i + (t0 + 2 * k), 2 * i + (b0 + k)))
                for j in range(n_staged + 1, n_staged + n_more):
                    hook = hooks[j - n_staged - 1] if hooks else None
                    multiply(j, j, (lambda: hook(t0 + 2 * n_staged + j - n_staged - 1)) if hook else None)
                at.chunk += n_staged + n_more
                at.block += n_staged + n_more
                at.group += 2 * n_staged

            def units(n, scores, weigh, z_taken):
                pe.wait_ge(blocks_used, at.block + 1)
                u0, t0 = at.unit, at.group
                for s in range(n + 2):
                    if s < n:
                        if s >= 2:
                            pe.wait_ge(*z_taken(s - 2, u0))
                        scores(s, ACC[:, s % 2, 0:3 * P]).then_inc(z_ready, 1)
                    if 1 <= s <= n:
                        u = s - 1
                        t = t0 + u
                        pe.wait_ge(w_ready, u0 + u + 1)
                        pe.wait_ge(groups_used, t)
                        for i in range(3):
                            mm = nc.tensor.transpose(TB[t % 2][:, i * P:(i + 1) * P], UW[:, u % 2, i * P:(i + 1) * P], ident)
                        mm.then_inc(groups_ready, 1)
                    if s >= 2:
                        u = s - 2
                        pe.wait_ge(groups_used, t0 + u + 2)
                        if u >= 2:
                            pe.wait_ge(o_used, u0 + u - 1)
                        weigh(u, ACC[:, 2 + u % 2, 0:2 * (DH + 1)].rearrange("p (t e) -> p t e", t=2),
                              UT[:, u % 2, :]).then_inc(o_ready, 1)
                at.unit += n
                at.group += n

            def head_scores(q, k, z, add=None):
                for lo, hi, queries in ((0, P, slice(0, P)), (P, 3 * P, slice(P, 2 * P))):
                    mm = nc.tensor.matmul(z[:, lo:hi], q[:, queries], k[:, 0:hi - lo], start=True, stop=add is None)
                    if add:
                        table = add[1][:, lo:hi] if add[1] is MK else add[1][:, SEQ - (hi - lo):]
                        mm = nc.tensor.matmul(z[:, lo:hi], add[0], table, start=False, stop=True)
                return mm

            def head_output(v, o, w, n):
                nc.tensor.matmul(o[:, 0, 0:n], w[:, 0:P], v(0), start=True, stop=True)
                nc.tensor.matmul(o[:, 1, 0:n], w[:, P:2 * P], v(0), start=True, stop=False)
                return nc.tensor.matmul(o[:, 1, 0:n], w[:, 2 * P:3 * P], v(1), start=False, stop=True)

            def attn(layer):
                prenorm()
                projections(4, 2)
                pe.wait_ge(groups_used, at.group + 1)

                def scores(s, z):
                    side, h = divmod(s, HEADS)
                    part = slice(DH * (h % 2), DH * (h % 2) + DH)
                    if s == HEADS:
                        pe.wait_ge(bias_ready, 16)
                    return head_scores(QT[part, 2 * side, h // 2, :], QT[part, 2 * side + 1, h // 2, :], z,
                                       (flip, BT[:, h, :]) if side else None)

                def weigh(u, o, w):
                    side, h = divmod(u, HEADS)
                    n = DH + side
                    return head_output(lambda t: VS[:, side, t, h, 0:n], o, w, n)

                units(2 * HEADS, scores, weigh,
                      lambda u, u0: (logits_ready if u < HEADS else w_ready, u0 + u + 1))
                activations((o_used, at.unit))
                out_product()
                at.normed += 4

            def small_group(t, wait, products):
                pe.wait_ge(*wait)
                pe.wait_ge(groups_used, t)
                for mm in products(TB[t % 2]):
                    pass
                mm.then_inc(groups_ready, 1)

            def mlstm(layer):
                prenorm()
                product(XH, XL, at.chunk, at.chunk % 2, at.block, at.block % 2, 0, KD, 2 * HEADS, True, True)
                at.chunk += 1
                at.block += 1

                def running_sums(t):
                    small_group(t, (gates_dve, 1), lambda bank: [
                        nc.tensor.matmul(bank[:, tok * HEADS:(tok + 1) * HEADS], upto, LF[:, tok, :], start=True, stop=True)
                        for tok in range(NTOK)])

                def by_head(t):
                    small_group(t, (groups_used, t + 1), lambda bank: [
                        nc.tensor.transpose(bank[0:HEADS, i * P:(i + 1) * P], src, ident)
                        for i, src in enumerate((VV[:, 0, :], VV[:, 1, :], BC[:, 0, :]))])

                def by_token(t):
                    small_group(t, (gates_dve, 2), lambda bank: [
                        nc.tensor.transpose(bank[:, c * HEADS:(c + 1) * HEADS], MU[:, c * P:(c + 1) * P],
                                            ident[0:HEADS, 0:HEADS]) for c in range(NTOK)] + [
                        nc.tensor.matmul(bank[:, 2 * HEADS:4 * HEADS], one[0:HEADS, :].broadcast_to([HEADS, P]), DG[:, :],
                                         start=True, stop=True)])

                projections(4, 4, (running_sums, by_head, by_token))
                at.group += 3
                for g in range(2):
                    small_group(at.group, (silus, 8), lambda bank: [
                        nc.tensor.transpose(bank[:, i * P:(i + 1) * P], QK[:, HEADS + 4 * g + i, 0:P], ident) for i in range(4)])
                    at.group += 1
                for h0 in range(0, HEADS, 3):
                    small_group(at.group, (groups_used, at.group if h0 else at.group + 1), lambda bank: [
                        nc.tensor.matmul(bank[:, i * (P + 1):(i + 1) * (P + 1)], KN[:, h0 + i, :], VA[:, 0, h0 + i, :],
                                         start=True, stop=True) for i in range(min(3, HEADS - h0))])
                    at.group += 1
                pe.wait_ge(groups_used, at.group + 1)
                pe.wait_ge(blocks_used, at.block + 1)
                u0 = at.unit
                for s in range(HEADS + 1):
                    if s < HEADS:
                        if s >= 2:
                            pe.wait_ge(logits_ready, u0 + s - 1)
                        z = ACC[:, s % 2, :]
                        for c in range(NTOK):
                            t = slice(c * P, (c + 1) * P)
                            nc.tensor.matmul(z[:, t], QK[:, HEADS + s, t], QK[:, s, t], start=True, stop=True)
                        m = z[:, SEQ:2 * SEQ]
                        nc.tensor.matmul(m, ident[0:HEADS, s:s + 1].broadcast_to([HEADS, P]), MU[:, :], start=True, stop=False)
                        nc.tensor.matmul(m.rearrange("p (c t) -> p c t", c=2), ident,
                                         after.unsqueeze(1).broadcast_to([P, 2, P]), start=False, stop=True).then_inc(z_ready, 1)
                    if s >= 1:
                        h = s - 1
                        pe.wait_ge(logits_ready, u0 + h + 1)
                        if h >= 2:
                            pe.wait_ge(o_used, u0 + h - 1)
                        o = ACC[:, 2 + h % 2, 0:3 * (P + 1)].rearrange("p (i e) -> p i e", i=3)
                        for c in range(NTOK):
                            nc.tensor.matmul(o[:, c, :], PT[:, h % 2, c * P:(c + 1) * P], VA[:, c, h, :], start=True, stop=True)
                        nc.tensor.matmul(o[:, 2, :], QK[:, h, P:2 * P], CA[:, h, :], start=True, stop=True).then_inc(o_ready, 1)
                at.unit += HEADS
                activations((mixed, 1))
                out_product()
                at.normed += 8

            def mix2(layer):
                prenorm()
                mid = XN[:, :, 0:COLS], XN[:, :, COLS:D]

                def transposes(of, wait):
                    for g in range(2):
                        group(at.group % 2, at.group, lambda tok, kk: of[:, tok, (2 * g + kk) * P:(2 * g + kk + 1) * P],
                              wait if g == 0 else None)
                        at.group += 1

                def roped(of):
                    at.staged += 1
                    transposes(of, (rope_done, at.staged))

                def taken_out(kind):
                    return (blocks_used, b0 + ORDER.index(kind) + 2)

                b0 = at.block

                def ik():
                    at.staged += 1
                    pe.wait_ge(rope_done, at.staged)
                    pe.wait_ge(groups_used, at.group)
                    for tok in range(NTOK):
                        mm = nc.tensor.transpose(TB[at.group % 2][:, tok * P:(tok + 1) * P], ST[:, tok, 0:P], ident)
                    mm.then_inc(groups_ready, 1)
                    at.group += 1

                def halves(h):
                    return slice(DH * (h % 2), DH * (h % 2) + DH)

                def index(h):
                    if h == 0:
                        pe.wait_ge(groups_used, at.group + 1)
                    if at.index:
                        pe.wait_ge(relu_ready, at.index)
                    head_scores(QT2[halves(h), 2, h // 2, :], IKT[halves(h), :], ZB[:, 0:3 * P]).then_inc(index_z_ready, 1)
                    at.index += 1

                def unit(s):
                    u0 = at.unit
                    if s < HEADS:
                        if s == 0:
                            pe.wait_ge(relu_ready, at.index)
                            pe.wait_ge(mask_ready, layer + 1)
                        else:
                            pe.wait_ge(w_ready, u0 + s)
                        head_scores(QT2[halves(s), 0, s // 2, :], QT2[halves(s), 1, s // 2, :], ZB[:, 0:3 * P],
                                    (ident, MK)).then_inc(z_ready, 1)
                    if 1 <= s <= HEADS:
                        u = s - 1
                        pe.wait_ge(w_ready, u0 + u + 1)
                        pe.wait_ge(groups_used, at.group)
                        for i in range(3):
                            mm = nc.tensor.transpose(TB[at.group % 2][:, i * P:(i + 1) * P], UW[:, u % 2, i * P:(i + 1) * P], ident)
                        mm.then_inc(groups_ready, 1)
                        at.group += 1
                        unit_group.append(at.group)
                    if s >= 2:
                        u = s - 2
                        pe.wait_ge(groups_used, unit_group[u] + 1)
                        if u >= 1:
                            pe.wait_ge(o_used, u0 + u)
                        head_output(lambda t: V2[:, t, u, :], OB[:, 0:2 * (DH + 1)].rearrange("p (t e) -> p t e", t=2),
                                    UT[:, u % 2, :], DH + 1).then_inc(o_ready, 1)
                    if s == HEADS + 1:
                        at.unit += HEADS

                def pooled():
                    pe.wait_ge(*taken_out("pu"))
                    for g2 in range(2):
                        pe.wait_ge(groups_used, at.group)
                        for k in range(2):
                            g = 2 * g2 + k
                            bank = TB[at.group % 2][:, k * SEQ:(k + 1) * SEQ]
                            u = [SX[:, tok, g * P:(g + 1) * P] for tok in range(NTOK)]
                            nc.tensor.matmul(bank[:, 0:P], u[0], PM[:, g, 0:P], start=True, stop=True)
                            nc.tensor.matmul(bank[:, P:SEQ], u[1], PM[:, g, P:2 * P], start=True, stop=False)
                            mm = nc.tensor.matmul(bank[:, P:P + WINDOWS[-1]], u[0], PM[:, g, 2 * P:], start=False, stop=True)
                        mm.then_inc(groups_ready, 1)
                        at.group += 1

                def pool_mix():
                    pe.wait_ge(pool_w_loaded, 16 * (layer + 1))
                    pe.wait_ge(groups_used, at.group + 1)
                    for g2 in range(2):
                        pe.wait_ge(groups_used, at.group)
                        for k in range(2):
                            g = 2 * g2 + k
                            mm = nc.tensor.matmul(TB[at.group % 2][:, k * SEQ:(k + 1) * SEQ], PW[:, g, :], PL[:, g, :],
                                                  start=True, stop=True)
                        mm.then_inc(groups_ready, 1)
                        at.group += 1

                def attn_out():
                    pe.wait_ge(o_used, at.unit)
                    for g in range(2):
                        group(at.group % 2, at.group, lambda tok, kk: AG[:, tok, (2 * g + kk) * P:(2 * g + kk + 1) * P])
                        at.group += 1

                unit_group = []
                tasks = dict(ik=ik, q=lambda: roped(mid[0]), k=lambda: roped(mid[1]), iq=lambda: roped(ST),
                             conv_in=lambda: transposes(mid[0], taken_out("cc")),
                             conv_gate=lambda: transposes(mid[1], taken_out("cb")),
                             pool_gate=lambda: transposes(ST, taken_out("pgate")), pooled=pooled, pool_mix=pool_mix, attn_out=attn_out,
                             index=index, unit=unit, select=lambda tile: None, split=lambda branch: None)
                branch = 0
                for b, kind in enumerate(ORDER):
                    if kind == "branch":
                        if branch % 2 == 0:
                            pe.wait_ge(branch_ready, 3 * layer + branch // 2 + 1)
                        branch += 1
                    if kind == "out" and ORDER[b - 1] != "out":
                        pe.wait_ge(blocks_used, at.block + 1)
                        activations(None)
                    xh, xl, k, n = (BH, BL, 4, COLS) if kind == "branch" else (XH, XL, KD, IKW if kind == "ik_iw" else COLS)
                    product(xh, xl, at.chunk, at.chunk % 2, at.block, at.block % 2, 0, k, n, True, True,
                            between=lambda: run_tasks(tasks, 2 * b))
                    run_tasks(tasks, 2 * b + 1)
                    at.chunk += 1
                    at.block += 1

            pe.sem_inc(weights_used, 1)
            pe.wait_ge(consts_loaded, 48)
            pe.wait_ge(mask_set, 1)
            nc.tensor.matmul(TB[0][0:HEADS, 0:3 * P], RB[:, :], ONEHOT[:, :], start=True, stop=True)\
                .then_inc(bias_summed, 1)
            pe.wait_ge(bias_rows, 1)
            for stage in stages:
                {"ffn": ffn, "attn": attn, "mlstm": mlstm, "mix2": mix2}[stage[0]](*stage[1:])

        @block.scalar
        def _(act):
            at = At()

            def split_hi(c, slot, raw_wait, size):
                act.wait_ge(raw_ready[slot], raw_wait)
                if not (isinstance(c, int) and c == 0):
                    act.wait_ge(weights_used, c)
                nc.scalar.activation(WH[:, slot, 0:size], RAW[:, slot, 0:size], ACT.Copy).then_inc(hi_ready, 1)

            def split_next(size):
                c = at.chunk + 1
                if size:
                    split_hi(c, c % 2, raw_value(c), size)

            def group_hi(bank_odd, ready, dst):
                act.wait_ge(groups_ready, ready)
                nc.scalar.activation(dst, TB[bank_odd][:, :], ACT.Copy).then_inc(groups_hi, 1)

            def activations():
                for g in range(KD // 2):
                    group_hi(at.group % 2, at.group + 1, XH[:, 2 * g:2 * g + 2, :].rearrange("p k n -> p (k n)"))
                    at.group += 1

            def square(src, dst, col):
                nc.scalar.activation(dst, src, ACT.Square, accum_out=SS[:, col:col + 1]).then_inc(squares, 1)

            def prenorm():
                act.wait_ge(blocks_used, at.block + 1)
                for tok in range(NTOK):
                    square(X[:, tok, :], XN[:, tok, :], tok)
                activations()

            def block_ready(tok, last_chunk, block):
                if tok == 0:
                    act.wait_ge(tile0_ready, block + 1)
                else:
                    act.wait_ge(weights_used, last_chunk + 2)

            def postnorm(chunks_per_half):
                for half in range(2):
                    b = at.block - 2 + half
                    c = at.chunk - 1 - (1 - half) * chunks_per_half
                    for tok in range(NTOK):
                        block_ready(tok, c, b)
                        square(ACC[:, half * 2 + tok, :], XN[:, tok, half * COLS:(half + 1) * COLS], half * 2 + tok)

            def ffn(layer, which, next_size):
                prenorm()
                c0, b0, t0 = at.chunk, at.block, at.group

                def silu(b, b_odd, c):
                    for tok in range(NTOK):
                        block_ready(tok, c, b)
                        if tok == 0:
                            act.wait_ge(blocks_used, b + 1)
                        nc.scalar.activation(SIDE[:, tok, :], ACC[:, b_odd * 2 + tok, 0:GU], ACT.Silu)\
                            .then_inc(silu_ready, 1)

                split_next(SLOT)
                silu(b0, b0 % 2, c0)
                with act.Fori(0, (NGU - 1) // 2) as i:
                    for odd in range(2):
                        j = 2 * i + (1 + odd)
                        n = c0 + 2 + odd
                        split_hi(2 * i + n, n % 2, 32 * i + raw_value(n), SLOT)
                        group_hi((t0 + odd) % 2, j + t0,
                                 HH[:, bass.ds(4 * i + 2 * odd, 2), :].rearrange("p k n -> p (k n)"))
                        silu(j + b0, (b0 + 1 + odd) % 2, j + c0)
                group_hi((t0 + NGU - 1) % 2, t0 + NGU,
                         HH[:, KF - 2:KF, :].rearrange("p k n -> p (k n)"))
                at.chunk += NGU
                at.block += NGU
                at.group += NGU
                for size in DOWN_SIZES[1:] + [next_size]:
                    split_next(size)
                    at.chunk += 1
                at.block += 2
                postnorm(len(DOWN))

            def stage_block(j, scale):
                if j > 0:
                    act.wait_ge(groups_ready, at.group)
                for tok in range(NTOK):
                    block_ready(tok, at.chunk, at.block)
                    ins = nc.scalar.activation(ST[:, tok, :], ACC[:, (at.block % 2) * 2 + tok, :], ACT.Copy, scale=scale)
                ins.then_inc(blocks_used, 1)

            def out_product(next_size):
                split_next(FULL)
                at.chunk += 1
                split_next(next_size)
                at.chunk += 1
                at.block += 2
                postnorm(1)

            def attn(layer, next_size):
                prenorm()
                for j in range(6):
                    split_next(FULL)
                    if j < 4:
                        stage_block(j, DH ** -0.5 if j % 2 == 0 else 1.0)
                        at.group += 2
                    else:
                        for tok in range(NTOK):
                            block_ready(tok, at.chunk, at.block)
                            ins = nc.scalar.activation(VS[:, j - 4, tok, :, 0:DH],
                                                       ACC[:, (at.block % 2) * 2 + tok, :].rearrange("p (h e) -> p h e", e=DH),
                                                       ACT.Copy)
                        ins.then_inc(blocks_used, 1)
                    at.chunk += 1
                    at.block += 1
                act.preload_act_table_set("natural_log_exp_and_others")
                u0, t0 = at.unit, at.group
                n = 2 * HEADS
                for s in range(n + 1):
                    if s < HEADS:
                        z = ACC[:, s % 2, 0:3 * P]
                        a = UA[:, s % 2, :]
                        at.ln += 1
                        act.wait_ge(z_ready, u0 + s + 1)
                        if s >= 2:
                            act.wait_ge(logits_ready, u0 + s - 1)
                        nc.scalar.activation(a, z, ACT.Abs).then_inc(abs_ready, 1)
                        act.wait_ge(abs_ready, at.ln)
                        nc.scalar.activation(a, a, ACT.Exp, scale=-1.0).then_inc(exp_ready, 1)
                        act.wait_ge(exp_ready, at.ln)
                        nc.scalar.activation(a, a, ACT.Ln, bias=1.0).then_inc(ln_ready, 1)
                    if s >= 1:
                        u = s - 1
                        act.wait_ge(logits_ready, u0 + u + 1)
                        if u >= 2:
                            act.wait_ge(groups_ready, t0 + u - 1)
                        if u < HEADS:
                            nc.scalar.activation(UW[:, u % 2, :], UL[:, u % 2, :], ACT.Exp).then_inc(w_ready, 1)
                        else:
                            softmax_exp(u)
                at.unit += n
                at.group += n
                activations()
                out_product(next_size)

            def mlstm(layer, next_size):
                prenorm()
                split_next(FULL)
                at.chunk += 1
                at.block += 1
                act.preload_act_table_set("natural_log_exp_and_others")
                at.ln += 1
                act.wait_ge(blocks_used, at.block + 1)
                nc.scalar.activation(LS[:, :, :], GT[:, :, HEADS:], ACT.Abs).then_inc(abs_ready, 1)
                act.wait_ge(abs_ready, at.ln)
                nc.scalar.activation(LS[:, :, :], LS[:, :, :], ACT.Exp, scale=-1.0).then_inc(exp_ready, 1)
                act.wait_ge(exp_ready, at.ln)
                nc.scalar.activation(LS[:, :, :], LS[:, :, :], ACT.Ln, bias=1.0).then_inc(gates_act, 1)
                t0 = at.group
                for j in range(8):
                    split_next(FULL)
                    if j < 4:
                        stage_block(j, 1.0)
                        at.group += 2
                    if 1 <= j < 5:
                        for g in range(2):
                            i = 2 * (j - 1) + g
                            act.wait_ge(groups_used, t0 + i + 2)
                            nc.scalar.activation(QK[:, 2 * i:2 * i + 2, :].rearrange("p k n -> p (k n)"), YC[:, i % 2, :],
                                                 ACT.Silu).then_inc(silus, 1)
                    if j >= 4:
                        side = j % 2
                        for tok in range(NTOK):
                            block_ready(tok, at.chunk, at.block)
                            src = ACC[:, (at.block % 2) * 2 + tok, :]
                            if j < 6:
                                ins = nc.scalar.activation(VA[:, tok, 4 * side:4 * side + 4, 0:P],
                                                           src.rearrange("p (h e) -> p h e", e=P), ACT.Copy)
                            else:
                                ins = nc.scalar.activation(SO[:, tok, side * COLS:(side + 1) * COLS], src, ACT.Sigmoid)
                        ins.then_inc(blocks_used, 1)
                    at.chunk += 1
                    at.block += 1
                at.group += 3
                act.wait_ge(gates_dve, 3)
                nc.scalar.activation(EX[:, :], EA[:, :], ACT.Exp).then_inc(gates_act, 1)
                act.wait_ge(gates_act, 2)
                for g in range(2):
                    act.wait_ge(groups_ready, at.group + 1)
                    for i in range(4):
                        h = 4 * g + i
                        ins = nc.scalar.activation(KN[:, h, :], TB[at.group % 2][:, i * P:(i + 1) * P], ACT.Copy,
                                                   scale=EX[:, h:h + 1])
                    ins.then_inc(groups_used, 1)
                    at.group += 1
                for h0 in range(0, HEADS, 3):
                    n = min(3, HEADS - h0)
                    act.wait_ge(groups_ready, at.group + 1)
                    nc.scalar.activation(CA[:, h0:h0 + n, :].rearrange("p h e -> p (h e)"),
                                         TB[at.group % 2][:, 0:n * (P + 1)], ACT.Copy).then_inc(groups_used, 1)
                    at.group += 1
                u0 = at.unit
                for s in range(HEADS + 2):
                    if s < HEADS:
                        act.wait_ge(z_ready, u0 + s + 1)
                        if s >= 2:
                            act.wait_ge(logits_ready, u0 + s - 1)
                        for c in range(NTOK):
                            ins = nc.scalar.activation(DT[:, s % 2, c * P:(c + 1) * P],
                                                       ACC[:, s % 2, SEQ + c * P:SEQ + (c + 1) * P], ACT.Exp,
                                                       bias=VV[:, c, s:s + 1], scale=-1.0)
                        ins.then_inc(w_ready, 1)
                    if 1 <= s <= HEADS:
                        h = s - 1
                        act.wait_ge(o_ready, u0 + h + 1)
                        o = ACC[:, 2 + h % 2, 0:2 * (P + 1)].rearrange("p (i e) -> p i e", i=2)
                        nc.scalar.activation(XN[:, :, h * P:(h + 1) * P], o[:, :, 0:P], ACT.Copy).then_inc(ho_ready, 1)
                    if s >= 2:
                        h = s - 2
                        act.wait_ge(o_used, u0 + h + 1)
                        for c in range(NTOK):
                            nc.scalar.activation(SIDE[:, 0, 0:P], XN[:, c, h * P:(h + 1) * P], ACT.Square,
                                                 accum_out=HS[:, c, h:h + 1]).then_inc(heads_squared, 1)
                            act.wait_ge(heads_squared, 2 * h + c + 1)
                at.unit += HEADS
                activations()
                out_product(next_size)

            def mix2(layer, next_size):
                prenorm()

                def skip(n):
                    at.group += n

                def index(h):
                    at.index += 1
                    act.wait_ge(index_z_ready, at.index)
                    if at.index > 2:
                        act.wait_ge(index_summed, at.index - 2)
                    nc.scalar.activation(UA[:, h % 2, :], ZB[:, 0:3 * P], ACT.Relu, scale=DH ** -0.5).then_inc(relu_ready, 1)

                def unit(s):
                    if s < HEADS:
                        act.wait_ge(logits_ready, at.unit + s + 1)
                        if s >= 2:
                            act.wait_ge(groups_ready, unit_group[s - 2] + 1)
                        softmax_exp(s, ZB[:, 0:3 * P])
                    if 1 <= s <= HEADS:
                        unit_group.append(at.group)
                        at.group += 1
                    if s == HEADS + 1:
                        at.unit += HEADS

                def split(branch):
                    at.branch += 1
                    act.wait_ge(groups_used, at.group + 1)
                    if branch:
                        act.wait_ge(weights_used, at.chunk + 1)
                    nc.scalar.activation(BH[:, :, :], YT[:, :, :], ACT.Copy).then_inc(branch_hi, 1)

                unit_group = []
                tasks = dict(ik=lambda: skip(1), index=index, unit=unit, select=lambda tile: None, split=split)
                for name in ("q", "k", "iq", "conv_in", "conv_gate", "pooled", "pool_gate", "pool_mix", "attn_out"):
                    tasks[name] = lambda: skip(2)

                def take_out(dst, func, n=COLS):
                    for tok in range(NTOK):
                        block_ready(tok, at.chunk, at.block)
                        src = ACC[:, (at.block % 2) * 2 + tok, 0:n]
                        if dst is V2:
                            src = src.rearrange("p (h e) -> p h e", e=DH)
                            ins = nc.scalar.activation(V2[:, tok, :, 0:DH], src, func)
                        else:
                            ins = nc.scalar.activation(dst[:, tok, 0:n], src, func)
                    ins.then_inc(blocks_used, 1)

                for b, kind in enumerate(ORDER):
                    if b + 1 < len(ORDER):
                        split_next(SIZES[b + 1])
                    else:
                        split_next(next_size)
                    run_tasks(tasks, 2 * b)
                    if kind in ("ik_iw", "q", "k", "iq"):
                        if b:
                            act.wait_ge(rope_done, at.staged)
                        at.staged += 1
                        if kind in ("q", "k"):
                            for tok in range(NTOK):
                                block_ready(tok, at.chunk, at.block)
                                nc.scalar.activation(SQ[:, tok, :], ACC[:, (at.block % 2) * 2 + tok, :], ACT.Square)
                        take_out(QS, ACT.Copy, IKW if kind == "ik_iw" else COLS)
                    elif kind == "v":
                        take_out(V2, ACT.Copy)
                    elif kind == "agate":
                        take_out(AG, ACT.Silu)
                    elif kind in ("cx", "cgate", "pu"):
                        if kind != "cx":
                            act.wait_ge(blocks_used, at.block + 1)
                        take_out(SX, {"cgate": ACT.Silu}.get(kind, ACT.Copy))
                    elif kind == "pgate":
                        take_out(ST, ACT.Silu)
                    elif kind == "mgate":
                        act.wait_ge(blocks_used, at.block + 1)
                        act.wait_ge(groups_ready, at.group)
                        take_out(ST, ACT.Sigmoid)
                    run_tasks(tasks, 2 * b + 1)
                    at.chunk += 1
                    at.block += 1
                    if b + 1 < len(ORDER) and ORDER[b + 1] == "out" and kind != "out":
                        activations()

            def softmax_exp(u, z=None):
                z = ACC[:, u % 2, 0:3 * P] if z is None else z
                nc.scalar.activation(UW[:, u % 2, 0:P], z[:, 0:P], ACT.Exp, bias=NM[:, u % 2, 0:1])
                nc.scalar.activation(UW[:, u % 2, P:3 * P], z[:, P:3 * P], ACT.Exp,
                                     bias=NM[:, u % 2, 1:2]).then_inc(w_ready, 1)

            split_hi(0, 0, raw_value(0), SLOT)
            act.wait_ge(x_loaded, 16 * NTOK)
            for i, stage in enumerate(stages):
                {"ffn": ffn, "attn": attn, "mlstm": mlstm, "mix2": mix2}[stage[0]](*stage[1:], first_size(i + 1))

        @block.gpsimd
        def _(pool):
            at = At()
            steps = [0]

            def step(ins):
                steps[0] += 1
                ins.then_inc(pool_step, 1)
                pool.wait_ge(pool_step, steps[0])

            def load_row(r):
                if r < len(rows):
                    pool.dma_start(G[:, r % 2, :], rows[r].partition_broadcast(P)).then_inc(row_loaded[r % 2], 16)

            def rsqrt(n_squares, scale):
                at.square += n_squares
                pool.wait_ge(squares, at.square)
                src = SS[:, 0:2]
                if n_squares == 4:
                    step(nc.gpsimd.tensor_tensor(TMP2[:, :], SS[:, 0:2], SS[:, 2:4], ALU.add))
                    src = TMP2[:, :]
                step(nc.gpsimd.tensor_scalar(MS[:, :], src, 1.0 / D, EPS, ALU.mult, ALU.add))
                if scale is None:
                    nc.gpsimd.tensor_tensor(RS[:, :], MS[:, :], HALF[:, :], ALU.pow).then_inc(rsqrts, 1)
                else:
                    step(nc.gpsimd.tensor_tensor(TMP2[:, :], MS[:, :], HALF[:, :], ALU.pow))
                    nc.gpsimd.tensor_scalar(RS[:, :], TMP2[:, :], scale, 0.0, ALU.mult, ALU.add).then_inc(rsqrts, 1)

            def row_used(n):
                at.normed += n
                pool.wait_ge(normed, at.normed)
                load_row(at.row + 2)
                at.row += 1

            def ffn(layer, which):
                rsqrt(2, None)
                row_used(2)
                rsqrt(4, 0.5)
                row_used(4)
                at.block += BLOCKS["ffn"]

            def attn(layer):
                pool.wait_ge(blocks_used, at.block + 1)
                pool.dma_start(BT[:, :, :], bias_by_query).then_inc(bias_ready, 16)
                at.block += BLOCKS["attn"]
                rsqrt(2, None)
                row_used(2)
                rsqrt(4, None)
                row_used(4)

            def mlstm(layer):
                at.block += BLOCKS["mlstm"]
                rsqrt(2, None)
                row_used(2)
                row_used(4)
                pool.wait_ge(heads_ready, 1)
                hq = HQ[:, :, :].rearrange("p t h -> p (t h)")
                step(nc.gpsimd.tensor_scalar(hq, hq, 1.0 / P, EPS, ALU.mult, ALU.add))
                nc.gpsimd.tensor_tensor(HF[:, :, :].rearrange("p t h -> p (t h)"), hq, HALF16[:, :], ALU.pow)\
                    .then_inc(heads_scaled, 1)
                rsqrt(4, None)
                row_used(4)

            def mix2(layer):
                pool.wait_ge(blocks_used, at.block + 1)
                if layer == 0:
                    pool.dma_start(CS[:, :, :, :], c_rope).then_inc(tables_loaded, 16)
                    pool.dma_start(PM[:, :, :], c_pool).then_inc(tables_loaded, 16)
                pool.dma_start(PW[:, :, :], pool_w_2[layer].rearrange("g c d -> c g d")).then_inc(pool_w_loaded, 16)
                rsqrt(2, None)
                row_used(2)
                for i in range(2):
                    at.head_norm += 1
                    pool.wait_ge(head_sums, at.head_norm)
                    step(nc.gpsimd.tensor_scalar(HM[:, :], HN[:, :], 1.0 / DH, EPS, ALU.mult, ALU.add))
                    nc.gpsimd.tensor_tensor(HR[:, :], HM[:, :], HALF16[:, :], ALU.pow).then_inc(head_rsqrts, 1)
                at.block += BLOCKS["mix2"]

            for layer in range(DEPTH):
                for i, gains in enumerate((q_norm_g_2, k_norm_g_2)):
                    pool.dma_start(GQK[:, layer, i, :], gains[layer].partition_broadcast(P)).then_inc(small_loaded, 16)
            pool.dma_start(CW2[:, :, :, :], conv_taps_2).then_inc(small_loaded, 16)
            pool.dma_start(PS2[:, :, :], pool_scale_2).then_inc(small_loaded, 16)
            pool.dma_start(CW[:, :, :], conv_taps).then_inc(small_loaded, 16)
            pool.dma_start(BG[:, :], mlstm_b_gates[0].partition_broadcast(P)).then_inc(small_loaded, 16)
            step(nc.gpsimd.memset(HALF16[:, :], -0.5))
            nc.gpsimd.memset(RB[32:33, :], NEG).then_inc(mask_set, 1)
            pool.wait_ge(mask_set, 1)
            step(nc.gpsimd.memset(HALF[:, :], -0.5))
            load_row(0)
            load_row(1)
            pool.wait_ge(bias_rows, 1)
            pool.dma_start(bias_dram, BROW[:, :]).then_inc(bias_stored, 16)
            pool.wait_ge(bias_stored, 16)
            for stage in stages:
                {"ffn": ffn, "attn": attn, "mlstm": mlstm, "mix2": mix2}[stage[0]](*stage[1:])

        @block.vector
        def _(dve):
            at = At()

            def split_lo(c, slot, size):
                dve.wait_ge(hi_ready, c + 1)
                nc.vector.tensor_tensor(WL[:, slot, 0:size], RAW[:, slot, 0:size],
                                        WH[:, slot, 0:size].bitcast(F32), ALU.subtract).then_inc(lo_ready, 1)

            def split_next(size):
                c = at.chunk + 1
                if size:
                    split_lo(c, c % 2, size)

            def group_lo(bank_odd, hi, dst_lo, src_hi):
                dve.wait_ge(groups_hi, hi)
                nc.vector.tensor_tensor(dst_lo, TB[bank_odd][:, :], src_hi.bitcast(F32), ALU.subtract)\
                    .then_inc(groups_used, 1)

            def activations():
                for g in range(KD // 2):
                    group_lo(at.group % 2, at.rounded + 1, XL[:, 2 * g:2 * g + 2, :].rearrange("p k n -> p (k n)"),
                             XH[:, 2 * g:2 * g + 2, :].rearrange("p k n -> p (k n)"))
                    at.group += 1
                    at.rounded += 1

            def normed_tile(dst, src, tok, row):
                nc.vector.scalar_tensor_tensor(dst, src, RS[:, tok:tok + 1], row, ALU.mult, ALU.mult)\
                    .then_inc(normed, 1)

            def wait_norm():
                at.rsqrt += 1
                dve.wait_ge(rsqrts, at.rsqrt)
                dve.wait_ge(row_loaded[at.row % 2], 16 * (at.row // 2 + 1))
                at.row += 1

            def prenorm():
                row = G[:, at.row % 2, :]
                wait_norm()
                for tok in range(NTOK):
                    normed_tile(XN[:, tok, :], X[:, tok, :], tok, row)
                at.normed += NTOK
                activations()

            def postnorm():
                row = at.row % 2
                wait_norm()
                for half in range(2):
                    for tok in range(NTOK):
                        cols = slice(half * COLS, (half + 1) * COLS)
                        normed_tile(XN[:, tok, cols], ACC[:, half * 2 + tok, :], tok, G[:, row, cols])
                at.normed += 2 * NTOK
                dve.wait_ge(normed, at.normed)
                for tok in range(NTOK):
                    nc.vector.tensor_tensor(X[:, tok, :], X[:, tok, :], XN[:, tok, :], ALU.add)\
                        .then_inc(blocks_used, 1)

            def ffn(layer, which, next_size):
                prenorm()
                c0, b0, t0, g0 = at.chunk, at.block, at.group, at.rounded

                def gated(b_odd, silus, groups):
                    for tok in range(NTOK):
                        dve.wait_ge(silu_ready, silus + tok + 1)
                        if tok == 0:
                            dve.wait_ge(groups_ready, groups)
                        mul = nc.vector.tensor_tensor(ST[:, tok, 0:GU], SIDE[:, tok, :],
                                                      ACC[:, b_odd * 2 + tok, GU:COLS], ALU.mult)
                    mul.then_inc(blocks_used, 1)

                s0 = at.silu
                split_next(SLOT)
                gated(b0 % 2, s0, t0)
                with dve.Fori(0, (NGU - 1) // 2) as i:
                    for odd in range(2):
                        j = 2 * i + (1 + odd)
                        n = c0 + 2 + odd
                        split_lo(2 * i + n, n % 2, SLOT)
                        at_k = bass.ds(4 * i + 2 * odd, 2)
                        group_lo((t0 + odd) % 2, j + g0,
                                 HL[:, at_k, :].rearrange("p k n -> p (k n)"),
                                 HH[:, at_k, :].rearrange("p k n -> p (k n)"))
                        gated((b0 + 1 + odd) % 2, 2 * j + s0, j + t0)
                group_lo((t0 + NGU - 1) % 2, g0 + NGU,
                         HL[:, KF - 2:KF, :].rearrange("p k n -> p (k n)"),
                         HH[:, KF - 2:KF, :].rearrange("p k n -> p (k n)"))
                at.silu += 2 * NGU
                at.chunk += NGU
                at.block += NGU
                at.group += NGU
                at.rounded += NGU
                for size in DOWN_SIZES[1:] + [next_size]:
                    split_next(size)
                    at.chunk += 1
                at.block += 2
                postnorm()

            steps = [0]

            def step(ins):
                steps[0] += 1
                ins.then_inc(dve_step, 1)
                dve.wait_ge(dve_step, steps[0])

            def group_plain(dst):
                dve.wait_ge(groups_ready, at.group + 1)
                nc.vector.tensor_copy(dst, TB[at.group % 2][:, :]).then_inc(groups_used, 1)
                at.group += 1

            def out_product(next_size):
                split_next(FULL)
                at.chunk += 1
                split_next(next_size)
                at.chunk += 1
                at.block += 2
                postnorm()

            def softmax_maxima(u, z=None):
                z = ACC[:, u % 2, 0:3 * P] if z is None else z
                nc.vector.tensor_reduce(NM[:, u % 2, 0:1], z[:, 0:P], AX_X, ALU.max, negate=True)
                nc.vector.tensor_reduce(NM[:, u % 2, 1:2], z[:, P:3 * P], AX_X, ALU.max, negate=True)\
                    .then_inc(logits_ready, 1)

            def softmax_output(u, dst):
                o = ACC[:, 2 + u % 2, 0:2 * (DH + 1)].rearrange("p (t e) -> p t e", t=2)
                step(nc.vector.reciprocal(RD[:, u % 2, :].unsqueeze(2), o[:, :, DH:DH + 1]))
                nc.vector.tensor_tensor(dst, o[:, :, 0:DH], RD[:, u % 2, :].unsqueeze(2).broadcast_to([P, 2, DH]), ALU.mult)\
                    .then_inc(o_used, 1)

            def attn(layer, next_size):
                nc.vector.memset(VS[:, :, :, :, DH:DH + 1], 1.0)
                prenorm()
                for j in range(6):
                    split_next(FULL)
                    if 1 <= j < 5:
                        for g in range(2):
                            group_plain(QT[:, j - 1, 2 * g:2 * g + 2, :].rearrange("p k n -> p (k n)"))
                    at.chunk += 1
                    at.block += 1
                u0, t0 = at.unit, at.group
                n = 2 * HEADS
                for s in range(n + 2):
                    if s < HEADS:
                        z = ACC[:, s % 2, 0:3 * P]
                        a, l = UA[:, s % 2, :], UL[:, s % 2, :]
                        at.ln += 1
                        dve.wait_ge(ln_ready, at.ln)
                        step(nc.vector.scalar_tensor_tensor(a, z, 0.0, a, ALU.max, ALU.add))
                        if s >= 2:
                            dve.wait_ge(w_ready, u0 + s - 1)
                        for lo, hi in ((0, P), (P, 3 * P)):
                            ins = nc.vector.tensor_tensor_scan(l[:, lo:hi][:, ::-1], goes_on[:, lo:hi][:, ::-1],
                                                               a[:, lo:hi][:, ::-1], 0.0, ALU.mult, ALU.add)
                        step(ins)
                        nc.vector.tensor_tensor(l, z, l, ALU.subtract).then_inc(logits_ready, 1)
                    elif s < n:
                        dve.wait_ge(z_ready, u0 + s + 1)
                        dve.wait_ge(w_ready, u0 + s - 1)
                        softmax_maxima(s)
                    if 1 <= s <= n:
                        u = s - 1
                        dve.wait_ge(groups_ready, t0 + u + 1)
                        if u >= 2:
                            dve.wait_ge(o_ready, u0 + u - 1)
                        nc.vector.tensor_tensor(UT[:, u % 2, :], TB[(t0 + u) % 2][:, 0:3 * P],
                                                past_t if u < HEADS else count_t, ALU.mult).then_inc(groups_used, 1)
                    if s >= 2:
                        u = s - 2
                        dve.wait_ge(o_ready, u0 + u + 1)
                        dst = XN[:, :, u * DH:(u + 1) * DH]
                        if u < HEADS:
                            o = ACC[:, 2 + u % 2, 0:2 * (DH + 1)].rearrange("p (t e) -> p t e", t=2)
                            nc.vector.tensor_copy(dst, o[:, :, 0:DH]).then_inc(o_used, 1)
                        else:
                            softmax_output(u, dst)
                at.unit += n
                at.group += n
                activations()
                out_product(next_size)

            def convolve(i):
                dve.wait_ge(groups_ready, at.group + 1)
                if i >= 2:
                    dve.wait_ge(silus, i - 1)
                for tap in range(3, -1, -1):
                    shift = 3 - tap
                    for kk in range(2):
                        src = TB[at.group % 2][:, kk * SEQ:(kk + 1) * SEQ - shift]
                        dst = YC[:, i % 2, kk * SEQ + shift:(kk + 1) * SEQ]
                        w = CW[:, 2 * i + kk, tap:tap + 1]
                        if shift == 0:
                            ins = nc.vector.tensor_scalar(dst, src, w, None, ALU.mult)
                        else:
                            ins = nc.vector.scalar_tensor_tensor(dst, src, w, dst, ALU.mult, ALU.add)
                    if tap:
                        step(ins)
                ins.then_inc(groups_used, 1)
                at.group += 1

            def mlstm(layer, next_size):
                nc.vector.memset(VA[:, :, :, P:P + 1], 1.0)
                prenorm()
                split_next(FULL)
                dve.wait_ge(small_loaded, 16 * 8)
                for tok in range(NTOK):
                    block_ready(tok, at.chunk, at.block)
                    ins = nc.vector.tensor_tensor(GT[:, tok, :], ACC[:, (at.block % 2) * 2 + tok, 0:2 * HEADS], BG[:, :], ALU.add)
                ins.then_inc(blocks_used, 1)
                at.chunk += 1
                at.block += 1
                dve.wait_ge(gates_act, 1)
                nc.vector.scalar_tensor_tensor(LF[:, :, :], GT[:, :, HEADS:], 0.0, LS[:, :, :], ALU.min, ALU.subtract)\
                    .then_inc(gates_dve, 1)
                gain = at.row
                at.row += 1
                for j in range(8):
                    split_next(FULL)
                    if 1 <= j < 5:
                        convolve(2 * (j - 1))
                        convolve(2 * (j - 1) + 1)
                    if j >= 5:
                        bank = TB[at.group % 2]
                        dve.wait_ge(groups_ready, at.group + 1)
                    if j == 5:
                        sums = bank[:, 0:2 * HEADS].rearrange("p (t h) -> p t h", t=2)
                        nc.vector.tensor_copy(BC[:, :, :], sums)
                        nc.vector.tensor_tensor(VV[:, :, :], GT[:, :, 0:HEADS], sums, ALU.subtract).then_inc(groups_used, 1)
                    if j == 6:
                        nc.vector.tensor_copy(GL[:, 0:1], bank[0:HEADS, 3 * P - 1:3 * P])
                        nc.vector.tensor_copy(VT[:, :], bank[0:HEADS, 0:SEQ]).then_inc(groups_used, 1)
                        dve.wait_ge(groups_used, at.group + 2)
                        step(nc.vector.tensor_tensor_scan(MU[:, 0:P], VT[:, 0:P], VT[:, 0:P], 0.0, ALU.max, ALU.max))
                        step(nc.vector.tensor_tensor(GL[:, 1:2], GL[:, 0:1], MU[:, P - 1:P], ALU.add))
                        nc.vector.tensor_tensor_scan(MU[:, P:], VT[:, P:], VT[:, P:], GL[:, 1:2], ALU.max, ALU.max)
                        nc.vector.tensor_scalar(DG[:, 0:HEADS], ident[0:HEADS, 0:HEADS], MU[:, P - 1:P], None, ALU.mult)
                        nc.vector.tensor_scalar(DG[:, HEADS:], ident[0:HEADS, 0:HEADS], GL[:, 1:2], None, ALU.mult)\
                            .then_inc(gates_dve, 1)
                    if j == 7:
                        nc.vector.tensor_copy(MUB[:, :], bank[:, 0:4 * HEADS]).then_inc(groups_used, 1)
                        dve.wait_ge(groups_used, at.group + 2)
                        H = HEADS
                        nc.vector.tensor_tensor(EA[:, 0:H], VV[:, 0, :], MUB[:, 2 * H:3 * H], ALU.subtract)
                        nc.vector.tensor_tensor(EA[:, H:2 * H], MUB[:, 3 * H:4 * H], MUB[:, H:2 * H], ALU.subtract)
                        nc.vector.scalar_tensor_tensor(EA[:, 2 * H:4 * H], BC[:, :, :].rearrange("p t h -> p (t h)"), -1.0,
                                                       MUB[:, 0:2 * H], ALU.mult, ALU.subtract).then_inc(gates_dve, 1)
                    if j >= 5:
                        at.group += 1
                    at.chunk += 1
                    at.block += 1
                dve.wait_ge(row_loaded[gain % 2], 16 * (gain // 2 + 1))
                dve.wait_ge(blocks_used, at.block + 1)
                for half in range(2):
                    for tok in range(NTOK):
                        cols = slice(half * COLS, (half + 1) * COLS)
                        nc.vector.tensor_tensor(SO[:, tok, cols], SO[:, tok, cols], G[:, gain % 2, cols], ALU.mult).then_inc(normed, 1)
                at.normed += 4
                dve.wait_ge(gates_act, 2)
                step(nc.vector.tensor_scalar(WI[:, :], EX[:, HEADS:2 * HEADS], P ** -0.5, None, ALU.mult))
                at.group += 5
                u0 = at.unit
                for s in range(HEADS + 1):
                    if s < HEADS:
                        dve.wait_ge(w_ready, u0 + s + 1)
                        if s >= 2:
                            dve.wait_ge(o_ready, u0 + s - 1)
                        nc.vector.scalar_tensor_tensor(PT[:, s % 2, :], ACC[:, s % 2, 0:SEQ], P ** -0.5, DT[:, s % 2, :],
                                                       ALU.mult, ALU.mult).then_inc(logits_ready, 1)
                    if s >= 1:
                        h = s - 1
                        dve.wait_ge(ho_ready, h + 1)
                        o = ACC[:, 2 + h % 2, 0:3 * (P + 1)].rearrange("p (i e) -> p i e", i=3)
                        nc.vector.tensor_copy(N3[:, h, :].unsqueeze(2), o[:, :, P:P + 1])
                        num = XN[:, 1, h * P:(h + 1) * P]
                        nc.vector.scalar_tensor_tensor(num, o[:, 2, 0:P], WI[:, h:h + 1], num, ALU.mult, ALU.add).then_inc(o_used, 1)
                at.unit += HEADS
                dve.wait_ge(o_used, at.unit)
                step(nc.vector.tensor_tensor(NI[:, :], N3[:, :, 2], EX[:, HEADS:2 * HEADS], ALU.mult))
                step(nc.vector.scalar_tensor_tensor(N3[:, :, 1], NI[:, :], P ** -0.5, N3[:, :, 1], ALU.mult, ALU.add))
                for c in range(NTOK):
                    ins = nc.vector.scalar_tensor_tensor(AN[:, c, :], N3[:, :, c], -1.0, EX[:, (2 + c) * HEADS:(3 + c) * HEADS],
                                                         ALU.mult, ALU.max)
                step(ins)
                step(nc.vector.tensor_tensor(AN[:, :, :], AN[:, :, :], N3[:, :, 0:NTOK].rearrange("p h c -> p c h"), ALU.max))
                step(nc.vector.reciprocal(RN[:, :, :], AN[:, :, :]))
                step(nc.vector.tensor_tensor(HQ[:, :, :], RN[:, :, :], RN[:, :, :], ALU.mult))
                dve.wait_ge(heads_squared, 2 * HEADS)
                nc.vector.tensor_tensor(HQ[:, :, :], HQ[:, :, :], HS[:, :, :], ALU.mult).then_inc(heads_ready, 1)
                dve.wait_ge(heads_scaled, 1)
                step(nc.vector.tensor_tensor(HF[:, :, :], HF[:, :, :], RN[:, :, :], ALU.mult))
                for c in range(NTOK):
                    for h in range(HEADS):
                        cols = slice(h * P, (h + 1) * P)
                        ins = nc.vector.scalar_tensor_tensor(XN[:, c, cols], XN[:, c, cols], HF[:, c, h:h + 1], SO[:, c, cols],
                                                             ALU.mult, ALU.mult)
                ins.then_inc(mixed, 1)
                activations()
                out_product(next_size)

            def mix2(layer, next_size):
                nc.vector.memset(V2[:, :, :, DH:DH + 1], 1.0)
                prenorm()
                if layer == 0:
                    dve.wait_ge(tables_loaded, 32)
                mid = XN[:, :, 0:COLS], XN[:, :, COLS:D]
                scores, work = UL[:, 0, :], UL[:, 1, :]
                tiles = ((0, 0, P), (1, P, 3 * P))

                def rope(width, dsts, gain=None):
                    n = width // DH
                    dve.wait_ge(blocks_used, at.block + 2)
                    if gain is not None:
                        heads = QS[:, :, :].rearrange("p t (h e) -> p (t h) e", e=DH)
                        nc.vector.tensor_reduce(HN[:, :], SQ[:, :, :].rearrange("p t (h e) -> p (t h) e", e=DH), AX_X, ALU.add)                            .then_inc(head_sums, 1)
                        at.head_norm += 1
                        dve.wait_ge(head_rsqrts, at.head_norm)
                        step(nc.vector.tensor_tensor(heads, heads, HR[:, :].unsqueeze(2).broadcast_to([P, NTOK * n, DH]), ALU.mult))
                        step(nc.vector.tensor_tensor(heads, heads, gain.unsqueeze(1).broadcast_to([P, NTOK * n, DH]), ALU.mult))

                    def heads_of(t):
                        return t[:, :, 0:width].rearrange("p t (h e) -> p t h e", e=DH)

                    def table(i, lo, hi):
                        return CS[:, i, :, lo:hi].unsqueeze(2).broadcast_to([P, NTOK, n, hi - lo])

                    q, a, b, m = heads_of(QS), heads_of(SQ), heads_of(T3), DH // 2
                    nc.vector.tensor_tensor(b[:, :, :, 0:m], q[:, :, :, m:DH], table(1, 0, m), ALU.mult)
                    nc.vector.tensor_tensor(b[:, :, :, m:DH], q[:, :, :, 0:m], table(1, m, DH), ALU.mult)
                    step(nc.vector.tensor_tensor(a, q, table(0, 0, DH), ALU.mult))
                    for dst in dsts:
                        ins = nc.vector.tensor_tensor(heads_of(dst), a, b, ALU.add)
                    ins.then_inc(rope_done, 1)

                def plain(dst):
                    for g in range(2):
                        group_plain(dst[:, 2 * g:2 * g + 2, :].rearrange("p k n -> p (k n)"))

                def ik():
                    dve.wait_ge(groups_ready, at.group + 1)
                    nc.vector.tensor_copy(IKT[:, :], TB[at.group % 2][:, 0:SEQ]).then_inc(groups_used, 1)
                    at.group += 1

                def q():
                    for g in range(2):
                        dve.wait_ge(groups_ready, at.group + 1)
                        nc.vector.tensor_scalar(QT2[:, 0, 2 * g:2 * g + 2, :].rearrange("p k n -> p (k n)"),
                                                TB[at.group % 2][:, :], DH ** -0.5, None, ALU.mult).then_inc(groups_used, 1)
                        at.group += 1

                def index(h):
                    at.index += 1
                    dve.wait_ge(relu_ready, at.index)
                    if h:
                        dve.wait_ge(index_summed, at.index - 1)
                    for tok, lo, hi in tiles:
                        r, s, w = UA[:, h % 2, lo:hi], scores[:, lo:hi], IW[:, tok, h:h + 1]
                        if h == 0:
                            ins = nc.vector.tensor_scalar(s, r, w, None, ALU.mult)
                        else:
                            ins = nc.vector.scalar_tensor_tensor(s, r, w, s, ALU.mult, ALU.add)
                    ins.then_inc(index_summed, 1)

                def select(tok):
                    _, lo, hi = tiles[tok]
                    s, w, m = scores[:, lo:hi], work[:, lo:hi], MK[:, lo:hi]
                    diag = slice(hi - P, hi)
                    if tok == 0:
                        dve.wait_ge(index_summed, at.index)
                    step(nc.vector.tensor_scalar(s, s, HEADS ** -0.5, None, ALU.mult))
                    step(nc.vector.tensor_tensor(scores[:, diag], scores[:, diag], later, ALU.add))
                    src = s
                    for i in range(TOPK // 8):
                        step(nc.vector.max(M8[:, :], src))
                        step(nc.vector.match_replace(w, M8[:, :], src, TAKEN))
                        src = w
                    step(nc.vector.tensor_scalar(m, w, TAKEN, NEG, ALU.not_equal, ALU.mult))
                    ins = nc.vector.tensor_tensor(MK[:, diag], MK[:, diag], later, ALU.add)
                    if tok == NTOK - 1:
                        ins.then_inc(mask_ready, 1)

                def unit(s):
                    if s < HEADS:
                        dve.wait_ge(z_ready, at.unit + s + 1)
                        if s >= 2:
                            dve.wait_ge(w_ready, at.unit + s - 1)
                        softmax_maxima(s, ZB[:, 0:3 * P])
                    if 1 <= s <= HEADS:
                        u = s - 1
                        dve.wait_ge(groups_ready, at.group + 1)
                        if u >= 2:
                            dve.wait_ge(o_ready, at.unit + u - 1)
                        nc.vector.tensor_copy(UT[:, u % 2, :], TB[at.group % 2][:, 0:3 * P]).then_inc(groups_used, 1)
                        at.group += 1
                    if s >= 2:
                        u = s - 2
                        dve.wait_ge(o_ready, at.unit + u + 1)
                        o = OB[:, 0:2 * (DH + 1)].rearrange("p (t e) -> p t e", t=2)
                        gate = AG[:, :, u * DH:(u + 1) * DH]
                        step(nc.vector.reciprocal(RD[:, u % 2, :].unsqueeze(2), o[:, :, DH:DH + 1]))
                        step(nc.vector.tensor_tensor(T2[:, :, :], o[:, :, 0:DH],
                                                     RD[:, u % 2, :].unsqueeze(2).broadcast_to([P, 2, DH]), ALU.mult))
                        nc.vector.tensor_tensor(gate, gate, T2[:, :, :], ALU.mult).then_inc(o_used, 1)
                    if s == HEADS + 1:
                        at.unit += HEADS

                def conv_in():
                    for g in range(2):
                        dve.wait_ge(groups_ready, at.group + 1)
                        for tap in range(TAPS_2 - 1, -1, -1):
                            shift = TAPS_2 - 1 - tap
                            for kk in range(2):
                                tile = 2 * g + kk
                                src = TB[at.group % 2][:, kk * SEQ:(kk + 1) * SEQ - shift]
                                w = CW2[:, layer, tile, tap:tap + 1]
                                dst = YT[:, tile, shift:]
                                if shift == 0:
                                    ins = nc.vector.tensor_scalar(dst, src, w, None, ALU.mult)
                                else:
                                    ins = nc.vector.scalar_tensor_tensor(dst, src, w, dst, ALU.mult, ALU.add)
                            if tap:
                                step(ins)
                        ins.then_inc(groups_used, 1)
                        at.group += 1

                def times_yt():
                    dve.wait_ge(groups_used, at.group + 1)
                    for g in range(2):
                        dve.wait_ge(groups_ready, at.group + 1)
                        y = YT[:, 2 * g:2 * g + 2, :].rearrange("p k n -> p (k n)")
                        nc.vector.tensor_tensor(y, y, TB[at.group % 2][:, :], ALU.mult).then_inc(groups_used, 1)
                        at.group += 1

                def pool_gate():
                    for g in range(2):
                        dve.wait_ge(groups_ready, at.group + 1)
                        for kk in range(2):
                            tile = 2 * g + kk
                            ins = nc.vector.tensor_scalar(YT[:, tile, :], TB[at.group % 2][:, kk * SEQ:(kk + 1) * SEQ],
                                                          PS2[:, layer, tile:tile + 1], None, ALU.mult)
                        ins.then_inc(groups_used, 1)
                        at.group += 1

                def split(branch):
                    at.branch += 1
                    dve.wait_ge(branch_hi, at.branch)
                    nc.vector.tensor_tensor(BL[:, :, :], YT[:, :, :], BH[:, :, :].bitcast(F32), ALU.subtract)                        .then_inc(branch_ready, 1)

                tasks = dict(ik=ik, q=q, k=lambda: plain(QT2[:, 1]), iq=lambda: plain(QT2[:, 2]), conv_in=conv_in,
                             conv_gate=times_yt, pooled=lambda: plain(PL), pool_gate=pool_gate, pool_mix=times_yt,
                             attn_out=lambda: plain(YT), index=index, unit=unit, select=select, split=split)
                branch = half = 0
                for b, kind in enumerate(ORDER):
                    if b + 1 < len(ORDER):
                        split_next(SIZES[b + 1])
                    else:
                        split_next(next_size)
                    run_tasks(tasks, 2 * b)
                    acc = [ACC[:, (at.block % 2) * 2 + tok, :] for tok in range(NTOK)]
                    if kind == "ik_iw":
                        dve.wait_ge(blocks_used, at.block + 2)
                        nc.vector.tensor_copy(IW[:, :, :], QS[:, :, DH:IKW])
                        rope(DH, (ST[:, :, 0:DH], ST[:, :, DH:2 * DH]))
                    elif kind == "q":
                        rope(COLS, (mid[0],), GQK[:, layer, 0, :])
                    elif kind == "k":
                        rope(COLS, (mid[1],), GQK[:, layer, 1, :])
                    elif kind == "iq":
                        rope(COLS, (ST,))
                    elif kind in ("cc", "cb"):
                        dst = mid[0] if kind == "cc" else mid[1]
                        dve.wait_ge(blocks_used, at.block + 1)
                        for tok in range(NTOK):
                            block_ready(tok, at.chunk, at.block)
                            ins = nc.vector.tensor_tensor(dst[:, tok, :], SX[:, tok, :], acc[tok], ALU.mult)
                        ins.then_inc(blocks_used, 1)
                    elif kind == "branch":
                        cols = slice((branch % 2) * COLS, (branch % 2 + 1) * COLS)
                        dve.wait_ge(blocks_used, at.block + 1)
                        for tok in range(NTOK):
                            block_ready(tok, at.chunk, at.block)
                            dst = XN[:, tok, cols] if branch < 2 else SX[:, tok, :]
                            ins = nc.vector.tensor_tensor(dst, ST[:, tok, :], acc[tok], ALU.mult)
                        if branch >= 2:
                            step(ins)
                            ins = nc.vector.tensor_tensor(XN[:, :, cols], XN[:, :, cols], SX[:, :, :], ALU.add)
                        ins.then_inc(blocks_used, 1)
                        branch += 1
                    elif kind == "out":
                        cols = slice(half * COLS, (half + 1) * COLS)
                        for tok in range(NTOK):
                            block_ready(tok, at.chunk, at.block)
                            ins = nc.vector.tensor_tensor(X[:, tok, cols], X[:, tok, cols], acc[tok], ALU.add)
                        ins.then_inc(blocks_used, 1)
                        half += 1
                    run_tasks(tasks, 2 * b + 1)
                    at.chunk += 1
                    at.block += 1
                    if b + 1 < len(ORDER) and ORDER[b + 1] == "out" and kind != "out":
                        activations()

            def block_ready(tok, last_chunk, block):
                if tok == 0:
                    dve.wait_ge(tile0_ready, block + 1)
                else:
                    dve.wait_ge(weights_used, last_chunk + 2)

            dve.wait_ge(bias_summed, 1)
            nc.vector.tensor_copy(BROW[:, :], TB[0][0:HEADS, 0:3 * P]).then_inc(bias_rows, 1)
            dve.sem_inc(blocks_used, 1)
            dve.sem_inc(groups_used, 1)
            split_lo(0, 0, SLOT)
            for i, stage in enumerate(stages):
                {"ffn": ffn, "attn": attn, "mlstm": mlstm, "mix2": mix2}[stage[0]](*stage[1:], first_size(i + 1))


def kernel(**inputs):
    import concourse.bacc as bacc
    from concourse.bass_utils import run_bass_kernel_spmd

    nc = bacc.Bacc("TRN2", target_bir_lowering=False, num_devices=1)
    given = {name: np.ascontiguousarray(inputs[name]) for name in inputs}
    given.update(CONSTANTS)
    given["conv_taps"] = np.ascontiguousarray(given.pop("mlstm_conv_w")[0].reshape(4, 2 * HEADS, P).transpose(2, 1, 0))
    given["conv_taps_2"] = np.ascontiguousarray(given.pop("conv_w_2").reshape(DEPTH, TAPS_2, 4, P).transpose(3, 0, 2, 1))
    given["pool_scale_2"] = np.ascontiguousarray(given["pool_scale_2"].reshape(DEPTH, 4, P).transpose(2, 0, 1))
    arrays, aps = {}, {}
    for name, a in given.items():
        arrays[name + "_in"] = a
        aps[name] = nc.dram_tensor(name + "_in", a.shape, mybir.dt.from_np(a.dtype), kind="ExternalInput").ap()
    out = nc.dram_tensor("out", (1, SEQ, D), F32, kind="ExternalOutput").ap()
    program(nc, **aps, out=out)
    r = run_bass_kernel_spmd(nc, [arrays], core_ids=[0])
    return r.results[0]["out"]
```

```python
from contextlib import ExitStack

import numpy as np

import concourse.bass as bass
from concourse import mybir

F32 = mybir.dt.float32
F32R = mybir.dt.float32r
ALU = mybir.AluOpType
ACT = mybir.ActivationFunctionType
AX_X = mybir.AxisListType.X

P = 128
SEQ = 256
NTOK = SEQ // P
D = 1024
KD = D // P
DFF = 2816
KF = DFF // P
DEPTH = 2
EPS = 1e-6
COLS = 512
SLOT = KD * COLS
GU = COLS // 2
NGU = DFF // GU
DOWN = (4, 4, 6, 8)
HEADS = 8
DH = 64
NEG = -1.0e30
TAKEN = -3.0e38
TOPK = SEQ // 4
WINDOWS = (2, 4, 8, 16)
TAPS_2 = 3
assert sum(DOWN) == KF and NGU * GU == DFF


class At:

    def __init__(self):
        self.chunk = self.block = self.group = self.row = 0
        self.square = self.rsqrt = self.stage = self.gains_used = 0
        self.unit = self.ln = self.silu = self.rounded = 0
        self.staged = self.index = self.head_norm = self.side = self.branch = 0



def relative_bucket(dist, num_buckets=32, max_distance=2048):
    exact = num_buckets // 2
    d = np.maximum(dist, 1).astype(np.float32)
    log_b = exact + (np.log(d / np.float32(exact)) / np.float32(np.log(max_distance / exact))
                     * np.float32(num_buckets - exact)).astype(np.int32)
    return np.where(dist < exact, dist, np.minimum(log_b, num_buckets - 1))


def branch_count(dist):
    near = (dist >= 0) & (dist <= 128)
    return (near.astype(np.float32) + ((dist >= 0) & (dist % 4 == 0)) + ((dist >= 0) & (dist % 16 == 0))).astype(np.float32)


def rope_constants():
    exponent = np.arange(0, DH, 2) / DH
    inv = np.float32(1) / np.power(10000.0, exponent).astype(np.float32)
    angle = np.arange(SEQ, dtype=np.float32)[:, None] * inv[None, :]
    cos, sin = np.cos(angle), np.sin(angle)
    both = np.stack([np.concatenate([cos, cos], 1), np.concatenate([-sin, sin], 1)])
    return np.ascontiguousarray(both.reshape(2, NTOK, P, DH).transpose(2, 0, 1, 3)).astype(np.float32)


def pool_constants():
    s = np.arange(P)[:, None]
    t = np.arange(P)[None, :]
    tiles = []
    for w in WINDOWS:
        inside = (s <= t) & (s > t - w)
        near = (s > t + P - w)[:, 0:WINDOWS[-1]]
        tiles.append(np.concatenate([inside / np.minimum(t + 1, w) - (s == t), inside / w - (s == t), near / w], axis=1))
    return np.ascontiguousarray(np.stack(tiles, axis=1)).astype(np.float32)


def shape_constants():
    part = np.arange(P)[:, None]
    free = np.arange(P)[None, :]
    far = np.concatenate([free, free, free + P], axis=1)
    dist = (np.arange(3 * P) - P)[::-1]
    onehot = np.zeros((33, 3 * P), np.float32)
    seen = branch_count(dist) > 0
    onehot[relative_bucket(np.maximum(dist, 0)), np.arange(3 * P)] = seen
    onehot[32] = ~seen
    q_of = np.concatenate([part + 0 * free, part + P + 0 * free, part + P + 0 * free], axis=1)
    k_of = np.concatenate([free + 0 * part, free + 0 * part, free + P + 0 * part], axis=1)
    goes_on = (k_of + 1 < q_of).astype(np.float32)
    qt = np.concatenate([free + 0 * part, free + P + 0 * part, free + P + 0 * part], axis=1)
    kt = np.concatenate([part + 0 * free, part + 0 * free, part + P + 0 * free], axis=1)
    past = (kt < qt).astype(np.float32)
    count = branch_count(qt - kt)
    ident = np.eye(P, dtype=np.float32)
    return {"c_onehot": onehot, "c_tiles": np.concatenate([
        ident, goes_on, past, count, ident[:, ::-1],
        (part <= free).astype(np.float32),
        np.float32(-NEG) * (part > free), np.ones((P, 1)),
        np.float32(NEG) * (free > part)], axis=1).astype(np.float32),
        "c_rope": rope_constants(), "c_pool": pool_constants()}


CONSTANTS = shape_constants()
C_IDENT, C_GOES_ON, C_PAST, C_COUNT, C_FLIP = 0, P, 4 * P, 7 * P, 10 * P
C_UPTO, C_AFTER, C_ONE, C_LATER = 11 * P, 12 * P, 13 * P, 13 * P + 1


def program(nc, x, norm_g, ffn_w_gate, ffn_w_up, ffn_w_down, attn_w_in, attn_w_out, rel_bias,
            mlstm_w_in, mlstm_w_out, conv_taps, mlstm_b_gates, mlstm_head_g,
            w_in_2, w_out_conv_2, q_norm_g_2, k_norm_g_2, w_out_attn_2, pool_w_2,
            w_out_pool_2, w_o_2, conv_taps_2, pool_scale_2,
            gains_by_feature, c_onehot, c_tiles, c_rope, c_pool, out):
    ctx = ExitStack()
    top = [(nc.sbuf_base + 31) // 32 * 32]

    sbuf_at = {}

    def sb(name, shape, dt=F32, offset=None):
        size = int(np.prod(shape[1:])) * 4
        sbuf_at[name] = top[0] if offset is None else offset
        t = nc.alloc_sbuf_tensor_at(name, list(shape), dt, offset=top[0] if offset is None else offset)
        if offset is None:
            top[0] += (size + 31) // 32 * 32
        return t

    def sem(name):
        return ctx.enter_context(nc.semaphore(name))

    with ctx:
        X = sb("X", [P, NTOK, D])
        RAW = sb("RAW", [P, 2, SLOT])
        WH = sb("WH", [P, 2, SLOT], F32R)
        WL = sb("WL", [P, 2, SLOT], F32R)
        XH = sb("XH", [P, KD, SEQ], F32R)
        XL = sb("XL", [P, KD, SEQ], F32R)
        XN = sb("XN", [P, NTOK, D])
        G = sb("G", [P, 2, D])
        ST = sb("ST", [P, NTOK, COLS])
        SIDE = sb("SIDE", [P, NTOK, GU])
        CT = sb("CT", list(c_tiles.shape))
        SS = sb("SS", [P, 4])
        MS = sb("MS", [P, 2])
        RX = sb("RX", [P, 2])
        RS = sb("RS", [P, 2])
        GX = sb("GX", [P, 4 * DEPTH, KD])
        HALF = sb("HALF", [P, 2])
        TMP2 = sb("TMP2", [P, 2])
        arena = top[0]
        HH = sb("HH", [P, KF, SEQ], F32R)
        HL = sb("HL", [P, KF, SEQ], F32R)
        o = arena
        QT = sb("QT", [P, 4, 4, SEQ], offset=o)
        o += 4 * 4 * SEQ * 4
        VS = sb("VS", [P, 2, NTOK, HEADS, DH + 1], offset=o)
        o += 2 * NTOK * HEADS * (DH + 1) * 4
        BT = sb("BT", [P, HEADS, SEQ], offset=o)
        o += HEADS * SEQ * 4
        assert o <= top[0]
        o = arena
        QK = sb("QK", [P, 2 * HEADS, SEQ], offset=o)
        o += 2 * HEADS * SEQ * 4
        VA = sb("VA", [P, NTOK, HEADS, P + 1], offset=o)
        o += NTOK * HEADS * (P + 1) * 4
        SO = sb("SO", [P, NTOK, D], offset=o)
        o += NTOK * D * 4
        KN = sb("KN", [P, HEADS, P], offset=o)
        o += HEADS * P * 4
        CA = sb("CA", [P, HEADS, P + 1], offset=o)
        o += HEADS * (P + 1) * 4
        assert o <= top[0]
        o = arena
        QT2 = sb("QT2", [P, 3, 4, SEQ], offset=o)
        o += 3 * 4 * SEQ * 4
        IKT = sb("IKT", [P, SEQ], offset=o)
        o += SEQ * 4
        V2 = sb("V2", [P, NTOK, HEADS, DH + 1], offset=o)
        o += NTOK * HEADS * (DH + 1) * 4
        AG = sb("AG", [P, NTOK, COLS], offset=o)
        o += NTOK * COLS * 4
        BH = sb("BH", [P, 4, SEQ], F32R, offset=o)
        o += 4 * SEQ * 4
        BL = sb("BL", [P, 4, SEQ], F32R, offset=o)
        o += 4 * SEQ * 4
        MK = sb("MK", [P, 3 * P], F32R, offset=o)
        o += 3 * P * 4
        SX = sb("SX", [P, NTOK, COLS], offset=o)
        o += NTOK * COLS * 4
        YT = sb("YT", [P, 4, SEQ], offset=o)
        o += 4 * SEQ * 4
        PM = sb("PM", list(c_pool.shape), offset=o)
        o += int(np.prod(c_pool.shape[1:])) * 4
        CS = sb("CS", list(c_rope.shape), offset=o)
        o += int(np.prod(c_rope.shape[1:])) * 4
        assert o <= top[0]
        PW = sb("PW", [P, 4, P], offset=sbuf_at["SIDE"])
        GQK = sb("GQK", [P, DEPTH, 2, DH])
        CW2 = sb("CW2", [P, DEPTH, 4, TAPS_2])
        PS2 = sb("PS2", [P, DEPTH, 4])
        IW = sb("IW", [P, NTOK, HEADS])
        HN = sb("HN", [P, NTOK * HEADS])
        HM = sb("HM", [P, NTOK * HEADS])
        HR = sb("HR", [P, NTOK * HEADS])
        M8 = sb("M8", [P, 8])
        IDR = sb("IDR", [P, P], F32R, offset=sbuf_at["CT"] + C_GOES_ON * 4)
        T2 = sb("T2", [P, NTOK, DH])
        CW = sb("CW", [P, 2 * HEADS, 4])
        BG = sb("BG", [P, 2 * HEADS])
        HALF16 = sb("HALF16", [P, NTOK * HEADS])
        NM = sb("NM", [P, 2, 2])
        RD = sb("RD", [P, 2, 2])
        RB = sb("RB", [33, HEADS])
        units_at = top[0]
        UA = sb("UA", [P, 2, 3 * P])
        UL = sb("UL", [P, 2, 3 * P])
        UW = sb("UW", [P, 2, 3 * P])
        UT = sb("UT", [P, 2, 3 * P])
        ONEHOT = sb("ONEHOT", [33, 3 * P], offset=units_at)
        BROW = sb("BROW", [HEADS, 3 * P], offset=units_at + 3 * P * 4)
        YC = sb("YC", [P, 2, 2 * SEQ], offset=units_at)
        DT = sb("DT", [P, 2, SEQ], offset=units_at + 2 * 2 * SEQ * 4)
        PT = sb("PT", [P, 2, SEQ], offset=units_at + 3 * 2 * SEQ * 4)
        small_at = [units_at + 4 * 2 * SEQ * 4]
        QS = sb("QS", [P, NTOK, COLS], offset=units_at)
        SQ = sb("SQ", [P, NTOK, COLS], offset=units_at + NTOK * COLS * 4)
        T3 = sb("T3", [P, NTOK, COLS], offset=units_at + 2 * NTOK * COLS * 4)
        RELU = sb("RELU", [P, 2, 3 * P], offset=sbuf_at["BH"])
        IS = sb("IS", [P, 2, 3 * P], offset=sbuf_at["BL"])
        PL = sb("PL", [P, 4, SEQ], offset=units_at)

        def small(name, shape):
            t = sb(name, shape, offset=small_at[0])
            small_at[0] += (int(np.prod(shape[1:])) * 4 + 31) // 32 * 32
            return t

        GT = small("GT", [P, NTOK, 2 * HEADS])
        LS = small("LS", [P, NTOK, HEADS])
        LF = small("LF", [P, NTOK, HEADS])
        BC = small("BC", [P, NTOK, HEADS])
        VV = small("VV", [P, NTOK, HEADS])
        VT = small("VT", [HEADS, SEQ])
        MU = small("MU", [HEADS, SEQ])
        GL = small("GL", [HEADS, 2])
        DG = small("DG", [HEADS, 2 * HEADS])
        MUB = small("MUB", [P, 4 * HEADS])
        EA = small("EA", [P, 4 * HEADS])
        EX = small("EX", [P, 4 * HEADS])
        WI = small("WI", [P, HEADS])
        N3 = small("N3", [P, HEADS, 3])
        NI = small("NI", [P, HEADS])
        AN = small("AN", [P, NTOK, HEADS])
        RN = small("RN", [P, NTOK, HEADS])
        HS = small("HS", [P, NTOK, HEADS])
        HQ = small("HQ", [P, NTOK, HEADS])
        HF = small("HF", [P, NTOK, HEADS])
        assert small_at[0] <= top[0]
        assert top[0] <= nc.sbuf_usable_end, (top[0], nc.sbuf_usable_end)
        bias_dram = nc.dram_tensor("bias_by_distance", (HEADS, 3 * P), F32, kind="Internal").ap()

        ACC = ctx.enter_context(nc.psum_tensor("ACC", [P, 4, COLS], F32))
        ZB = ctx.enter_context(nc.psum_tensor("ZB", [P, COLS], F32))
        OB = ctx.enter_context(nc.psum_tensor("OB", [P, COLS], F32))
        TB = [ctx.enter_context(nc.psum_tensor(f"TB{i}", [P, COLS], F32)) for i in range(2)]

        raw_ready = [sem(f"raw_ready{i}") for i in range(2)]
        hi_ready = sem("hi_ready")
        lo_ready = sem("lo_ready")
        weights_used = sem("weights_used")
        tile0_ready = sem("tile0_ready")
        blocks_used = sem("blocks_used")
        groups_ready = sem("groups_ready")
        groups_hi = sem("groups_hi")
        groups_used = sem("groups_used")
        silu_ready = sem("silu_ready")
        squares = sem("squares")
        rsqrts = sem("rsqrts")
        pool_step = sem("pool_step")
        x_loaded = [sem(f"x_loaded{i}") for i in range(NTOK)]
        x_ready = sem("x_ready")
        gain_used = sem("gain_used")
        ident_loaded = sem("ident_loaded")
        gains_loaded = sem("gains_loaded")
        consts_loaded = sem("consts_loaded")
        row_loaded = [sem(f"row_loaded{i}") for i in range(2)]
        out_stored = sem("out_stored")
        z_ready = sem("z_ready")
        abs_ready = sem("abs_ready")
        exp_ready = sem("exp_ready")
        ln_ready = sem("ln_ready")
        dve_step = sem("dve_step")
        logits_ready = sem("logits_ready")
        w_ready = sem("w_ready")
        o_ready = sem("o_ready")
        o_used = sem("o_used")
        mask_set = sem("mask_set")
        small_loaded = sem("small_loaded")
        silus = sem("silus")
        gates_dve = sem("gates_dve")
        gates_act = sem("gates_act")
        ho_ready = sem("ho_ready")
        heads_squared = sem("heads_squared")
        heads_ready = sem("heads_ready")
        heads_scaled = sem("heads_scaled")
        mixed = sem("mixed")
        bias_rows = sem("bias_rows")
        bias_stored = sem("bias_stored")
        bias_ready = sem("bias_ready")

        rope_done = sem("rope_done")
        head_sums = sem("head_sums")
        head_rsqrts = sem("head_rsqrts")
        tables_loaded = sem("tables_loaded")
        pool_w_loaded = sem("pool_w_loaded")
        index_z_ready = sem("index_z_ready")
        relu_ready = sem("relu_ready")
        index_summed = sem("index_summed")
        mask_ready = sem("mask_ready")
        branch_hi = sem("branch_hi")
        branch_ready = sem("branch_ready")

        ident = CT[:, C_IDENT:C_IDENT + P]
        goes_on = CT[:, C_GOES_ON:C_GOES_ON + 3 * P]
        past_t = CT[:, C_PAST:C_PAST + 3 * P]
        count_t = CT[:, C_COUNT:C_COUNT + 3 * P]
        flip = CT[:, C_FLIP:C_FLIP + P]
        upto = CT[:, C_UPTO:C_UPTO + P]
        after = CT[:, C_AFTER:C_AFTER + P]
        later = CT[:, C_LATER:C_LATER + P]
        one = CT[:, C_ONE:C_ONE + 1]

        rows = []
        for layer in range(DEPTH):
            rows += [norm_g[layer, 2 * i + 1, :] for i in range(3)]
        rows.insert(3 + 1, mlstm_head_g[0])

        def raw_value(chunk):
            return 32 * (chunk // 2 + 1)

        bias_by_query = bass.AP(tensor=bias_dram.tensor, offset=0, ap=[[1, P], [3 * P, HEADS], [1, SEQ]])

        FULL = (KD, COLS)
        DOWN_SIZES = [(k, COLS) for k in DOWN] * 2

        stages = [("ffn", 0, 0), ("attn", 0), ("ffn", 0, 1), ("ffn", 1, 0), ("mlstm", 1), ("ffn", 1, 1),
                  ("mix2", 0), ("mix2", 1)]

        BLOCKS = {"ffn": NGU + 2, "attn": 8, "mlstm": 11, "mix2": 26}

        W2 = dict(cb=0, cc=512, cx=1024, cgate=1536, q=2048, k=2560, v=3072, agate=3584, iq=4096,
                  ik_iw=4608, pu=4680, pgate=5192, mgate=5704)
        IKW = DH + HEADS
        ORDER = ["iq", "ik_iw", "v", "q", "agate", "k", "cx", "cc", "cgate", "cb", "pu", "pgate"]
        BRANCHES = [(w_out_conv_2, 0), (w_out_pool_2, 2), (w_out_attn_2, 1)]
        for branch in range(3):
            ORDER += ["mgate", "branch", "mgate", "branch"]
        ORDER += ["out", "out"]
        SIZES = [(KD, IKW) if kind == "ik_iw" else (4, COLS) if kind == "branch" else FULL for kind in ORDER]
        TASKS = {}

        def task(slot, *names):
            TASKS.setdefault(slot, []).extend(names)

        task(4, ("rotate", "iq"), ("rotate", "ik_iw"))
        task(6, "iq", "ik")
        task(8, ("rotate", "q"))
        task(10, "q")
        task(12, ("rotate", "k"))
        task(14, "k")
        for h in range(HEADS):
            task(8 + h // 2, ("index", h))
        task(14, ("select", 0))
        task(16, ("select", 1))
        task(18, "conv_in")
        task(20, "conv_gate", ("split", 0))
        task(22, "pooled")
        task(24, "pool_gate")
        task(26, "pool_mix")
        for s, slot in enumerate((21, 22, 23, 24, 25, 27, 28, 29, 30, 32)):
            task(slot, ("unit", s))
        task(32, ("split", 1))
        task(34, "attn_out")
        task(40, ("split", 2))
        task(45, "merged")

        def x_value(stage, tok, half):
            by_half = stages[stage - 1][0] == "mix2"
            return 4 * (stage - 1) + (2 * half + tok if by_half else 2 * tok + half) + 1

        def pair(block):
            return (block % 2) * 2

        def run_tasks(tasks, slot):
            for task in TASKS.get(slot, []):
                name, args = (task, ()) if isinstance(task, str) else (task[0], task[1:])
                tasks[name](*args)

        def first_size(i):
            if i >= len(stages):
                return None
            return {"mlstm": (KD, 2 * HEADS)}.get(stages[i][0], FULL)

        block = ctx.enter_context(nc.Block())

        @block.sync
        def _(sp):
            at = At()

            def load(chunk, slot, wait, dst_src):
                if wait is not None:
                    sp.wait_ge(lo_ready, 2 * wait)
                for dst, src in dst_src:
                    sp.dma_start(dst, src).then_inc(raw_ready[slot], 16)

            def tiles(slot, k, n):
                return RAW[:, slot, 0:k * n].rearrange("p (k n) -> p k n", k=k)

            def load_cols(w, k0, k, col, n):
                c = at.chunk
                dst = tiles(c % 2, k, n)
                src = w.rearrange("(k p) n -> p k n", p=P)[:, k0:k0 + k, col:col + n]
                cut = k // 2
                load(c, c % 2, c - 1 if c >= 2 else None,
                     [(dst[:, :cut, :], src[:, :cut, :]), (dst[:, cut:, :], src[:, cut:, :])])
                at.chunk += 1

            def ffn(layer, which):
                wg = ffn_w_gate[layer, which].rearrange("(k p) n -> p k n", p=P)
                wu = ffn_w_up[layer, which].rearrange("(k p) n -> p k n", p=P)
                c0 = at.chunk

                def gate_up(j, slot, wait):
                    dst = tiles(slot, KD, COLS)
                    load(None, slot, wait,
                         [(dst[:, :, 0:GU], wg[:, :, bass.ds(j * GU, GU)]),
                          (dst[:, :, GU:COLS], wu[:, :, bass.ds(j * GU, GU)])])

                first = 3 if c0 == 0 else 1
                for j in range(first):
                    c = c0 + j
                    gate_up(j, c % 2, c - 1 if c >= 2 else None)
                with sp.Fori(0, (NGU - first) // 2) as i:
                    for odd in range(2):
                        j = 2 * i + (first + odd)
                        gate_up(j, (c0 + first + odd) % 2, 2 * i + (c0 + first + odd - 1))
                at.chunk += NGU
                for half in range(2):
                    k0 = 0
                    for k in DOWN:
                        load_cols(ffn_w_down[layer, which], k0, k, half * COLS, COLS)
                        k0 += k

            def attn(layer):
                for col in (0, 1, 3, 4, 2, 5):
                    load_cols(attn_w_in[layer], 0, KD, col * COLS, COLS)
                for half in range(2):
                    load_cols(attn_w_out[layer], 0, KD, half * COLS, COLS)

            def mlstm(layer):
                load_cols(mlstm_w_in[0], 0, KD, 4 * D, 2 * HEADS)
                for j in range(8):
                    load_cols(mlstm_w_in[0], 0, KD, j * COLS, COLS)
                for half in range(2):
                    load_cols(mlstm_w_out[0], 0, KD, half * COLS, COLS)

            def mix2(layer):
                mgate = branch = out_half = 0
                for kind in ORDER:
                    if kind == "mgate":
                        gate = BRANCHES[mgate // 2][1]
                        load_cols(w_in_2[layer], 0, KD, W2["mgate"] + gate * D + (mgate % 2) * COLS, COLS)
                        mgate += 1
                    elif kind == "branch":
                        load_cols(BRANCHES[branch // 2][0][layer], 0, 4, (branch % 2) * COLS, COLS)
                        branch += 1
                    elif kind == "out":
                        load_cols(w_o_2[layer], 0, KD, out_half * COLS, COLS)
                        out_half += 1
                    else:
                        load_cols(w_in_2[layer], 0, KD, W2[kind], IKW if kind == "ik_iw" else COLS)

            sp.dma_start(CT[:, 0:P], c_tiles[:, 0:P]).then_inc(ident_loaded, 16)
            for tok in range(NTOK):
                sp.dma_start(X[:, tok, :], x[0].rearrange("(t p) d -> p t d", p=P)[:, tok, :]).then_inc(x_loaded[tok], 16)
            for stage in stages:
                {"ffn": ffn, "attn": attn, "mlstm": mlstm, "mix2": mix2}[stage[0]](*stage[1:])
            for tok in range(NTOK):
                sp.wait_ge(x_ready, x_value(len(stages), tok, 1))
                sp.dma_start(out[0].rearrange("(t p) d -> p t d", p=P)[:, tok, :], X[:, tok, :]).then_inc(out_stored, 16)
            sp.wait_ge(out_stored, 16 * NTOK)

        @block.tensor
        def _(pe):
            at = At()

            def product(xh, xl, chunk, slot, b_wait, block_odd, k0, k, n, first, last, between=None,
                        acc_of=None, fresh=None, tail=None):
                if first:
                    pe.wait_ge(blocks_used, b_wait)
                wh = WH[:, slot, 0:k * n].rearrange("p (k n) -> p k n", k=k)
                wl = WL[:, slot, 0:k * n].rearrange("p (k n) -> p k n", k=k)
                for tok in range(NTOK):
                    bank = acc_of(tok) if acc_of else ACC[:, block_odd * 2 + tok, 0:n]
                    for i in range(k):
                        if fresh is not None and i in (0, k // 2):
                            if tok == 0 and i:
                                of_x(1, fresh + 2)
                            pe.wait_ge(groups_used, fresh + 2 * tok + (2 if i == 0 else 3))
                        if tok == 0 and i in (0, k // 2):
                            pe.wait_ge(lo_ready, 2 * chunk + (1 if i == 0 else 2))
                        if tail and tok == NTOK - 1 and i == k - 1:
                            tail()
                        lh = xh[:, k0 + i, tok * P:(tok + 1) * P]
                        ll = xl[:, k0 + i, tok * P:(tok + 1) * P]
                        nc.tensor.matmul(bank, lh, wl[:, i, :], start=first and i == 0, stop=False)
                        nc.tensor.matmul(bank, lh, wh[:, i, :], start=False, stop=False)
                        mm = nc.tensor.matmul(bank, ll, wh[:, i, :], start=False, stop=last and i == k - 1)
                    if tok == 0:
                        if last:
                            mm.then_inc(tile0_ready, 1)
                        if between:
                            between()
                mm.then_inc(weights_used, 1)

            def of_x(tok, t):
                for half in range(2):
                    if at.stage == 0:
                        pe.wait_ge(x_loaded[tok], 16)
                    else:
                        pe.wait_ge(x_ready, x_value(at.stage, tok, half))
                    pe.wait_ge(groups_used, t + half)
                    for i in range(4):
                        mm = nc.tensor.transpose(TB[(t + half) % 2][:, i * P:(i + 1) * P],
                                                 X[:, tok, (4 * half + i) * P:(4 * half + i + 1) * P], ident)
                    mm.then_inc(groups_ready, 1)

            def group(bank_odd, used, source, wait=None):
                if wait:
                    pe.wait_ge(*wait)
                pe.wait_ge(groups_used, used)
                for kk in range(2):
                    for tok in range(NTOK):
                        o = (kk * NTOK + tok) * P
                        mm = nc.tensor.transpose(TB[bank_odd][:, o:o + P], source(tok, kk), ident)
                mm.then_inc(groups_ready, 1)

            def activations(wait):
                for g in range(KD // 2):
                    group(at.group % 2, at.group,
                          lambda tok, kk: XN[:, tok, (2 * g + kk) * P:(2 * g + kk + 1) * P],
                          wait if g == 0 else None)
                    at.group += 1
                pe.wait_ge(groups_used, at.group + 1)

            def first_product(n=COLS, between=None):
                t = at.group
                if at.stage == 0:
                    of_x(0, t)
                product(XH, XL, at.chunk, at.chunk % 2, at.block, at.block % 2, 0, KD, n, True, True,
                        between=between, fresh=t)
                at.group += 4
                at.stage += 1

            def next_x():
                if at.stage < len(stages):
                    of_x(0, at.group)

            def out_product(second_half=None):
                if second_half is None:
                    for half in range(2):
                        product(XH, XL, at.chunk, at.chunk % 2, at.block, at.block % 2, 0, KD, COLS, True, True,
                                tail=next_x if half else None)
                        at.chunk += 1
                        at.block += 1
                    return
                pe.wait_ge(groups_used, at.group + 1)
                for part in range(2):
                    for half in range(2):
                        c, b = at.chunk + half, at.block + half
                        if part == 0:
                            pe.wait_ge(blocks_used, b)
                        elif half == 0:
                            pe.wait_ge(groups_used, at.group + 1)
                        pe.wait_ge(lo_ready, 2 * c + part + 1)
                        wh = WH[:, c % 2, :].rearrange("p (k n) -> p k n", k=KD)
                        wl = WL[:, c % 2, :].rearrange("p (k n) -> p k n", k=KD)
                        for tok in range(NTOK):
                            bank = ACC[:, pair(b) + tok, :]
                            for k in range(part * KD // 2, (part + 1) * KD // 2):
                                t = slice(tok * P, (tok + 1) * P)
                                if half and tok and k == KD - 1:
                                    next_x()
                                nc.tensor.matmul(bank, XH[:, k, t], wl[:, k, :], start=k == 0, stop=False)
                                nc.tensor.matmul(bank, XH[:, k, t], wh[:, k, :], start=False, stop=False)
                                mm = nc.tensor.matmul(bank, XL[:, k, t], wh[:, k, :], start=False, stop=k == KD - 1)
                            if part and tok == 0:
                                mm.then_inc(tile0_ready, 1)
                        if part:
                            mm.then_inc(weights_used, 1)
                        elif half == 0:
                            second_half()
                at.chunk += 2
                at.block += 2

            def ffn(layer, which):
                c0, b0 = at.chunk, at.block
                first_product()
                t0 = at.group

                def hidden(bank_odd, g, b):
                    group(bank_odd, g, lambda tok, kk: ST[:, tok, kk * P:(kk + 1) * P],
                          (blocks_used, b + 2))

                with pe.Fori(0, (NGU - 1) // 2) as i:
                    for odd in range(2):
                        j = 2 * i + (1 + odd)
                        product(XH, XL, j + c0, (c0 + 1 + odd) % 2, j + b0, (b0 + 1 + odd) % 2, 0, KD, COLS,
                                True, True,
                                between=lambda: hidden((t0 + odd) % 2, j + (t0 - 1), j + (b0 - 1)))
                at.chunk += NGU
                at.block += NGU
                at.group += NGU
                last_hidden = lambda: hidden((t0 + NGU - 1) % 2, t0 + NGU - 1, b0 + NGU - 1)
                for half in range(2):
                    k0 = 0
                    for q, k in enumerate(DOWN):
                        if half == 0 and q in (0, len(DOWN) - 1):
                            pe.wait_ge(groups_used, at.group + (q > 0))
                        product(HH, HL, at.chunk, at.chunk % 2, at.block, at.block % 2, k0, k, COLS,
                                q == 0, q == len(DOWN) - 1, between=last_hidden if half == q == 0 else None,
                                tail=next_x if half and q == len(DOWN) - 1 else None)
                        k0 += k
                        at.chunk += 1
                    at.block += 1

            def staged(j_groups, used, b, of=ST):
                for g in range(2):
                    group(j_groups[g], used + g, lambda tok, kk: ST[:, tok, (2 * g + kk) * P:(2 * g + kk + 1) * P],
                          (blocks_used, b + 2) if g == 0 else None)

            def projections(n_staged, n_more, hooks=(), first=True, between0=None):
                c0, b0 = at.chunk, at.block
                if first:
                    first_product(between=between0)
                    t0 = at.group
                else:
                    t0 = at.group

                def multiply(j, odd, between=None):
                    product(XH, XL, j + c0, (c0 + odd) % 2, j + b0, (b0 + odd) % 2, 0, KD, COLS, True, True,
                            between=between)

                if not first:
                    multiply(0, 0)
                with pe.Fori(0, n_staged // 2) as i:
                    for k in range(2):
                        j = 2 * i + (1 + k)
                        multiply(j, 1 + k, lambda: staged([t0 % 2, (t0 + 1) % 2], 4 * i + (t0 + 2 * k), 2 * i + (b0 + k)))
                for j in range(n_staged + 1, n_staged + n_more):
                    hook = hooks[j - n_staged - 1] if hooks else None
                    multiply(j, j, (lambda: hook(t0 + 2 * n_staged + j - n_staged - 1)) if hook else None)
                at.chunk += n_staged + n_more
                at.block += n_staged + n_more
                at.group += 2 * n_staged

            def units(n, scores, weigh, z_taken):
                pe.wait_ge(blocks_used, at.block + 1)
                u0, t0 = at.unit, at.group
                for s in range(n + 3):
                    if s < n:
                        if s >= 2:
                            pe.wait_ge(*z_taken(s - 2, u0))
                        scores(s, ACC[:, s % 2, 0:3 * P]).then_inc(z_ready, 1)
                    if 2 <= s <= n + 1:
                        u = s - 2
                        t = t0 + u
                        pe.wait_ge(w_ready, u0 + u + 1)
                        pe.wait_ge(groups_used, t)
                        for i in range(3):
                            mm = nc.tensor.transpose(TB[t % 2][:, i * P:(i + 1) * P], UW[:, u % 2, i * P:(i + 1) * P], ident)
                        mm.then_inc(groups_ready, 1)
                    if s >= 3:
                        u = s - 3
                        pe.wait_ge(groups_used, t0 + u + 2)
                        if u >= 2:
                            pe.wait_ge(o_used, u0 + u - 1)
                        weigh(u, ACC[:, 2 + u % 2, 0:2 * (DH + 1)].rearrange("p (t e) -> p t e", t=2),
                              UT[:, u % 2, :]).then_inc(o_ready, 1)
                at.unit += n
                at.group += n

            def head_scores(q, k, z, add=None):
                for lo, hi, queries in ((0, P, slice(0, P)), (P, 3 * P, slice(P, 2 * P))):
                    mm = nc.tensor.matmul(z[:, lo:hi], q[:, queries], k[:, 0:hi - lo], start=True, stop=add is None)
                    if add:
                        table = add[1][:, lo:hi] if add[1] is MK else add[1][:, SEQ - (hi - lo):]
                        mm = nc.tensor.matmul(z[:, lo:hi], add[0], table, start=False, stop=True)
                return mm

            def head_output(v, o, w, n):
                nc.tensor.matmul(o[:, 0, 0:n], w[:, 0:P], v(0), start=True, stop=True)
                nc.tensor.matmul(o[:, 1, 0:n], w[:, P:2 * P], v(0), start=True, stop=False)
                return nc.tensor.matmul(o[:, 1, 0:n], w[:, 2 * P:3 * P], v(1), start=False, stop=True)

            def attn(layer):
                def bias_table():
                    t = at.group + 4
                    pe.wait_ge(consts_loaded, 48)
                    pe.wait_ge(mask_set, 1)
                    pe.wait_ge(groups_used, t)
                    nc.tensor.matmul(TB[t % 2][0:HEADS, 0:3 * P], RB[:, :], ONEHOT[:, :], start=True, stop=True)\
                        .then_inc(groups_ready, 1)
                    at.group += 1

                projections(4, 2, between0=bias_table)
                pe.wait_ge(groups_used, at.group + 1)

                def scores(s, z):
                    side, h = divmod(s, HEADS)
                    part = slice(DH * (h % 2), DH * (h % 2) + DH)
                    if s == HEADS:
                        pe.wait_ge(bias_ready, 16)
                    return head_scores(QT[part, 2 * side, h // 2, :], QT[part, 2 * side + 1, h // 2, :], z,
                                       (flip, BT[:, h, :]) if side else None)

                def weigh(u, o, w):
                    side, h = divmod(u, HEADS)
                    n = DH + side
                    return head_output(lambda t: VS[:, side, t, h, 0:n], o, w, n)

                units(2 * HEADS, scores, weigh,
                      lambda u, u0: (logits_ready if u < HEADS else w_ready, u0 + u + 1))
                activations((o_used, at.unit))
                out_product()

            def small_group(t, wait, products):
                pe.wait_ge(*wait)
                pe.wait_ge(groups_used, t)
                for mm in products(TB[t % 2]):
                    pass
                mm.then_inc(groups_ready, 1)

            def mlstm(layer):
                first_product(2 * HEADS)
                at.chunk += 1
                at.block += 1

                def running_sums(t):
                    small_group(t, (gates_dve, 1), lambda bank: [
                        nc.tensor.matmul(bank[:, tok * HEADS:(tok + 1) * HEADS], upto, LF[:, tok, :], start=True, stop=True)
                        for tok in range(NTOK)])

                def by_head(t):
                    small_group(t, (groups_used, t + 1), lambda bank: [
                        nc.tensor.transpose(bank[0:HEADS, i * P:(i + 1) * P], src, ident)
                        for i, src in enumerate((VV[:, 0, :], VV[:, 1, :], BC[:, 0, :]))])

                def by_token(t):
                    small_group(t, (gates_dve, 2), lambda bank: [
                        nc.tensor.transpose(bank[:, c * HEADS:(c + 1) * HEADS], MU[:, c * P:(c + 1) * P],
                                            ident[0:HEADS, 0:HEADS]) for c in range(NTOK)] + [
                        nc.tensor.matmul(bank[:, 2 * HEADS:4 * HEADS], one[0:HEADS, :].broadcast_to([HEADS, P]), DG[:, :],
                                         start=True, stop=True)])

                projections(4, 4, (running_sums, by_head, by_token), first=False)
                at.group += 3
                for g in range(2):
                    small_group(at.group, (silus, 8), lambda bank: [
                        nc.tensor.transpose(bank[:, i * P:(i + 1) * P], QK[:, HEADS + 4 * g + i, 0:P], ident) for i in range(4)])
                    at.group += 1
                for h0 in range(0, HEADS, 3):
                    small_group(at.group, (groups_used, at.group if h0 else at.group + 1), lambda bank: [
                        nc.tensor.matmul(bank[:, i * (P + 1):(i + 1) * (P + 1)], KN[:, h0 + i, :], VA[:, 0, h0 + i, :],
                                         start=True, stop=True) for i in range(min(3, HEADS - h0))])
                    at.group += 1
                pe.wait_ge(groups_used, at.group + 1)
                pe.wait_ge(blocks_used, at.block + 1)
                u0 = at.unit
                for s in range(HEADS + 1):
                    if s < HEADS:
                        if s >= 2:
                            pe.wait_ge(logits_ready, u0 + s - 1)
                        z = ACC[:, s % 2, :]
                        for c in range(NTOK):
                            t = slice(c * P, (c + 1) * P)
                            nc.tensor.matmul(z[:, t], QK[:, HEADS + s, t], QK[:, s, t], start=True, stop=True)
                        m = z[:, SEQ:2 * SEQ]
                        nc.tensor.matmul(m, ident[0:HEADS, s:s + 1].broadcast_to([HEADS, P]), MU[:, :], start=True, stop=False)
                        nc.tensor.matmul(m.rearrange("p (c t) -> p c t", c=2), ident,
                                         after.unsqueeze(1).broadcast_to([P, 2, P]), start=False, stop=True).then_inc(z_ready, 1)
                    if s >= 1:
                        h = s - 1
                        pe.wait_ge(logits_ready, u0 + h + 1)
                        if h >= 2:
                            pe.wait_ge(o_used, u0 + h - 1)
                        o = ACC[:, 2 + h % 2, 0:3 * (P + 1)].rearrange("p (i e) -> p i e", i=3)
                        for c in range(NTOK):
                            nc.tensor.matmul(o[:, c, :], PT[:, h % 2, c * P:(c + 1) * P], VA[:, c, h, :], start=True, stop=True)
                        nc.tensor.matmul(o[:, 2, :], QK[:, h, P:2 * P], CA[:, h, :], start=True, stop=True).then_inc(o_ready, 1)
                at.unit += HEADS
                def heads_of(half):
                    for g in (2 * half, 2 * half + 1):
                        group(at.group % 2, at.group, lambda tok, kk: XN[:, tok, (2 * g + kk) * P:(2 * g + kk + 1) * P],
                              (mixed, half + 1))
                        at.group += 1

                heads_of(0)
                out_product(lambda: heads_of(1))

            def mix2(layer):
                mid = XN[:, :, 0:COLS], XN[:, :, COLS:D]

                def transposes(of, wait):
                    for g in range(2):
                        group(at.group % 2, at.group, lambda tok, kk: of[:, tok, (2 * g + kk) * P:(2 * g + kk + 1) * P],
                              wait if g == 0 else None)
                        at.group += 1

                def roped(of):
                    at.staged += 1
                    transposes(of, (rope_done, at.staged))

                def taken_out(kind):
                    return (blocks_used, b0 + ORDER.index(kind) + 2)

                b0 = at.block

                def ik():
                    at.staged += 1
                    pe.wait_ge(rope_done, at.staged)
                    pe.wait_ge(groups_used, at.group)
                    for tok in range(NTOK):
                        mm = nc.tensor.transpose(TB[at.group % 2][:, tok * P:(tok + 1) * P], mid[0][:, tok, 0:P], ident)
                    mm.then_inc(groups_ready, 1)
                    at.group += 1

                def halves(h):
                    return slice(DH * (h % 2), DH * (h % 2) + DH)

                def index(h):
                    if h == 0:
                        pe.wait_ge(groups_used, at.group + 1)
                    if at.index >= 2:
                        pe.wait_ge(relu_ready, at.index - 1)
                    head_scores(QT2[halves(h), 2, h // 2, :], IKT[halves(h), :], (ZB, OB)[h % 2][:, 0:3 * P]).then_inc(index_z_ready, 1)
                    at.index += 1

                def unit(s):
                    u0 = at.unit
                    if s < HEADS:
                        if s == 0:
                            pe.wait_ge(relu_ready, at.index)
                            pe.wait_ge(mask_ready, layer + 1)
                        else:
                            pe.wait_ge(w_ready, u0 + s)
                        head_scores(QT2[halves(s), 0, s // 2, :], QT2[halves(s), 1, s // 2, :], ZB[:, 0:3 * P],
                                    (IDR[:, :], MK)).then_inc(z_ready, 1)
                    if 1 <= s <= HEADS:
                        u = s - 1
                        pe.wait_ge(w_ready, u0 + u + 1)
                        pe.wait_ge(groups_used, at.group)
                        for i in range(3):
                            mm = nc.tensor.transpose(TB[at.group % 2][:, i * P:(i + 1) * P], UW[:, u % 2, i * P:(i + 1) * P], ident)
                        mm.then_inc(groups_ready, 1)
                        at.group += 1
                        unit_group.append(at.group)
                    if s >= 2:
                        u = s - 2
                        pe.wait_ge(groups_used, unit_group[u] + 1)
                        if u >= 1:
                            pe.wait_ge(o_used, u0 + u)
                        head_output(lambda t: V2[:, t, u, :], OB[:, 0:2 * (DH + 1)].rearrange("p (t e) -> p t e", t=2),
                                    UT[:, u % 2, :], DH + 1).then_inc(o_ready, 1)
                    if s == HEADS + 1:
                        at.unit += HEADS

                def pooled():
                    pe.wait_ge(*taken_out("pu"))
                    for g2 in range(2):
                        pe.wait_ge(groups_used, at.group)
                        for k in range(2):
                            g = 2 * g2 + k
                            bank = TB[at.group % 2][:, k * SEQ:(k + 1) * SEQ]
                            u = [SX[:, tok, g * P:(g + 1) * P] for tok in range(NTOK)]
                            nc.tensor.matmul(bank[:, 0:P], u[0], PM[:, g, 0:P], start=True, stop=True)
                            nc.tensor.matmul(bank[:, P:SEQ], u[1], PM[:, g, P:2 * P], start=True, stop=False)
                            mm = nc.tensor.matmul(bank[:, P:P + WINDOWS[-1]], u[0], PM[:, g, 2 * P:], start=False, stop=True)
                        mm.then_inc(groups_ready, 1)
                        at.group += 1

                def pool_mix():
                    pe.wait_ge(pool_w_loaded, 16 * (layer + 1))
                    pe.wait_ge(groups_used, at.group + 1)
                    for g2 in range(2):
                        pe.wait_ge(groups_used, at.group)
                        for k in range(2):
                            g = 2 * g2 + k
                            mm = nc.tensor.matmul(TB[at.group % 2][:, k * SEQ:(k + 1) * SEQ], PW[:, g, :], PL[:, g, :],
                                                  start=True, stop=True)
                        mm.then_inc(groups_ready, 1)
                        at.group += 1

                def merged(half):
                    for g in (2 * half, 2 * half + 1):
                        group(at.group % 2, at.group, lambda tok, kk: XN[:, tok, (2 * g + kk) * P:(2 * g + kk + 1) * P],
                              (blocks_used, at.block + 1))
                        at.group += 1

                def attn_out():
                    pe.wait_ge(o_used, at.unit)
                    for g in range(2):
                        group(at.group % 2, at.group, lambda tok, kk: AG[:, tok, (2 * g + kk) * P:(2 * g + kk + 1) * P])
                        at.group += 1

                unit_group = []
                tasks = dict(ik=ik, q=lambda: roped(mid[0]), k=lambda: roped(mid[1]), iq=lambda: roped(ST),
                             conv_in=lambda: transposes(mid[0], taken_out("cc")),
                             conv_gate=lambda: transposes(mid[1], taken_out("cb")),
                             pool_gate=lambda: transposes(ST, taken_out("pgate")), pooled=pooled, pool_mix=pool_mix, attn_out=attn_out,
                             index=index, unit=unit, select=lambda tile: None, split=lambda branch: None,
                             rotate=lambda kind: None, merged=lambda: merged(0))
                branch = 0
                for b, kind in enumerate(ORDER):
                    if kind == "branch":
                        if branch % 2 == 0:
                            pe.wait_ge(branch_ready, 3 * layer + branch // 2 + 1)
                        branch += 1
                    if kind == "out":
                        break
                    xh, xl, k, n = (BH, BL, 4, COLS) if kind == "branch" else (XH, XL, KD, IKW if kind == "ik_iw" else COLS)
                    if b == 0:
                        first_product()
                    else:
                        product(xh, xl, at.chunk, at.chunk % 2, at.block, at.block % 2, 0, k, n, True, True,
                                between=lambda: run_tasks(tasks, 2 * b))
                    run_tasks(tasks, 2 * b + 1)
                    at.chunk += 1
                    at.block += 1
                out_product(lambda: merged(1))

            pe.sem_inc(weights_used, 1)
            pe.wait_ge(ident_loaded, 16)
            for stage in stages:
                {"ffn": ffn, "attn": attn, "mlstm": mlstm, "mix2": mix2}[stage[0]](*stage[1:])

        @block.scalar
        def _(act):
            at = At()

            def split_hi(c, slot, raw_wait, size):
                k, n = size
                act.wait_ge(raw_ready[slot], raw_wait)
                if not (isinstance(c, int) and c == 0):
                    act.wait_ge(weights_used, c)
                for lo, hi in ((0, k // 2 * n), (k // 2 * n, k * n)):
                    nc.scalar.activation(WH[:, slot, lo:hi], RAW[:, slot, lo:hi], ACT.Copy).then_inc(hi_ready, 1)

            def split_next(size):
                c = at.chunk + 1
                if size:
                    split_hi(c, c % 2, raw_value(c), size)

            def group_hi(bank_odd, ready, dst):
                act.wait_ge(groups_ready, ready)
                nc.scalar.activation(dst, TB[bank_odd][:, :], ACT.Copy).then_inc(groups_hi, 1)

            def activations(gs=range(KD // 2)):
                for g in gs:
                    group_hi(at.group % 2, at.group + 1, XH[:, 2 * g:2 * g + 2, :].rearrange("p k n -> p (k n)"))
                    at.group += 1

            def square(src, dst, col, since):
                if at.square >= since:
                    act.wait_ge(squares, at.square - since + 1)
                at.square += 1
                nc.scalar.activation(dst, src, ACT.Square, accum_out=SS[:, col:col + 1]).then_inc(squares, 1)

            def x_hi(tok):
                for half in range(2):
                    act.wait_ge(groups_ready, at.group + 1)
                    if at.stage == 0:
                        act.wait_ge(gains_loaded, 16)
                    for i in range(4):
                        k = 4 * half + i
                        ins = nc.scalar.activation(XH[:, k, tok * P:(tok + 1) * P], TB[at.group % 2][:, i * P:(i + 1) * P],
                                                   ACT.Copy, scale=GX[:, at.stage, k:k + 1])
                    ins.then_inc(groups_hi, 1)
                    at.group += 1

            def prenorm():
                if at.stage == 0:
                    x_hi(0)
                    split_hi(0, 0, raw_value(0), FULL)
                x_hi(1)
                for tok in range(NTOK):
                    square(X[:, tok, :], ST[:, :, :].rearrange("p t c -> p (t c)"), tok, 1)
                at.stage += 1
                at.rsqrt += 1

            def next_x():
                if at.stage < len(stages):
                    x_hi(0)

            def wait_rx():
                act.wait_ge(rsqrts, at.rsqrt)

            def block_ready(tok, last_chunk, block):
                if tok == 0:
                    act.wait_ge(tile0_ready, block + 1)
                else:
                    act.wait_ge(weights_used, last_chunk + 2)

            def postnorm(chunks_per_half):
                for half in range(2):
                    b = at.block - 2 + half
                    c = at.chunk - 1 - (1 - half) * chunks_per_half
                    for tok in range(NTOK):
                        if half and tok:
                            next_x()
                        block_ready(tok, c, b)
                        square(ACC[:, pair(b) + tok, :], ST[:, tok, :], half * 2 + tok, 2)
                at.rsqrt += 2

            def ffn(layer, which, next_size):
                prenorm()
                c0, b0, t0 = at.chunk, at.block, at.group

                def silu(b, b_odd, c):
                    for tok in range(NTOK):
                        block_ready(tok, c, b)
                        if tok == 0:
                            act.wait_ge(blocks_used, b + 1)
                        nc.scalar.activation(SIDE[:, tok, :], ACC[:, b_odd * 2 + tok, 0:GU], ACT.Silu, scale=RX[:, tok:tok + 1])\
                            .then_inc(silu_ready, 1)

                split_next(FULL)
                wait_rx()
                silu(b0, b0 % 2, c0)
                with act.Fori(0, (NGU - 1) // 2) as i:
                    for odd in range(2):
                        j = 2 * i + (1 + odd)
                        n = c0 + 2 + odd
                        split_hi(2 * i + n, n % 2, 32 * i + raw_value(n), FULL)
                        group_hi((t0 + odd) % 2, j + t0,
                                 HH[:, bass.ds(4 * i + 2 * odd, 2), :].rearrange("p k n -> p (k n)"))
                        silu(j + b0, (b0 + 1 + odd) % 2, j + c0)
                group_hi((t0 + NGU - 1) % 2, t0 + NGU,
                         HH[:, KF - 2:KF, :].rearrange("p k n -> p (k n)"))
                at.chunk += NGU
                at.block += NGU
                at.group += NGU
                for i, size in enumerate(DOWN_SIZES[1:] + [next_size]):
                    split_next(size)
                    at.chunk += 1
                at.block += 2
                postnorm(len(DOWN))

            def stage_block(j):
                if j > 0:
                    act.wait_ge(groups_ready, at.group)
                for tok in range(NTOK):
                    block_ready(tok, at.chunk, at.block)
                    ins = nc.scalar.activation(ST[:, tok, :], ACC[:, (at.block % 2) * 2 + tok, :], ACT.Copy,
                                               scale=RX[:, tok:tok + 1])
                ins.then_inc(blocks_used, 1)

            def out_product(next_size, split=True):
                if split:
                    split_next(FULL)
                at.chunk += 1
                split_next(next_size)
                at.chunk += 1
                at.block += 2
                postnorm(1)

            def attn(layer, next_size):
                prenorm()
                for j in range(6):
                    split_next(FULL)
                    if j == 0:
                        at.group += 1
                        wait_rx()
                    if j < 4:
                        stage_block(j)
                        at.group += 2
                    else:
                        for tok in range(NTOK):
                            block_ready(tok, at.chunk, at.block)
                            ins = nc.scalar.activation(VS[:, j - 4, tok, :, 0:DH],
                                                       ACC[:, (at.block % 2) * 2 + tok, :].rearrange("p (h e) -> p h e", e=DH),
                                                       ACT.Copy, scale=RX[:, tok:tok + 1])
                        ins.then_inc(blocks_used, 1)
                    at.chunk += 1
                    at.block += 1
                act.preload_act_table_set("natural_log_exp_and_others")
                act.wait_ge(bias_stored, 16)
                u0, t0 = at.unit, at.group
                n = 2 * HEADS
                for s in range(n + 1):
                    if s < HEADS:
                        z = ACC[:, s % 2, 0:3 * P]
                        a = UA[:, s % 2, :]
                        at.ln += 1
                        act.wait_ge(z_ready, u0 + s + 1)
                        if s >= 2:
                            act.wait_ge(logits_ready, u0 + s - 1)
                        nc.scalar.activation(a, z, ACT.Abs).then_inc(abs_ready, 1)
                        act.wait_ge(abs_ready, at.ln)
                        nc.scalar.activation(a, a, ACT.Exp, scale=-1.0).then_inc(exp_ready, 1)
                        act.wait_ge(exp_ready, at.ln)
                        nc.scalar.activation(a, a, ACT.Ln, bias=1.0).then_inc(ln_ready, 1)
                    if s >= 1:
                        u = s - 1
                        act.wait_ge(logits_ready, u0 + u + 1)
                        if u >= 2:
                            act.wait_ge(groups_ready, t0 + u - 1)
                        if u < HEADS:
                            nc.scalar.activation(UW[:, u % 2, :], UL[:, u % 2, :], ACT.Exp).then_inc(w_ready, 1)
                        else:
                            softmax_exp(u)
                at.unit += n
                at.group += n
                activations()
                out_product(next_size)

            def mlstm(layer, next_size):
                prenorm()
                split_next(FULL)
                at.chunk += 1
                at.block += 1
                act.preload_act_table_set("natural_log_exp_and_others")
                at.ln += 1
                wait_rx()
                act.wait_ge(blocks_used, at.block + 1)
                nc.scalar.activation(LS[:, :, :], GT[:, :, HEADS:], ACT.Abs).then_inc(abs_ready, 1)
                act.wait_ge(abs_ready, at.ln)
                nc.scalar.activation(LS[:, :, :], LS[:, :, :], ACT.Exp, scale=-1.0).then_inc(exp_ready, 1)
                act.wait_ge(exp_ready, at.ln)
                nc.scalar.activation(LS[:, :, :], LS[:, :, :], ACT.Ln, bias=1.0).then_inc(gates_act, 1)
                t0 = at.group
                for j in range(8):
                    split_next(FULL)
                    if j < 4:
                        stage_block(j)
                        at.group += 2
                    if 1 <= j < 5:
                        for g in range(2):
                            i = 2 * (j - 1) + g
                            act.wait_ge(groups_used, t0 + i + 2)
                            nc.scalar.activation(QK[:, 2 * i:2 * i + 2, :].rearrange("p k n -> p (k n)"), YC[:, i % 2, :],
                                                 ACT.Silu).then_inc(silus, 1)
                    if j >= 4:
                        side = j % 2
                        for tok in range(NTOK):
                            block_ready(tok, at.chunk, at.block)
                            src = ACC[:, (at.block % 2) * 2 + tok, :]
                            if j < 6:
                                ins = nc.scalar.activation(VA[:, tok, 4 * side:4 * side + 4, 0:P],
                                                           src.rearrange("p (h e) -> p h e", e=P), ACT.Copy,
                                                           scale=RX[:, tok:tok + 1])
                            else:
                                ins = nc.scalar.activation(SO[:, tok, side * COLS:(side + 1) * COLS], src, ACT.Sigmoid,
                                                           scale=RX[:, tok:tok + 1])
                        ins.then_inc(blocks_used, 1)
                    at.chunk += 1
                    at.block += 1
                at.group += 3
                act.wait_ge(gates_dve, 3)
                nc.scalar.activation(EX[:, :], EA[:, :], ACT.Exp).then_inc(gates_act, 1)
                act.wait_ge(gates_act, 2)
                for g in range(2):
                    act.wait_ge(groups_ready, at.group + 1)
                    for i in range(4):
                        h = 4 * g + i
                        ins = nc.scalar.activation(KN[:, h, :], TB[at.group % 2][:, i * P:(i + 1) * P], ACT.Copy,
                                                   scale=EX[:, h:h + 1])
                    ins.then_inc(groups_used, 1)
                    at.group += 1
                for h0 in range(0, HEADS, 3):
                    n = min(3, HEADS - h0)
                    act.wait_ge(groups_ready, at.group + 1)
                    nc.scalar.activation(CA[:, h0:h0 + n, :].rearrange("p h e -> p (h e)"),
                                         TB[at.group % 2][:, 0:n * (P + 1)], ACT.Copy).then_inc(groups_used, 1)
                    at.group += 1
                u0 = at.unit
                for s in range(HEADS + 2):
                    if s < HEADS:
                        act.wait_ge(z_ready, u0 + s + 1)
                        if s >= 2:
                            act.wait_ge(logits_ready, u0 + s - 1)
                        for c in range(NTOK):
                            ins = nc.scalar.activation(DT[:, s % 2, c * P:(c + 1) * P],
                                                       ACC[:, s % 2, SEQ + c * P:SEQ + (c + 1) * P], ACT.Exp,
                                                       bias=VV[:, c, s:s + 1], scale=-1.0)
                        ins.then_inc(w_ready, 1)
                    if 1 <= s <= HEADS:
                        h = s - 1
                        act.wait_ge(o_ready, u0 + h + 1)
                        o = ACC[:, 2 + h % 2, 0:2 * (P + 1)].rearrange("p (i e) -> p i e", i=2)
                        nc.scalar.activation(XN[:, :, h * P:(h + 1) * P], o[:, :, 0:P], ACT.Copy).then_inc(ho_ready, 1)
                    if s >= 2:
                        h = s - 2
                        act.wait_ge(o_used, u0 + h + 1)
                        for c in range(NTOK):
                            nc.scalar.activation(SIDE[:, 0, 0:P], XN[:, c, h * P:(h + 1) * P], ACT.Square,
                                                 accum_out=HS[:, c, h:h + 1]).then_inc(heads_squared, 1)
                            act.wait_ge(heads_squared, 2 * h + c + 1)
                at.unit += HEADS
                split_next(FULL)
                activations()
                out_product(next_size, False)

            def mix2(layer, next_size):
                prenorm()

                def skip(n):
                    at.group += n

                def index(h):
                    at.index += 1
                    act.wait_ge(index_z_ready, at.index)
                    if at.index > 2:
                        act.wait_ge(index_summed, at.index - 2)
                    nc.scalar.activation(RELU[:, h % 2, :], (ZB, OB)[h % 2][:, 0:3 * P], ACT.Relu, scale=DH ** -0.5).then_inc(relu_ready, 1)

                def unit(s):
                    if s < HEADS:
                        act.wait_ge(logits_ready, at.unit + s + 1)
                        if s >= 2:
                            act.wait_ge(groups_ready, unit_group[s - 2] + 1)
                        softmax_exp(s, ZB[:, 0:3 * P])
                    if 1 <= s <= HEADS:
                        u = s - 1
                        unit_group.append(at.group)
                        act.wait_ge(groups_ready, at.group + 1)
                        if u >= 2:
                            act.wait_ge(o_ready, at.unit + u - 1)
                        nc.scalar.activation(UT[:, u % 2, :], TB[at.group % 2][:, 0:3 * P], ACT.Copy).then_inc(groups_used, 1)
                        at.group += 1
                    if s == HEADS + 1:
                        at.unit += HEADS

                def split(branch):
                    at.branch += 1
                    act.wait_ge(groups_used, at.group + 1)
                    if branch:
                        act.wait_ge(weights_used, at.chunk + 1)
                    nc.scalar.activation(BH[:, :, :], YT[:, :, :], ACT.Copy).then_inc(branch_hi, 1)

                unit_group = []
                tasks = dict(ik=lambda: skip(1), index=index, unit=unit, select=lambda tile: None, split=split)
                tasks.update(rotate=lambda kind: None, merged=lambda: activations((0, 1)))
                for name in ("conv_in", "conv_gate", "pool_gate", "pool_mix"):
                    tasks[name] = lambda: skip(2)

                def plain(dst, scale=1.0):
                    for g in range(2):
                        act.wait_ge(groups_ready, at.group + 1)
                        nc.scalar.activation(dst[:, 2 * g:2 * g + 2, :].rearrange("p k n -> p (k n)"), TB[at.group % 2][:, :],
                                             ACT.Copy, scale=scale).then_inc(groups_used, 1)
                        at.group += 1

                def attn_out():
                    act.wait_ge(branch_ready, at.branch)
                    plain(YT)

                tasks.update(q=lambda: plain(QT2[:, 0], DH ** -0.5), k=lambda: plain(QT2[:, 1]), iq=lambda: plain(QT2[:, 2]),
                             pooled=lambda: plain(PL), attn_out=attn_out)

                def take_out(dst, func, n=COLS):
                    for tok in range(NTOK):
                        block_ready(tok, at.chunk, at.block)
                        src = ACC[:, (at.block % 2) * 2 + tok, 0:n]
                        if dst is V2:
                            src = src.rearrange("p (h e) -> p h e", e=DH)
                            ins = nc.scalar.activation(V2[:, tok, :, 0:DH], src, func, scale=RX[:, tok:tok + 1])
                        else:
                            ins = nc.scalar.activation(dst[:, tok, 0:n], src, func, scale=RX[:, tok:tok + 1])
                    ins.then_inc(blocks_used, 1)

                for b, kind in enumerate(ORDER):
                    if b + 1 < len(ORDER):
                        split_next(SIZES[b + 1])
                    else:
                        split_next(next_size)
                    if b == len(ORDER) - 2:
                        activations((2, 3))
                    run_tasks(tasks, 2 * b)
                    if b == 0:
                        wait_rx()
                    if kind in ("q", "k", "iq"):
                        if kind != "iq":
                            act.wait_ge(rope_done, at.staged)
                            for tok in range(NTOK):
                                block_ready(tok, at.chunk, at.block)
                                nc.scalar.activation(SQ[:, tok, :], ACC[:, (at.block % 2) * 2 + tok, :], ACT.Square,
                                                     scale=RX[:, tok:tok + 1])
                        at.staged += 2 if kind == "iq" else 1
                        take_out(QS, ACT.Copy)
                    elif kind == "ik_iw":
                        take_out(XN[:, :, COLS:], ACT.Copy, IKW)
                    elif kind == "v":
                        take_out(V2, ACT.Copy)
                    elif kind == "agate":
                        take_out(AG, ACT.Silu)
                    elif kind in ("cx", "cgate", "pu"):
                        if kind != "cx":
                            act.wait_ge(blocks_used, at.block + 1)
                        take_out(SX, {"cgate": ACT.Silu}.get(kind, ACT.Copy))
                    elif kind == "pgate":
                        take_out(ST, ACT.Silu)
                    elif kind == "mgate":
                        act.wait_ge(blocks_used, at.block + 1)
                        act.wait_ge(groups_ready, at.group)
                        take_out(ST, ACT.Sigmoid)
                    run_tasks(tasks, 2 * b + 1)
                    at.chunk += 1
                    at.block += 1
                next_x()

            def softmax_exp(u, z=None):
                z = ACC[:, u % 2, 0:3 * P] if z is None else z
                nc.scalar.activation(UW[:, u % 2, 0:P], z[:, 0:P], ACT.Exp, bias=NM[:, u % 2, 0:1])
                nc.scalar.activation(UW[:, u % 2, P:3 * P], z[:, P:3 * P], ACT.Exp,
                                     bias=NM[:, u % 2, 1:2]).then_inc(w_ready, 1)

            act.dma_start(GX[:, :, :], gains_by_feature).then_inc(gains_loaded, 16)
            for i, stage in enumerate(stages):
                {"ffn": ffn, "attn": attn, "mlstm": mlstm, "mix2": mix2}[stage[0]](*stage[1:], first_size(i + 1))

        @block.gpsimd
        def _(pool):
            at = At()
            steps = [0]

            def step(ins):
                steps[0] += 1
                ins.then_inc(pool_step, 1)
                pool.wait_ge(pool_step, steps[0])

            def load_row(r):
                if r < len(rows):
                    pool.dma_start(G[:, r % 2, :], rows[r].partition_broadcast(P)).then_inc(row_loaded[r % 2], 16)

            def rsqrt_of_x():
                at.square += NTOK
                pool.wait_ge(squares, at.square)
                step(nc.gpsimd.tensor_scalar(MS[:, :], SS[:, 0:2], 1.0 / D, EPS, ALU.mult, ALU.add))
                nc.gpsimd.tensor_tensor(RX[:, :], MS[:, :], HALF[:, :], ALU.pow).then_inc(rsqrts, 1)

            def rsqrt_of_sum(scale):
                for tok in range(NTOK):
                    pool.wait_ge(squares, at.square + 3 + tok)
                    ms, t = MS[:, tok:tok + 1], TMP2[:, tok:tok + 1]
                    step(nc.gpsimd.tensor_tensor(t, SS[:, tok:tok + 1], SS[:, 2 + tok:3 + tok], ALU.add))
                    step(nc.gpsimd.tensor_scalar(ms, t, scale ** -2 / D, scale ** -2 * EPS, ALU.mult, ALU.add))
                    nc.gpsimd.tensor_tensor(RS[:, tok:tok + 1], ms, HALF[:, tok:tok + 1], ALU.pow).then_inc(rsqrts, 1)
                    at.rsqrt += 1
                    pool.wait_ge(rsqrts, at.rsqrt)
                at.square += 4

            def row_used():
                pool.wait_ge(blocks_used, at.block + 1)
                load_row(at.row + 2)
                at.row += 1

            def constants():
                load_row(0)
                load_row(1)
                pool.dma_start(CT[:, P:], c_tiles[:, P:]).then_inc(consts_loaded, 16)
                pool.dma_start(ONEHOT[:, :], c_onehot).then_inc(consts_loaded, 16)
                pool.dma_start(RB[0:32, :], rel_bias).then_inc(consts_loaded, 16)
                for layer in range(DEPTH):
                    for i, gains in enumerate((q_norm_g_2, k_norm_g_2)):
                        pool.dma_start(GQK[:, layer, i, :], gains[layer].partition_broadcast(P)).then_inc(small_loaded, 16)
                pool.dma_start(CW2[:, :, :, :], conv_taps_2).then_inc(small_loaded, 16)
                pool.dma_start(PS2[:, :, :], pool_scale_2).then_inc(small_loaded, 16)
                pool.dma_start(CW[:, :, :], conv_taps).then_inc(small_loaded, 16)
                pool.dma_start(BG[:, :], mlstm_b_gates[0].partition_broadcast(P)).then_inc(small_loaded, 16)

            def ffn(layer, which):
                rsqrt_of_x()
                at.rsqrt += 1
                if layer == which == 0:
                    constants()
                rsqrt_of_sum(0.5)
                at.block += BLOCKS["ffn"]
                row_used()

            def attn(layer):
                pool.wait_ge(blocks_used, at.block + 1)
                rsqrt_of_x()
                at.rsqrt += 1
                pool.wait_ge(bias_rows, 1)
                pool.dma_start(bias_dram, BROW[:, :]).then_inc(bias_stored, 16)
                pool.wait_ge(bias_stored, 16)
                pool.dma_start(BT[:, :, :], bias_by_query).then_inc(bias_ready, 16)
                rsqrt_of_sum(1.0)
                at.block += BLOCKS["attn"]
                row_used()

            def mlstm(layer):
                at.block += BLOCKS["mlstm"]
                rsqrt_of_x()
                at.rsqrt += 1
                pool.wait_ge(gain_used, 4)
                load_row(at.row + 2)
                at.row += 1
                pool.wait_ge(heads_ready, 1)
                hq = HQ[:, :, :].rearrange("p t h -> p (t h)")
                step(nc.gpsimd.tensor_scalar(hq, hq, 1.0 / P, EPS, ALU.mult, ALU.add))
                nc.gpsimd.tensor_tensor(HF[:, :, :].rearrange("p t h -> p (t h)"), hq, HALF16[:, :], ALU.pow)\
                    .then_inc(heads_scaled, 1)
                rsqrt_of_sum(1.0)
                row_used()

            def mix2(layer):
                pool.wait_ge(blocks_used, at.block + 1)
                if layer == 0:
                    pool.dma_start(CS[:, :, :, :], c_rope).then_inc(tables_loaded, 16)
                    pool.dma_start(PM[:, :, :], c_pool).then_inc(tables_loaded, 16)
                pool.dma_start(PW[:, :, :], pool_w_2[layer].rearrange("g c d -> c g d")).then_inc(pool_w_loaded, 16)
                rsqrt_of_x()
                at.rsqrt += 1
                for i in range(2):
                    at.head_norm += 1
                    pool.wait_ge(head_sums, at.head_norm)
                    step(nc.gpsimd.tensor_scalar(HM[:, :], HN[:, :], 1.0 / DH, EPS, ALU.mult, ALU.add))
                    nc.gpsimd.tensor_tensor(HR[:, :], HM[:, :], HALF16[:, :], ALU.pow).then_inc(head_rsqrts, 1)
                at.block += BLOCKS["mix2"]

            step(nc.gpsimd.memset(HALF[:, :], -0.5))
            step(nc.gpsimd.memset(HALF16[:, :], -0.5))
            nc.gpsimd.memset(RB[32:33, :], NEG).then_inc(mask_set, 1)
            pool.wait_ge(mask_set, 1)
            for stage in stages:
                {"ffn": ffn, "attn": attn, "mlstm": mlstm, "mix2": mix2}[stage[0]](*stage[1:])

        @block.vector
        def _(dve):
            at = At()

            def split_lo(c, slot, size):
                k, n = size
                for part, (lo, hi) in enumerate(((0, k // 2 * n), (k // 2 * n, k * n))):
                    dve.wait_ge(hi_ready, 2 * c + (part + 1))
                    nc.vector.tensor_tensor(WL[:, slot, lo:hi], RAW[:, slot, lo:hi],
                                            WH[:, slot, lo:hi].bitcast(F32), ALU.subtract).then_inc(lo_ready, 1)

            def split_next(size):
                c = at.chunk + 1
                if size:
                    split_lo(c, c % 2, size)

            def group_lo(bank_odd, hi, dst_lo, src_hi):
                dve.wait_ge(groups_hi, hi)
                nc.vector.tensor_tensor(dst_lo, TB[bank_odd][:, :], src_hi.bitcast(F32), ALU.subtract)\
                    .then_inc(groups_used, 1)

            def activations(gs=range(KD // 2)):
                for g in gs:
                    group_lo(at.group % 2, at.rounded + 1, XL[:, 2 * g:2 * g + 2, :].rearrange("p k n -> p (k n)"),
                             XH[:, 2 * g:2 * g + 2, :].rearrange("p k n -> p (k n)"))
                    at.group += 1
                    at.rounded += 1

            def x_lo(tok):
                if at.stage == 0:
                    dve.wait_ge(gains_loaded, 16)
                for half in range(2):
                    dve.wait_ge(groups_hi, at.rounded + 1)
                    for i in range(4):
                        k = 4 * half + i
                        t = slice(tok * P, (tok + 1) * P)
                        ins = nc.vector.scalar_tensor_tensor(XL[:, k, t], TB[at.group % 2][:, i * P:(i + 1) * P],
                                                             GX[:, at.stage, k:k + 1], XH[:, k, t].bitcast(F32),
                                                             ALU.mult, ALU.subtract)
                    ins.then_inc(groups_used, 1)
                    at.group += 1
                    at.rounded += 1

            def prenorm():
                if at.stage == 0:
                    x_lo(0)
                    split_lo(0, 0, FULL)
                x_lo(1)
                at.stage += 1
                at.rsqrt += 1
                at.square += NTOK

            def next_x():
                if at.stage < len(stages):
                    x_lo(0)

            def wait_rx():
                dve.wait_ge(rsqrts, at.rsqrt)

            def postnorm():
                row = at.row % 2
                dve.wait_ge(row_loaded[row], 16 * (at.row // 2 + 1))
                at.row += 1
                def scaled(half, tok):
                    at.square += 1
                    dve.wait_ge(squares, at.square)
                    cols = slice(half * COLS, (half + 1) * COLS)
                    return nc.vector.tensor_tensor(XN[:, tok, cols], ACC[:, pair(at.block - 2 + half) + tok, :], G[:, row, cols], ALU.mult)

                def add(tok):
                    at.rsqrt += 1
                    dve.wait_ge(rsqrts, at.rsqrt)
                    for half in range(2):
                        cols = slice(half * COLS, (half + 1) * COLS)
                        nc.vector.scalar_tensor_tensor(X[:, tok, cols], XN[:, tok, cols], RS[:, tok:tok + 1], X[:, tok, cols],
                                                       ALU.mult, ALU.add).then_inc(x_ready, 1)

                scaled(0, 0)
                scaled(0, 1).then_inc(blocks_used, 1)
                step(scaled(1, 0))
                add(0)
                next_x()
                scaled(1, 1).then_inc(blocks_used, 1)
                dve.wait_ge(blocks_used, at.block + 1)
                add(1)

            def ffn(layer, which, next_size):
                prenorm()
                c0, b0, t0, g0 = at.chunk, at.block, at.group, at.rounded

                def gated(b_odd, silus, groups):
                    for tok in range(NTOK):
                        dve.wait_ge(silu_ready, silus + tok + 1)
                        if tok == 0:
                            dve.wait_ge(groups_ready, groups)
                        mul = nc.vector.scalar_tensor_tensor(ST[:, tok, 0:GU], ACC[:, b_odd * 2 + tok, GU:COLS],
                                                             RX[:, tok:tok + 1], SIDE[:, tok, :], ALU.mult, ALU.mult)
                    mul.then_inc(blocks_used, 1)

                s0 = at.silu
                split_next(FULL)
                wait_rx()
                gated(b0 % 2, s0, t0)
                with dve.Fori(0, (NGU - 1) // 2) as i:
                    for odd in range(2):
                        j = 2 * i + (1 + odd)
                        n = c0 + 2 + odd
                        split_lo(2 * i + n, n % 2, FULL)
                        at_k = bass.ds(4 * i + 2 * odd, 2)
                        group_lo((t0 + odd) % 2, j + g0,
                                 HL[:, at_k, :].rearrange("p k n -> p (k n)"),
                                 HH[:, at_k, :].rearrange("p k n -> p (k n)"))
                        gated((b0 + 1 + odd) % 2, 2 * j + s0, j + t0)
                group_lo((t0 + NGU - 1) % 2, g0 + NGU,
                         HL[:, KF - 2:KF, :].rearrange("p k n -> p (k n)"),
                         HH[:, KF - 2:KF, :].rearrange("p k n -> p (k n)"))
                at.silu += 2 * NGU
                at.chunk += NGU
                at.block += NGU
                at.group += NGU
                at.rounded += NGU
                for size in DOWN_SIZES[1:] + [next_size]:
                    split_next(size)
                    at.chunk += 1
                at.block += 2
                postnorm()

            steps = [0]

            def step(ins):
                steps[0] += 1
                ins.then_inc(dve_step, 1)
                dve.wait_ge(dve_step, steps[0])

            def group_plain(dst, scale=None):
                dve.wait_ge(groups_ready, at.group + 1)
                src = TB[at.group % 2][:, :]
                ins = nc.vector.tensor_copy(dst, src) if scale is None else nc.vector.tensor_scalar(dst, src, scale, None, ALU.mult)
                ins.then_inc(groups_used, 1)
                at.group += 1

            def out_product(next_size, split=True):
                if split:
                    split_next(FULL)
                at.chunk += 1
                split_next(next_size)
                at.chunk += 1
                at.block += 2
                postnorm()

            def softmax_maxima(u, z=None):
                z = ACC[:, u % 2, 0:3 * P] if z is None else z
                nc.vector.tensor_reduce(NM[:, u % 2, 0:1], z[:, 0:P], AX_X, ALU.max, negate=True)
                nc.vector.tensor_reduce(NM[:, u % 2, 1:2], z[:, P:3 * P], AX_X, ALU.max, negate=True)\
                    .then_inc(logits_ready, 1)

            def softmax_output(u, dst):
                o = ACC[:, 2 + u % 2, 0:2 * (DH + 1)].rearrange("p (t e) -> p t e", t=2)
                step(nc.vector.reciprocal(RD[:, u % 2, :].unsqueeze(2), o[:, :, DH:DH + 1]))
                nc.vector.tensor_tensor(dst, o[:, :, 0:DH], RD[:, u % 2, :].unsqueeze(2).broadcast_to([P, 2, DH]), ALU.mult)\
                    .then_inc(o_used, 1)

            def attn(layer, next_size):
                nc.vector.memset(VS[:, :, :, :, DH:DH + 1], 1.0)
                prenorm()
                for j in range(6):
                    split_next(FULL)
                    if j == 0:
                        dve.wait_ge(groups_ready, at.group + 1)
                        nc.vector.tensor_copy(BROW[:, :], TB[at.group % 2][0:HEADS, 0:3 * P]).then_inc(bias_rows, 1)
                        dve.wait_ge(bias_rows, 1)
                        dve.sem_inc(groups_used, 1)
                        at.group += 1
                    if 1 <= j < 5:
                        for g in range(2):
                            group_plain(QT[:, j - 1, 2 * g:2 * g + 2, :].rearrange("p k n -> p (k n)"),
                                        DH ** -0.5 if j % 2 else None)
                    at.chunk += 1
                    at.block += 1
                u0, t0 = at.unit, at.group
                n = 2 * HEADS
                for s in range(n + 3):
                    if s < HEADS:
                        z = ACC[:, s % 2, 0:3 * P]
                        a, l = UA[:, s % 2, :], UL[:, s % 2, :]
                        at.ln += 1
                        dve.wait_ge(ln_ready, at.ln)
                        step(nc.vector.scalar_tensor_tensor(a, z, 0.0, a, ALU.max, ALU.add))
                        if s >= 2:
                            dve.wait_ge(w_ready, u0 + s - 1)
                        for lo, hi in ((0, P), (P, 3 * P)):
                            ins = nc.vector.tensor_tensor_scan(l[:, lo:hi][:, ::-1], goes_on[:, lo:hi][:, ::-1],
                                                               a[:, lo:hi][:, ::-1], 0.0, ALU.mult, ALU.add)
                        step(ins)
                        nc.vector.tensor_tensor(l, z, l, ALU.subtract).then_inc(logits_ready, 1)
                    elif s < n:
                        dve.wait_ge(z_ready, u0 + s + 1)
                        dve.wait_ge(w_ready, u0 + s - 1)
                        softmax_maxima(s)
                    if 2 <= s <= n + 1:
                        u = s - 2
                        dve.wait_ge(groups_ready, t0 + u + 1)
                        if u >= 2:
                            dve.wait_ge(o_ready, u0 + u - 1)
                        nc.vector.tensor_tensor(UT[:, u % 2, :], TB[(t0 + u) % 2][:, 0:3 * P],
                                                past_t if u < HEADS else count_t, ALU.mult).then_inc(groups_used, 1)
                    if s >= 3:
                        u = s - 3
                        dve.wait_ge(o_ready, u0 + u + 1)
                        dst = XN[:, :, u * DH:(u + 1) * DH]
                        if u < HEADS:
                            o = ACC[:, 2 + u % 2, 0:2 * (DH + 1)].rearrange("p (t e) -> p t e", t=2)
                            nc.vector.tensor_copy(dst, o[:, :, 0:DH]).then_inc(o_used, 1)
                        else:
                            softmax_output(u, dst)
                at.unit += n
                at.group += n
                activations()
                out_product(next_size)

            def convolve(i):
                dve.wait_ge(groups_ready, at.group + 1)
                if i >= 2:
                    dve.wait_ge(silus, i - 1)
                for tap in range(3, -1, -1):
                    shift = 3 - tap
                    for kk in range(2):
                        src = TB[at.group % 2][:, kk * SEQ:(kk + 1) * SEQ - shift]
                        dst = YC[:, i % 2, kk * SEQ + shift:(kk + 1) * SEQ]
                        w = CW[:, 2 * i + kk, tap:tap + 1]
                        if shift == 0:
                            ins = nc.vector.tensor_scalar(dst, src, w, None, ALU.mult)
                        else:
                            ins = nc.vector.scalar_tensor_tensor(dst, src, w, dst, ALU.mult, ALU.add)
                    if tap:
                        step(ins)
                ins.then_inc(groups_used, 1)
                at.group += 1

            def mlstm(layer, next_size):
                nc.vector.memset(VA[:, :, :, P:P + 1], 1.0)
                prenorm()
                split_next(FULL)
                dve.wait_ge(small_loaded, 16 * 8)
                wait_rx()
                for tok in range(NTOK):
                    block_ready(tok, at.chunk, at.block)
                    ins = nc.vector.scalar_tensor_tensor(GT[:, tok, :], ACC[:, (at.block % 2) * 2 + tok, 0:2 * HEADS],
                                                         RX[:, tok:tok + 1], BG[:, :], ALU.mult, ALU.add)
                ins.then_inc(blocks_used, 1)
                at.chunk += 1
                at.block += 1
                dve.wait_ge(gates_act, 1)
                nc.vector.scalar_tensor_tensor(LF[:, :, :], GT[:, :, HEADS:], 0.0, LS[:, :, :], ALU.min, ALU.subtract)\
                    .then_inc(gates_dve, 1)
                gain = at.row
                at.row += 1
                for j in range(8):
                    split_next(FULL)
                    if 1 <= j < 5:
                        convolve(2 * (j - 1))
                        convolve(2 * (j - 1) + 1)
                    if j >= 5:
                        bank = TB[at.group % 2]
                        dve.wait_ge(groups_ready, at.group + 1)
                    if j == 5:
                        sums = bank[:, 0:2 * HEADS].rearrange("p (t h) -> p t h", t=2)
                        nc.vector.tensor_copy(BC[:, :, :], sums)
                        nc.vector.tensor_tensor(VV[:, :, :], GT[:, :, 0:HEADS], sums, ALU.subtract).then_inc(groups_used, 1)
                    if j == 6:
                        nc.vector.tensor_copy(GL[:, 0:1], bank[0:HEADS, 3 * P - 1:3 * P])
                        nc.vector.tensor_copy(VT[:, :], bank[0:HEADS, 0:SEQ]).then_inc(groups_used, 1)
                        dve.wait_ge(groups_used, at.group + 2)
                        step(nc.vector.tensor_tensor_scan(MU[:, 0:P], VT[:, 0:P], VT[:, 0:P], 0.0, ALU.max, ALU.max))
                        step(nc.vector.tensor_tensor(GL[:, 1:2], GL[:, 0:1], MU[:, P - 1:P], ALU.add))
                        nc.vector.tensor_tensor_scan(MU[:, P:], VT[:, P:], VT[:, P:], GL[:, 1:2], ALU.max, ALU.max)
                        nc.vector.tensor_scalar(DG[:, 0:HEADS], ident[0:HEADS, 0:HEADS], MU[:, P - 1:P], None, ALU.mult)
                        nc.vector.tensor_scalar(DG[:, HEADS:], ident[0:HEADS, 0:HEADS], GL[:, 1:2], None, ALU.mult)\
                            .then_inc(gates_dve, 1)
                    if j == 7:
                        nc.vector.tensor_copy(MUB[:, :], bank[:, 0:4 * HEADS]).then_inc(groups_used, 1)
                        dve.wait_ge(groups_used, at.group + 2)
                        H = HEADS
                        nc.vector.tensor_tensor(EA[:, 0:H], VV[:, 0, :], MUB[:, 2 * H:3 * H], ALU.subtract)
                        nc.vector.tensor_tensor(EA[:, H:2 * H], MUB[:, 3 * H:4 * H], MUB[:, H:2 * H], ALU.subtract)
                        nc.vector.scalar_tensor_tensor(EA[:, 2 * H:4 * H], BC[:, :, :].rearrange("p t h -> p (t h)"), -1.0,
                                                       MUB[:, 0:2 * H], ALU.mult, ALU.subtract).then_inc(gates_dve, 1)
                    if j >= 5:
                        at.group += 1
                    at.chunk += 1
                    at.block += 1
                dve.wait_ge(row_loaded[gain % 2], 16 * (gain // 2 + 1))
                dve.wait_ge(blocks_used, at.block + 1)
                for half in range(2):
                    for tok in range(NTOK):
                        cols = slice(half * COLS, (half + 1) * COLS)
                        nc.vector.tensor_tensor(SO[:, tok, cols], SO[:, tok, cols], G[:, gain % 2, cols], ALU.mult).then_inc(gain_used, 1)
                dve.wait_ge(gates_act, 2)
                step(nc.vector.tensor_scalar(WI[:, :], EX[:, HEADS:2 * HEADS], P ** -0.5, None, ALU.mult))
                at.group += 5
                u0 = at.unit
                for s in range(HEADS + 1):
                    if s < HEADS:
                        dve.wait_ge(w_ready, u0 + s + 1)
                        if s >= 2:
                            dve.wait_ge(o_ready, u0 + s - 1)
                        nc.vector.scalar_tensor_tensor(PT[:, s % 2, :], ACC[:, s % 2, 0:SEQ], P ** -0.5, DT[:, s % 2, :],
                                                       ALU.mult, ALU.mult).then_inc(logits_ready, 1)
                    if s >= 1:
                        h = s - 1
                        dve.wait_ge(ho_ready, h + 1)
                        o = ACC[:, 2 + h % 2, 0:3 * (P + 1)].rearrange("p (i e) -> p i e", i=3)
                        nc.vector.tensor_copy(N3[:, h, :].unsqueeze(2), o[:, :, P:P + 1])
                        num = XN[:, 1, h * P:(h + 1) * P]
                        nc.vector.scalar_tensor_tensor(num, o[:, 2, 0:P], WI[:, h:h + 1], num, ALU.mult, ALU.add).then_inc(o_used, 1)
                at.unit += HEADS
                dve.wait_ge(o_used, at.unit)
                step(nc.vector.tensor_tensor(NI[:, :], N3[:, :, 2], EX[:, HEADS:2 * HEADS], ALU.mult))
                step(nc.vector.scalar_tensor_tensor(N3[:, :, 1], NI[:, :], P ** -0.5, N3[:, :, 1], ALU.mult, ALU.add))
                for c in range(NTOK):
                    ins = nc.vector.scalar_tensor_tensor(AN[:, c, :], N3[:, :, c], -1.0, EX[:, (2 + c) * HEADS:(3 + c) * HEADS],
                                                         ALU.mult, ALU.max)
                step(ins)
                step(nc.vector.tensor_tensor(AN[:, :, :], AN[:, :, :], N3[:, :, 0:NTOK].rearrange("p h c -> p c h"), ALU.max))
                step(nc.vector.reciprocal(RN[:, :, :], AN[:, :, :]))
                step(nc.vector.tensor_tensor(HQ[:, :, :], RN[:, :, :], RN[:, :, :], ALU.mult))
                dve.wait_ge(heads_squared, 2 * HEADS)
                nc.vector.tensor_tensor(HQ[:, :, :], HQ[:, :, :], HS[:, :, :], ALU.mult).then_inc(heads_ready, 1)
                dve.wait_ge(heads_scaled, 1)
                step(nc.vector.tensor_tensor(HF[:, :, :], HF[:, :, :], RN[:, :, :], ALU.mult))
                for half in range(2):
                    for c in range(NTOK):
                        for h in range(half * HEADS // 2, (half + 1) * HEADS // 2):
                            cols = slice(h * P, (h + 1) * P)
                            ins = nc.vector.scalar_tensor_tensor(XN[:, c, cols], XN[:, c, cols], HF[:, c, h:h + 1], SO[:, c, cols],
                                                                 ALU.mult, ALU.mult)
                    ins.then_inc(mixed, 1)
                    if half == 0:
                        activations((0, 1))
                split_next(FULL)
                activations((2, 3))
                out_product(next_size, False)

            def mix2(layer, next_size):
                nc.vector.memset(V2[:, :, :, DH:DH + 1], 1.0)
                prenorm()
                if layer == 0:
                    dve.wait_ge(tables_loaded, 32)
                    nc.vector.tensor_copy(IDR[:, :], ident)
                mid = XN[:, :, 0:COLS], XN[:, :, COLS:D]
                scores, work = IS[:, 0, :], IS[:, 1, :]
                tiles = ((0, 0, P), (1, P, 3 * P))

                def rope(src, width, dsts, gain=None):
                    n = width // DH
                    if at.staged:
                        dve.wait_ge(rope_done, at.staged)
                    at.staged += 1
                    if gain is not None:
                        heads = QS[:, :, :].rearrange("p t (h e) -> p (t h) e", e=DH)
                        nc.vector.tensor_reduce(HN[:, :], SQ[:, :, :].rearrange("p t (h e) -> p (t h) e", e=DH), AX_X, ALU.add)                            .then_inc(head_sums, 1)
                        at.head_norm += 1
                        dve.wait_ge(head_rsqrts, at.head_norm)
                        step(nc.vector.tensor_tensor(heads, heads, HR[:, :].unsqueeze(2).broadcast_to([P, NTOK * n, DH]), ALU.mult))
                        step(nc.vector.tensor_tensor(heads, heads, gain.unsqueeze(1).broadcast_to([P, NTOK * n, DH]), ALU.mult))

                    def heads_of(t):
                        return t[:, :, 0:width].rearrange("p t (h e) -> p t h e", e=DH)

                    def table(i, lo, hi):
                        return CS[:, i, :, lo:hi].unsqueeze(2).broadcast_to([P, NTOK, n, hi - lo])

                    q, a, b, m = heads_of(src), heads_of(SQ), heads_of(T3), DH // 2
                    nc.vector.tensor_tensor(b[:, :, :, 0:m], q[:, :, :, m:DH], table(1, 0, m), ALU.mult)
                    nc.vector.tensor_tensor(b[:, :, :, m:DH], q[:, :, :, 0:m], table(1, m, DH), ALU.mult)
                    step(nc.vector.tensor_tensor(a, q, table(0, 0, DH), ALU.mult))
                    for dst in dsts:
                        ins = nc.vector.tensor_tensor(heads_of(dst), a, b, ALU.add)
                    ins.then_inc(rope_done, 1)

                def rotate(kind):
                    dve.wait_ge(blocks_used, b0 + ORDER.index(kind) + 2)
                    if kind == "iq":
                        rope(QS, COLS, (ST,))
                    elif kind == "ik_iw":
                        of = XN[:, :, COLS:]
                        nc.vector.tensor_copy(IW[:, :, :], of[:, :, DH:IKW])
                        rope(of, DH, (mid[0][:, :, 0:DH], mid[0][:, :, DH:2 * DH]))
                    else:
                        i = ("q", "k").index(kind)
                        rope(QS, COLS, (mid[i],), GQK[:, layer, i, :])

                b0 = at.block

                def skip(n):
                    at.group += n

                def ik():
                    dve.wait_ge(groups_ready, at.group + 1)
                    nc.vector.tensor_copy(IKT[:, :], TB[at.group % 2][:, 0:SEQ]).then_inc(groups_used, 1)
                    at.group += 1

                def index(h):
                    at.index += 1
                    dve.wait_ge(relu_ready, at.index)
                    if h:
                        dve.wait_ge(index_summed, at.index - 1)
                    for tok, lo, hi in tiles:
                        r, s, w = RELU[:, h % 2, lo:hi], scores[:, lo:hi], IW[:, tok, h:h + 1]
                        if h == 0:
                            ins = nc.vector.tensor_scalar(s, r, w, None, ALU.mult)
                        else:
                            ins = nc.vector.scalar_tensor_tensor(s, r, w, s, ALU.mult, ALU.add)
                    ins.then_inc(index_summed, 1)

                def select(tok):
                    _, lo, hi = tiles[tok]
                    s, w, m = scores[:, lo:hi], work[:, lo:hi], MK[:, lo:hi]
                    diag = slice(hi - P, hi)
                    if tok == 0:
                        dve.wait_ge(index_summed, at.index)
                    step(nc.vector.tensor_scalar(s, s, HEADS ** -0.5, None, ALU.mult))
                    step(nc.vector.tensor_tensor(scores[:, diag], scores[:, diag], later, ALU.add))
                    src = s
                    for i in range(TOPK // 8):
                        step(nc.vector.max(M8[:, :], src))
                        step(nc.vector.match_replace(w, M8[:, :], src, TAKEN))
                        src = w
                    step(nc.vector.tensor_scalar(m, w, TAKEN, NEG, ALU.not_equal, ALU.mult))
                    ins = nc.vector.tensor_tensor(MK[:, diag], MK[:, diag].bitcast(F32), later, ALU.add)
                    if tok == NTOK - 1:
                        ins.then_inc(mask_ready, 1)

                def unit(s):
                    if s < HEADS:
                        dve.wait_ge(z_ready, at.unit + s + 1)
                        if s >= 2:
                            dve.wait_ge(w_ready, at.unit + s - 1)
                        softmax_maxima(s, ZB[:, 0:3 * P])
                    if 1 <= s <= HEADS:
                        skip(1)
                    if s >= 2:
                        u = s - 2
                        dve.wait_ge(o_ready, at.unit + u + 1)
                        o = OB[:, 0:2 * (DH + 1)].rearrange("p (t e) -> p t e", t=2)
                        gate = AG[:, :, u * DH:(u + 1) * DH]
                        step(nc.vector.reciprocal(RD[:, u % 2, :].unsqueeze(2), o[:, :, DH:DH + 1]))
                        step(nc.vector.tensor_tensor(T2[:, :, :], o[:, :, 0:DH],
                                                     RD[:, u % 2, :].unsqueeze(2).broadcast_to([P, 2, DH]), ALU.mult))
                        nc.vector.tensor_tensor(gate, gate, T2[:, :, :], ALU.mult).then_inc(o_used, 1)
                    if s == HEADS + 1:
                        at.unit += HEADS

                def conv_in():
                    for g in range(2):
                        dve.wait_ge(groups_ready, at.group + 1)
                        for tap in range(TAPS_2 - 1, -1, -1):
                            shift = TAPS_2 - 1 - tap
                            for kk in range(2):
                                tile = 2 * g + kk
                                src = TB[at.group % 2][:, kk * SEQ:(kk + 1) * SEQ - shift]
                                w = CW2[:, layer, tile, tap:tap + 1]
                                dst = YT[:, tile, shift:]
                                if shift == 0:
                                    ins = nc.vector.tensor_scalar(dst, src, w, None, ALU.mult)
                                else:
                                    ins = nc.vector.scalar_tensor_tensor(dst, src, w, dst, ALU.mult, ALU.add)
                            if tap:
                                step(ins)
                        ins.then_inc(groups_used, 1)
                        at.group += 1

                def times_yt():
                    dve.wait_ge(groups_used, at.group + 1)
                    for g in range(2):
                        dve.wait_ge(groups_ready, at.group + 1)
                        y = YT[:, 2 * g:2 * g + 2, :].rearrange("p k n -> p (k n)")
                        nc.vector.tensor_tensor(y, y, TB[at.group % 2][:, :], ALU.mult).then_inc(groups_used, 1)
                        at.group += 1

                def pool_gate():
                    for g in range(2):
                        dve.wait_ge(groups_ready, at.group + 1)
                        for kk in range(2):
                            tile = 2 * g + kk
                            ins = nc.vector.tensor_scalar(YT[:, tile, :], TB[at.group % 2][:, kk * SEQ:(kk + 1) * SEQ],
                                                          PS2[:, layer, tile:tile + 1], None, ALU.mult)
                        ins.then_inc(groups_used, 1)
                        at.group += 1

                def split(branch):
                    at.branch += 1
                    dve.wait_ge(branch_hi, at.branch)
                    nc.vector.tensor_tensor(BL[:, :, :], YT[:, :, :], BH[:, :, :].bitcast(F32), ALU.subtract)                        .then_inc(branch_ready, 1)

                tasks = dict(ik=ik, conv_in=conv_in, conv_gate=times_yt, pool_gate=pool_gate, pool_mix=times_yt, index=index, unit=unit, select=select, split=split,
                             rotate=rotate, merged=lambda: activations((0, 1)))
                for name in ("q", "k", "iq", "pooled", "attn_out"):
                    tasks[name] = lambda: skip(2)
                dve.wait_ge(small_loaded, 16 * 8)
                wait_rx()
                branch = half = 0
                for b, kind in enumerate(ORDER):
                    if b + 1 < len(ORDER):
                        split_next(SIZES[b + 1])
                    else:
                        split_next(next_size)
                    if b == len(ORDER) - 2:
                        activations((2, 3))
                    run_tasks(tasks, 2 * b)
                    acc = [ACC[:, (at.block % 2) * 2 + tok, :] for tok in range(NTOK)]
                    if kind in ("cc", "cb"):
                        dst = mid[0] if kind == "cc" else mid[1]
                        dve.wait_ge(blocks_used, at.block + 1)
                        for tok in range(NTOK):
                            block_ready(tok, at.chunk, at.block)
                            ins = nc.vector.scalar_tensor_tensor(dst[:, tok, :], acc[tok], RX[:, tok:tok + 1], SX[:, tok, :],
                                                                 ALU.mult, ALU.mult)
                        ins.then_inc(blocks_used, 1)
                    elif kind == "branch":
                        cols = slice((branch % 2) * COLS, (branch % 2 + 1) * COLS)
                        dve.wait_ge(blocks_used, at.block + 1)
                        for tok in range(NTOK):
                            block_ready(tok, at.chunk, at.block)
                            dst = XN[:, tok, cols] if branch < 2 else SX[:, tok, :]
                            ins = nc.vector.tensor_tensor(dst, ST[:, tok, :], acc[tok], ALU.mult)
                        if branch >= 2:
                            step(ins)
                            ins = nc.vector.tensor_tensor(XN[:, :, cols], XN[:, :, cols], SX[:, :, :], ALU.add)
                        ins.then_inc(blocks_used, 1)
                        branch += 1
                    elif kind == "out":
                        cols = slice(half * COLS, (half + 1) * COLS)
                        for tok in range(NTOK):
                            if half and tok:
                                next_x()
                            block_ready(tok, at.chunk, at.block)
                            nc.vector.tensor_tensor(X[:, tok, cols], X[:, tok, cols], acc[tok], ALU.add).then_inc(x_ready, 1)
                        dve.wait_ge(x_ready, 4 * (at.stage - 1) + 2 * half + 2)
                        dve.sem_inc(blocks_used, 1)
                        half += 1
                    run_tasks(tasks, 2 * b + 1)
                    at.chunk += 1
                    at.block += 1

            def block_ready(tok, last_chunk, block):
                if tok == 0:
                    dve.wait_ge(tile0_ready, block + 1)
                else:
                    dve.wait_ge(weights_used, last_chunk + 2)

            dve.sem_inc(blocks_used, 1)
            dve.sem_inc(groups_used, 1)
            for i, stage in enumerate(stages):
                {"ffn": ffn, "attn": attn, "mlstm": mlstm, "mix2": mix2}[stage[0]](*stage[1:], first_size(i + 1))


def kernel(**inputs):
    import concourse.bacc as bacc
    from concourse.bass_utils import run_bass_kernel_spmd

    nc = bacc.Bacc("TRN2", target_bir_lowering=False, num_devices=1)
    given = {name: np.ascontiguousarray(inputs[name]) for name in inputs}
    given.update(CONSTANTS)
    given["conv_taps"] = np.ascontiguousarray(given.pop("mlstm_conv_w")[0].reshape(4, 2 * HEADS, P).transpose(2, 1, 0))
    given["gains_by_feature"] = np.ascontiguousarray(
        np.concatenate([given["norm_g"][:, 0::2].reshape(3 * DEPTH, KD, P), given["norm_g_2"].reshape(DEPTH, KD, P)])
        .transpose(2, 0, 1))
    given["conv_taps_2"] = np.ascontiguousarray(given.pop("conv_w_2").reshape(DEPTH, TAPS_2, 4, P).transpose(3, 0, 2, 1))
    given["pool_scale_2"] = np.ascontiguousarray(given["pool_scale_2"].reshape(DEPTH, 4, P).transpose(2, 0, 1))
    del given["norm_g_2"]
    arrays, aps = {}, {}
    for name, a in given.items():
        arrays[name + "_in"] = a
        aps[name] = nc.dram_tensor(name + "_in", a.shape, mybir.dt.from_np(a.dtype), kind="ExternalInput").ap()
    out = nc.dram_tensor("out", (1, SEQ, D), F32, kind="ExternalOutput").ap()
    program(nc, **aps, out=out)
    r = run_bass_kernel_spmd(nc, [arrays], core_ids=[0])
    return r.results[0]["out"]
```
